# Optimizing a Trainium2 kernel written in Bass

```python
import jax
import jax.numpy as jnp
from jax import lax
import numpy as np

D_MODEL = 1024
BATCH = 1
SEQ = 512
DEPTH = 2
DEC_BATCH = 8
DEC_SEQ = 4
PAST_LEN = 2048
PAGE_SIZE = 128

N_MIXERS = 2
N_ATTN_LAYERS = (DEPTH + 1) // 2
N_CONV_LAYERS = DEPTH // 2
HEAD_DIM = 64
N_HEADS = D_MODEL // HEAD_DIM
N_KV_HEADS = 4
GQA_GROUP = N_HEADS // N_KV_HEADS
WINDOW = 128
BLOCK = WINDOW
WIN_BUF = min(WINDOW, PAST_LEN)
CONV_WIDTH = 31
D_CONV = D_MODEL
N_GROUPS = 4
EXPERTS_PER_GROUP = 8
N_EXPERTS = N_GROUPS * EXPERTS_PER_GROUP
TOP_K_IN_GROUP = 2
D_EXPERT = D_MODEL // 4
EPS = 1e-6
NEG_INF = -1e30

kernel_name = 'hybrid_swa_sink_conformer_hmoe_step'

def rms_norm(x, g):
    xf = x.astype(jnp.float32)
    y = xf * lax.rsqrt(jnp.mean(xf * xf, axis=-1, keepdims=True) + EPS)
    return (y * g.astype(jnp.float32)).astype(x.dtype)

def layer_norm(x, g, b):
    xf = x.astype(jnp.float32)
    xc = xf - jnp.mean(xf, axis=-1, keepdims=True)
    var = jnp.mean(xc * xc, axis=-1, keepdims=True)
    y = xc * lax.rsqrt(var + EPS) * g.astype(jnp.float32) + b.astype(jnp.float32)
    return y.astype(x.dtype)

def alibi_slopes():
    h = jnp.arange(1, N_HEADS + 1, dtype=jnp.float32)
    return jnp.exp2(-8.0 * h / N_HEADS).reshape(N_KV_HEADS, GQA_GROUP)

def sink_softmax(logits, sink):
    m = jnp.maximum(jnp.max(logits, axis=-1, keepdims=True), sink)
    p = jnp.exp(logits - m)
    return p / (jnp.sum(p, axis=-1, keepdims=True) + jnp.exp(sink - m))

def attend_probs(scores, dist, valid, sinks):
    slopes = alibi_slopes()[:, :, None, None]
    logits = scores * (HEAD_DIM ** -0.5) - slopes * dist.astype(jnp.float32)
    logits = jnp.where(valid, logits, NEG_INF)
    sink = sinks.astype(jnp.float32).reshape(N_KV_HEADS, GQA_GROUP)[:, :, None, None]
    return sink_softmax(logits, sink)

def split_qkv(h, w_qkv):
    b, t, _ = h.shape
    qkv = jnp.einsum('btd,de->bte', h, w_qkv)
    nq = N_HEADS * HEAD_DIM
    nk = N_KV_HEADS * HEAD_DIM
    q = qkv[..., :nq].reshape(b, t, N_KV_HEADS, GQA_GROUP, HEAD_DIM)
    k = qkv[..., nq:nq + nk].reshape(b, t, N_KV_HEADS, HEAD_DIM)
    v = qkv[..., nq + nk:].reshape(b, t, N_KV_HEADS, HEAD_DIM)
    return q, k, v

def attn_prompt(h, w_qkv, w_o, sinks):
    b, t, _ = h.shape
    nb = t // BLOCK
    q, k, v = split_qkv(h, w_qkv)
    qb = q.reshape(b, nb, BLOCK, N_KV_HEADS, GQA_GROUP, HEAD_DIM)

    def band(xf):
        xb = xf.reshape(b, nb, BLOCK, N_KV_HEADS, HEAD_DIM)
        prev = jnp.concatenate([jnp.zeros_like(xb[:, :1]), xb[:, :-1]], axis=1)
        return jnp.concatenate([prev, xb], axis=2)

    k_band, v_band = band(k), band(v)
    scores = jnp.einsum('bnqkgd,bnskd->bnkgqs', qb, k_band,
                        preferred_element_type=jnp.float32)
    qi = jnp.arange(BLOCK)[:, None]
    kj = jnp.arange(2 * BLOCK)[None, :]
    dist = qi + BLOCK - kj
    key_pos = jnp.arange(nb)[:, None, None] * BLOCK + kj[None] - BLOCK
    valid = (dist >= 0) & (dist < WINDOW) & (key_pos >= 0)
    p = attend_probs(scores, dist, valid[None, :, None, None], sinks)
    o = jnp.einsum('bnkgqs,bnskd->bnqkgd', p.astype(v_band.dtype), v_band)
    o = o.reshape(b, t, N_HEADS * HEAD_DIM)
    y = jnp.einsum('bte,ed->btd', o, w_o)
    return y, k[:, t - WIN_BUF:], v[:, t - WIN_BUF:]

def attn_sample(h, cache_k, cache_v, w_qkv, w_o, sinks):
    b, t, _ = h.shape
    n_past = cache_k.shape[1]
    q, k, v = split_qkv(h, w_qkv)
    k_all = jnp.concatenate([cache_k.astype(k.dtype), k], axis=1)
    v_all = jnp.concatenate([cache_v.astype(v.dtype), v], axis=1)
    scores = jnp.einsum('bqkgd,bskd->bkgqs', q, k_all,
                        preferred_element_type=jnp.float32)
    dist = (n_past + jnp.arange(t))[:, None] - jnp.arange(n_past + t)[None, :]
    valid = (dist >= 0) & (dist < WINDOW)
    p = attend_probs(scores, dist, valid, sinks)
    o = jnp.einsum('bkgqs,bskd->bqkgd', p.astype(v_all.dtype), v_all)
    o = o.reshape(b, t, N_HEADS * HEAD_DIM)
    y = jnp.einsum('bte,ed->btd', o, w_o)
    return y, k_all[:, -WIN_BUF:], v_all[:, -WIN_BUF:]

def conv_module(h, hist, w_pw1, b_pw1, w_dw, b_dw, ln_g, ln_b, w_pw2, b_pw2):
    a = jnp.einsum('btd,de->bte', h, w_pw1) + b_pw1
    u = a[..., :D_CONV] * jax.nn.sigmoid(a[..., D_CONV:])
    ext = jnp.concatenate([hist.astype(u.dtype), u], axis=1)
    c = lax.conv_general_dilated(ext, w_dw[:, None, :].astype(ext.dtype),
                                 window_strides=(1,), padding='VALID',
                                 dimension_numbers=('NWC', 'WIO', 'NWC'),
                                 feature_group_count=D_CONV) + b_dw
    c = jax.nn.silu(layer_norm(c, ln_g, ln_b))
    y = jnp.einsum('btc,cd->btd', c, w_pw2) + b_pw2
    return y, ext[:, -(CONV_WIDTH - 1):]

def hier_moe(h, w_gr, b_gr, w_er, b_er, w_gate, w_up, w_down):
    n_tok = h.shape[0]
    g_logits = jnp.einsum('td,dg->tg', h, w_gr).astype(jnp.float32) + b_gr.astype(jnp.float32)
    g_prob = jax.nn.softmax(g_logits, axis=-1)
    g_w, g_idx = lax.top_k(g_prob, 1)
    e_logits = (jnp.einsum('td,de->te', h, w_er).astype(jnp.float32)
                + b_er.astype(jnp.float32)).reshape(n_tok, N_GROUPS, EXPERTS_PER_GROUP)
    e_sel = jnp.take_along_axis(e_logits, g_idx[:, :, None], axis=1)[:, 0]
    e_prob = jax.nn.softmax(e_sel, axis=-1)
    top_v, top_i = lax.top_k(e_prob, TOP_K_IN_GROUP)
    top_v = top_v / jnp.sum(top_v, axis=-1, keepdims=True)
    expert_id = g_idx * EXPERTS_PER_GROUP + top_i
    weights = top_v * g_w
    combine = jnp.sum(jax.nn.one_hot(expert_id, N_EXPERTS, dtype=jnp.float32)
                      * weights[..., None], axis=1)
    out = jnp.zeros(h.shape, jnp.float32)
    for e in range(N_EXPERTS):
        hid = jax.nn.silu(h @ w_gate[e]) * (h @ w_up[e])
        out = out + combine[:, e:e + 1] * (hid @ w_down[e]).astype(jnp.float32)
    return out.astype(h.dtype)

def setup_inputs(seed: int = 0) -> dict:
    key = jax.random.key(seed)
    ks = jax.random.split(key, 32)
    f32 = jnp.float32

    def nrm(k, shape, scale):
        return jax.random.normal(k, shape, f32) * scale

    qkv_out = (N_HEADS + 2 * N_KV_HEADS) * HEAD_DIM
    return {
        'x_prompt': nrm(ks[0], (BATCH, SEQ, D_MODEL), 1.0),
        'x_sample': nrm(ks[1], (DEC_BATCH, DEC_SEQ, D_MODEL), 1.0),
        'cache_k': nrm(ks[2], (N_ATTN_LAYERS, DEC_BATCH, WIN_BUF, N_KV_HEADS, HEAD_DIM), 1.0),
        'cache_v': nrm(ks[3], (N_ATTN_LAYERS, DEC_BATCH, WIN_BUF, N_KV_HEADS, HEAD_DIM), 1.0),
        'state_conv': nrm(ks[4], (N_CONV_LAYERS, DEC_BATCH, CONV_WIDTH - 1, D_CONV), 1.0),
        'w_qkv': nrm(ks[5], (N_ATTN_LAYERS, D_MODEL, qkv_out), D_MODEL ** -0.5),
        'w_o': nrm(ks[6], (N_ATTN_LAYERS, N_HEADS * HEAD_DIM, D_MODEL), (N_HEADS * HEAD_DIM) ** -0.5),
        'attn_sinks': nrm(ks[7], (N_ATTN_LAYERS, N_HEADS), 0.5),
        'w_pw1': nrm(ks[8], (N_CONV_LAYERS, D_MODEL, 2 * D_CONV), D_MODEL ** -0.5),
        'b_pw1': nrm(ks[9], (N_CONV_LAYERS, 2 * D_CONV), 0.02),
        'w_dw': nrm(ks[10], (N_CONV_LAYERS, CONV_WIDTH, D_CONV), CONV_WIDTH ** -0.5),
        'b_dw': nrm(ks[11], (N_CONV_LAYERS, D_CONV), 0.02),
        'conv_ln_g': 1.0 + nrm(ks[12], (N_CONV_LAYERS, D_CONV), 0.02),
        'conv_ln_b': nrm(ks[13], (N_CONV_LAYERS, D_CONV), 0.02),
        'w_pw2': nrm(ks[14], (N_CONV_LAYERS, D_CONV, D_MODEL), D_CONV ** -0.5),
        'b_pw2': nrm(ks[15], (N_CONV_LAYERS, D_MODEL), 0.02),
        'norm_mix_g': 1.0 + nrm(ks[16], (DEPTH, D_MODEL), 0.02),
        'norm_ffn_g': 1.0 + nrm(ks[17], (DEPTH, D_MODEL), 0.02),
        'w_group_router': nrm(ks[18], (DEPTH, D_MODEL, N_GROUPS), D_MODEL ** -0.5),
        'b_group_router': nrm(ks[19], (DEPTH, N_GROUPS), 0.01),
        'w_expert_router': nrm(ks[20], (DEPTH, D_MODEL, N_EXPERTS), D_MODEL ** -0.5),
        'b_expert_router': nrm(ks[21], (DEPTH, N_EXPERTS), 0.01),
        'w_gate': nrm(ks[22], (DEPTH, N_EXPERTS, D_MODEL, D_EXPERT), D_MODEL ** -0.5),
        'w_up': nrm(ks[23], (DEPTH, N_EXPERTS, D_MODEL, D_EXPERT), D_MODEL ** -0.5),
        'w_down': nrm(ks[24], (DEPTH, N_EXPERTS, D_EXPERT, D_MODEL), D_EXPERT ** -0.5),
        'final_norm_g': 1.0 + nrm(ks[25], (D_MODEL,), 0.02),
    }

def reference(x_prompt, x_sample, cache_k, cache_v, state_conv,
              w_qkv, w_o, attn_sinks,
              w_pw1, b_pw1, w_dw, b_dw, conv_ln_g, conv_ln_b, w_pw2, b_pw2,
              norm_mix_g, norm_ffn_g,
              w_group_router, b_group_router, w_expert_router, b_expert_router,
              w_gate, w_up, w_down, final_norm_g):
    xp, xs = x_prompt, x_sample
    n_prompt_tok = xp.shape[0] * xp.shape[1]
    k_p, v_p, c_p, k_s, v_s, c_s = [], [], [], [], [], []
    for i in range(DEPTH):
        hp = rms_norm(xp, norm_mix_g[i])
        hs = rms_norm(xs, norm_mix_g[i])
        j = i // N_MIXERS
        if i % N_MIXERS == 0:
            yp, kp, vp = attn_prompt(hp, w_qkv[j], w_o[j], attn_sinks[j])
            ys, kn, vn = attn_sample(hs, cache_k[j], cache_v[j], w_qkv[j], w_o[j], attn_sinks[j])
            k_p.append(kp)
            v_p.append(vp)
            k_s.append(kn)
            v_s.append(vn)
        else:
            conv_params = (w_pw1[j], b_pw1[j], w_dw[j], b_dw[j], conv_ln_g[j], conv_ln_b[j],
                           w_pw2[j], b_pw2[j])
            hist0 = jnp.zeros((xp.shape[0], CONV_WIDTH - 1, D_CONV), xp.dtype)
            yp, cp = conv_module(hp, hist0, *conv_params)
            ys, cn = conv_module(hs, state_conv[j], *conv_params)
            c_p.append(cp)
            c_s.append(cn)
        xp = xp + yp
        xs = xs + ys
        h_all = jnp.concatenate([rms_norm(xp, norm_ffn_g[i]).reshape(-1, D_MODEL),
                                 rms_norm(xs, norm_ffn_g[i]).reshape(-1, D_MODEL)], axis=0)
        m = hier_moe(h_all, w_group_router[i], b_group_router[i], w_expert_router[i],
                     b_expert_router[i], w_gate[i], w_up[i], w_down[i])
        xp = xp + m[:n_prompt_tok].reshape(xp.shape)
        xs = xs + m[n_prompt_tok:].reshape(xs.shape)
    y_prompt = rms_norm(xp, final_norm_g)
    y_sample = rms_norm(xs, final_norm_g)
    return (y_prompt, y_sample, jnp.stack(k_p), jnp.stack(v_p), jnp.stack(c_p),
            jnp.stack(k_s), jnp.stack(v_s), jnp.stack(c_s))


_drawn_inputs = setup_inputs


def setup_inputs(seed=0):
    import zlib

    import numpy as np

    out = dict(_drawn_inputs(seed))
    spreads = {}
    factors = {}
    for name, (base, spread) in spreads.items():
        noise = np.random.default_rng([zlib.crc32(name.encode()), seed]).standard_normal(out[name].shape)
        drawn = base * np.exp(spread * noise) if base else spread * noise
        out[name] = jnp.asarray(drawn.astype(out[name].dtype))
    for name, factor in factors.items():
        out[name] = (out[name] * factor).astype(out[name].dtype)
    return out
```

```python
from contextlib import ExitStack

import numpy as np

import concourse.bass as bass
from concourse import mybir
from concourse.alu_op_type import AluOpType as ALU

F32 = mybir.dt.float32
I32 = mybir.dt.int32
U32 = mybir.dt.uint32
ACT = mybir.ActivationFunctionType
AX_X = mybir.AxisListType.X
ds = bass.ds

P = 128
D = 1024
KT = D // P
NP, NB, NQ = 512, 8, 4
NS = NB * NQ
T = NP + NS
TH = T // 2
NT = 5
H, HKV, DH = 16, 4, 64
G4 = H // HKV
WIN = 128
CW = 31
HIST = CW - 1
SEG = HIST + NQ
UW = HIST + NP + NB * SEG
NG, EG, NE = 4, 8, 32
F = 256
CAP = 96
CHUNKS = -(-T // CAP)
PAIRS = 2 * T
FAR = 1.0e6
LOW = -3.0e38
HIDE = 1.0e31
EPS = 1e-6
RING = 3
V_MIX, V_FFN, V_BA, V_BG, V_BDW, V_LNG, V_LNB, V_BPW2, V_DW = 0, 2, 4, 5, 6, 7, 8, 9, 10
NV = V_DW + CW
PE_TAPS = 3
ACT_TAPS = 8


def rows_of(t):
    return P if t < 4 else NS


class Steps:

    def __init__(self, eng, sem, start=0):
        self.eng, self.sem, self.start, self.n = eng, sem, start, 0

    def wait_before_last(self):
        self.eng.wait_ge(self.sem, self.start + self.n - 1)

    def done(self, ins):
        ins.then_inc(self.sem, 1)
        self.n += 1

    def wait(self):
        self.eng.wait_ge(self.sem, self.start + self.n)

    def link(self, ins):
        self.done(ins)
        self.wait()


def after(eng, sem, n):
    if not (isinstance(n, int) and n <= 0):
        eng.wait_ge(sem, n)


def settle(eng, sem):
    eng.sem_inc(sem, 1)


def hybrid_step(nc, x_prompt, x_sample, cache_k, cache_v, state_conv, w_qkv, w_o, attn_sinks,
                w_pw1, b_pw1, w_dw, b_dw, conv_ln_g, conv_ln_b, w_pw2, b_pw2, norm_mix_g, norm_ffn_g,
                w_group_router, b_group_router, w_expert_router, b_expert_router,
                w_gate, w_up, w_down, final_norm_g,
                y_prompt, y_sample, k_prompt, v_prompt, conv_prompt, k_sample, v_sample, conv_sample):
    ctx = ExitStack()

    def sb(name, shape, dt=F32):
        return ctx.enter_context(nc.sbuf_tensor(name, shape, dt))

    in_use = []

    def sem(name):
        in_use.append(nc.alloc_semaphore(name))
        return in_use[-1]

    def semaphores_back():
        nc.clear_and_free_semaphores(in_use)
        in_use.clear()
        nc.all_engine_barrier()

    with ctx:
        ps = ctx.enter_context(nc.psum_tensor("ps", [P, 8, 512], F32))
        x_T = sb("x_T", [P, KT, T])
        h_T = sb("h_T", [P, KT, T])
        ring = sb("ring", [P, RING, 6144])
        wring = sb("wring", [P, 2, KT, P])
        areaA = sb("areaA", [P, KT * T])
        areaB = sb("areaB", [P, KT * UW])
        areaC = sb("areaC", [P, KT * T])
        areaS = sb("areaS", [P, 5120])
        ident = sb("ident", [P, P])
        ones = sb("ones", [P, P])
        before = sb("before", [P, P])
        slot_no = sb("slot_no", [P, P])
        chan = sb("chan", [P, KT, NV])
        w_route = sb("w_route", [P, KT, NG + NE])
        small = sb("small", [P, 160])
        idx = sb("idx", [P, 12], U32)
        h_rows = nc.dram_tensor("h_rows", [T, D], F32, kind="Internal").ap()
        pair_rows = nc.dram_tensor("pair_rows", [PAIRS, D], F32, kind="Internal").ap()

        h_flat = h_T[:, :, :].rearrange("p k t -> p (k t)")
        q_T = areaA[:, :].rearrange("p (k t) -> p k t", t=T)
        c_T = q_T
        o_T = areaC[:, :].rearrange("p (k t) -> p k t", t=T)
        v_rows = areaS[:, 2752:2752 + NT * 256].rearrange("p (t n) -> p t n", t=NT)
        k_T = areaS[:, 4032:4032 + 2 * T].rearrange("p (m t) -> p m t", m=2)
        eps_col = small[:, 0:1]
        half = lambda a: a.rearrange("p (c t) -> p c t", c=2)
        x_prompt2 = x_prompt.rearrange("b t d -> (b t) d")
        x_sample2 = x_sample.rearrange("b t d -> (b t) d")

        ring_gate = lambda s: ring[:, s, 0:2048].rearrange("p (k f) -> p k f", f=F)
        ring_up = lambda s: ring[:, s, 2048:4096].rearrange("p (k f) -> p k f", f=F)
        ring_down = lambda s: ring[:, s, 4096:6144].rearrange("p (k n) -> p k n", n=D)

        gateup_landed, down_landed = {}, {}

        def load_gateup(sp, l, e, s):
            sp.dma_start(ring_gate(s), w_gate[l, e].rearrange("(k p) f -> p k f", p=P)).then_inc(gateup_landed[l][s], 16)
            sp.dma_start(ring_up(s), w_up[l, e].rearrange("(k p) f -> p k f", p=P)).then_inc(gateup_landed[l][s], 16)

        def load_down(sp, l, e, s):
            sp.dma_start(ring_down(s), w_down[l, e].rearrange("(k p) n -> p k n", p=P)).then_inc(down_landed[l][s], 16)

        def load_stage():
            x_in = areaS[:, :].rearrange("p (t d) -> p t d", t=NT)
            vals = areaA[0:NV, 0:D]
            landed = [sem(f"x_landed{t}") for t in range(NT)]
            vals_landed = sem("vals_landed")
            route_landed = sem("route_landed")
            const_step = sem("const_step")
            turned = sem("x_turned")
            copied = sem("x_copied")
            with nc.Block() as block:
                @block.sync
                def _(sp):
                    for t in range(NT):
                        src = x_prompt2[t * P:(t + 1) * P, :] if t < 4 else x_sample2
                        sp.dma_start(x_in[0:rows_of(t), t, :], src).then_inc(landed[t], 16)

                @block.scalar
                def _(act):
                    one = lambda a: a.rearrange("(a n) -> a n", a=1)
                    rows = [(V_MIX, norm_mix_g), (V_FFN, norm_ffn_g), (V_BA, b_pw1.rearrange("l (a n) -> (l a) n", a=2)),
                            (V_BDW, b_dw), (V_LNG, conv_ln_g), (V_LNB, conv_ln_b), (V_BPW2, b_pw2), (V_DW, w_dw[0])]
                    for at, src in rows:
                        act.dma_start(vals[at:at + src.shape[0], :], src).then_inc(vals_landed, 16)

                @block.gpsimd
                def _(gp):
                    c = Steps(gp, const_step)
                    c.done(gp.memset(ident[:, :], 0.0))
                    c.done(gp.memset(ones[:, :], 1.0))
                    c.done(gp.memset(eps_col, EPS))
                    c.done(gp.iota(slot_no[:, :], [[1, P]], base=0, channel_multiplier=0,
                                   allow_small_or_imprecise_dtypes=True))
                    c.wait()
                    c.done(gp.affine_select(ident[:, :], ident[:, :], [[-1, P]], ALU.not_equal, 1.0,
                                            base=0, channel_multiplier=1))
                    c.link(gp.affine_select(before[:, :], ones[:, :], [[1, P]], ALU.is_gt, 0.0,
                                            base=0, channel_multiplier=-1))

                @block.tensor
                def _(pe):
                    pe.wait_ge(const_step, 6)
                    pe.wait_ge(vals_landed, 8 * 16)
                    for k in range(KT):
                        mm = pe.transpose(ps[:, 7, k * NV:(k + 1) * NV], vals[:, k * P:(k + 1) * P], ident[0:NV, 0:NV])
                    mm.then_inc(turned, 1)
                    for t in range(NT):
                        r, b = rows_of(t), 2 * (t % 3)
                        pe.wait_ge(landed[t], 16)
                        if t >= 3:
                            pe.wait_ge(copied, t - 1)
                        for k in range(KT):
                            mm = pe.transpose(ps[:, b + k // 4, (k % 4) * P:(k % 4) * P + r],
                                              x_in[0:r, t, k * P:(k + 1) * P], ident[0:r, 0:r])
                        mm.then_inc(turned, 1)

                @block.vector
                def _(v):
                    v.wait_ge(turned, 1)
                    v.tensor_copy(chan[:, :, :].rearrange("p k n -> p (k n)"), ps[:, 7, 0:KT * NV]).then_inc(copied, 1)
                    for t in range(NT):
                        r, b = rows_of(t), 2 * (t % 3)
                        v.wait_ge(turned, t + 2)
                        v.tensor_copy(x_T[:, :, t * P:t * P + r],
                                      ps[:, b:b + 2, :].rearrange("p b (k t) -> p (b k) t", t=P)[:, :, 0:r]).then_inc(copied, 1)

        def norm_stage(name, gain):
            sq = areaS[:, 0:2 * T].rearrange("p (b t) -> p b t", b=2)
            rstd = areaS[:, 2 * T:3 * T]
            squared, used = sem(name + "_squared"), sem(name + "_used")
            rooted, step = sem(name + "_rooted"), sem(name + "_step")
            out = sem(name + "_out")
            with nc.Block() as block:
                @block.scalar
                def _(act):
                    for k in range(KT):
                        if k >= 2:
                            act.wait_ge(used, k - 1)
                        nc.scalar.activation(sq[:, k % 2, :], x_T[:, k, :], ACT.Square).then_inc(squared, 1)
                    act.wait_ge(used, KT)
                    nc.scalar.activation(half(rstd), ps[:, 0:2, 0:TH], ACT.Sqrt, scale=1.0 / D,
                                         bias=eps_col).then_inc(rooted, 1)

                @block.tensor
                def _(pe):
                    for k in range(KT):
                        pe.wait_ge(squared, k + 1)
                        for c in range(2):
                            mm = pe.matmul(ps[:, c, 0:TH], ones[:, :], sq[:, k % 2, c * TH:(c + 1) * TH],
                                           start=(k == 0), stop=(k == KT - 1))
                        mm.then_inc(used, 1)

                @block.vector
                def _(v):
                    s = Steps(v, step)
                    v.wait_ge(rooted, 1)
                    s.link(v.reciprocal(rstd, rstd))
                    for k in range(KT):
                        v.scalar_tensor_tensor(h_T[:, k, :], x_T[:, k, :], chan[:, k, gain:gain + 1], rstd,
                                               ALU.mult, ALU.mult).then_inc(out, 1)
                    v.wait_ge(out, KT)

        def matmul_block(pe, s, operand):
            for k in range(KT):
                for c in range(2):
                    mm = pe.matmul(ps[:, 2 * s + c, 0:TH], wring[:, s, k, :], operand[:, k, c * TH:(c + 1) * TH],
                                   start=(k == 0), stop=(k == KT - 1))
            return mm

        def columns(w, at):
            return w.rearrange("(k p) n -> p k n", p=P)[:, :, ds(at, P)]

        def qkv_stage():
            w_v = areaS[:, 0:2048].rearrange("p (k n) -> p k n", k=KT)
            w = w_qkv[0]
            landed = [sem(f"qk_weights_landed{s}") for s in range(2)]
            v_landed = sem("v_weights_landed")
            projected = [sem(f"qk_projected{s}") for s in range(2)]
            kept = [sem(f"qk_kept{s}") for s in range(2)]
            v_projected, v_kept = sem("v_projected"), sem("v_kept")
            with nc.Block() as block:
                @block.sync
                def _(sp):
                    sp.dma_start(w_v, w[:, 1280:1536].rearrange("(k p) n -> p k n", p=P)).then_inc(v_landed, 16)
                    wq = w[:, 0:1024].rearrange("(k p) (m a i c) -> m a i p k c", p=P, m=2, a=2, i=G4)
                    for j in range(8):
                        m, i, s = j // 4, j % 4, j % 2
                        if j >= 2:
                            sp.wait_ge(projected[s], j // 2)
                        for a in range(2):
                            sp.dma_start(wring[:, s, :, a * DH:(a + 1) * DH], wq[m, a, i]).then_inc(landed[s], 16)
                    for m in range(2):
                        sp.wait_ge(projected[m], 4)
                        sp.dma_start(wring[:, m], columns(w, 1024 + m * P)).then_inc(landed[m], 32)

                @block.tensor
                def _(pe):
                    pe.wait_ge(v_landed, 16)
                    for t in range(NT):
                        r, b = rows_of(t), 4 + t % 4
                        if t >= 4:
                            pe.wait_ge(v_kept, t - 3)
                        for k in range(KT):
                            mm = pe.matmul(ps[0:r, b, 0:256], h_T[:, k, t * P:t * P + r], w_v[:, k, :],
                                           start=(k == 0), stop=(k == KT - 1))
                        mm.then_inc(v_projected, 1)
                    for s in range(2):
                        pe.wait_ge(landed[s], 32)
                        matmul_block(pe, s, h_T).then_inc(projected[s], 1)
                    with pe.Fori(1, 5) as n:
                        for s in range(2):
                            pe.wait_ge(landed[s], 32 * n + 32)
                            pe.wait_ge(kept[s], n)
                            matmul_block(pe, s, h_T).then_inc(projected[s], 1)

                @block.scalar
                def _(act):
                    with act.Fori(0, 4) as n:
                        act.wait_ge(projected[0], n + 1)
                        nc.scalar.activation(half(q_T[:, ds(2 * n, 1), :].rearrange("p k t -> p (k t)")),
                                             ps[:, 0:2, 0:TH], ACT.Copy).then_inc(kept[0], 1)
                    act.wait_ge(projected[0], 5)
                    nc.scalar.activation(half(k_T[:, 0, :]), ps[:, 0:2, 0:TH], ACT.Copy).then_inc(kept[0], 1)

                @block.vector
                def _(v):
                    for t in range(NT):
                        r, b = rows_of(t), 4 + t % 4
                        v.wait_ge(v_projected, t + 1)
                        v.tensor_copy(v_rows[0:r, t, :], ps[0:r, b, 0:256]).then_inc(v_kept, 1)
                    with v.Fori(0, 4) as n:
                        v.wait_ge(projected[1], n + 1)
                        v.tensor_copy(half(q_T[:, ds(2 * n + 1, 1), :].rearrange("p k t -> p (k t)")),
                                      ps[:, 2:4, 0:TH]).then_inc(kept[1], 1)
                    v.wait_ge(projected[1], 5)
                    v.tensor_copy(half(k_T[:, 1, :]), ps[:, 2:4, 0:TH]).then_inc(kept[1], 1)

        def prompt_attention_stage():
            bias = areaB[:, 0:H * 256].rearrange("p (h s) -> p h s", h=H)
            q_blk = h_flat[:, 0:1024].rearrange("p (k t) -> p k t", k=KT)
            k_blk = h_flat[:, 1024:1536].rearrange("p (m s) -> p m s", m=2)
            p_T = h_flat[:, 1536:2560].rearrange("p (c q) -> p c q", q=P)
            o_blk = h_flat[:, 2560:3584]
            probs = areaS[:, 0:2048].rearrange("p (b h s) -> p b h s", b=2, h=G4)
            dist = h_flat[:, 3584:3840]
            sink8, top, nbias, total, gap, inv = (areaB[:, 4096 + 16 * i:4112 + 16 * i] for i in range(6))
            sink_row = small[0:1, 16:32]
            biased, sink_landed = sem("biased"), sem("sink_landed")
            bias_step, slots_filled = sem("bias_step"), sem("slots_filled")
            scored, topped, exped = sem("scored"), sem("topped"), sem("exped")
            probs_turned, probs_kept = sem("probs_turned"), sem("probs_kept")
            mixed, sunk, normed = sem("mixed"), sem("sunk"), sem("normed")
            o_turned, o_kept = sem("o_turned"), sem("o_kept")
            scores_seen = sem("scores_seen")
            top_step, norm_step = sem("top_step"), sem("norm_step")
            sunk_exped = sem("sunk_exped")
            sink_spread, sink_ready = sem("sink_spread"), sem("sink_ready")
            scores = lambda b: ps[:, 2 * b:2 * b + 2, :].rearrange("p c (h s) -> p (c h) s", s=256)
            turned = ps[:, 4:6, :].rearrange("p c (h s) -> p (c h) s", s=P)
            mix = ps[:, 6:8, :].rearrange("p c n -> p (c n)")

            with nc.Block() as block:
                @block.sync
                def _(sp):
                    sp.dma_start(sink_row, attn_sinks).then_inc(sink_landed, 16)

                @block.gpsimd
                def _(gp):
                    c = Steps(gp, bias_step)
                    c.link(gp.iota(dist[:, 0:P], [[-1, P]], base=0, channel_multiplier=1,
                                   allow_small_or_imprecise_dtypes=True))
                    c.link(gp.iota(dist[:, P:2 * P], [[-1, P]], base=WIN, channel_multiplier=1,
                                   allow_small_or_imprecise_dtypes=True))
                    c.link(gp.affine_select(dist[:, 0:P], dist[:, 0:P], [[-1, P]], ALU.is_ge, HIDE,
                                            base=0, channel_multiplier=1))
                    c.link(gp.affine_select(dist[:, P:2 * P], dist[:, P:2 * P], [[1, P]], ALU.is_gt, HIDE,
                                            base=0, channel_multiplier=-1))
                    for h in range(H):
                        gp.tensor_scalar(bias[:, h, :], dist, -8.0 * 2.0 ** (-8.0 * (h + 1) / H), None,
                                         ALU.mult).then_inc(biased, 1)

                    def fill(n, first):
                        if not first:
                            gp.wait_ge(scored, 4 * n)
                        at = n * P
                        gp.tensor_copy(q_blk, q_T[:, :, ds(at, P)]).then_inc(slots_filled, 1)
                        gp.tensor_copy(k_blk[:, :, 0:P], k_T[:, :, ds(at, P)]).then_inc(slots_filled, 1)
                        if not first:
                            gp.tensor_copy(k_blk[:, :, P:2 * P], k_T[:, :, ds(at - P, P)]).then_inc(slots_filled, 1)

                    fill(0, True)
                    with gp.Fori(1, 4) as n:
                        fill(n, False)

                @block.tensor
                def _(pe):
                    pe.wait_ge(sink_landed, 16)
                    pe.matmul(mix[:, 0:H], ones[0:1, :], sink_row, start=True, stop=True).then_inc(sink_spread, 1)

                    def score(n, g, keys):
                        if g == 0:
                            pe.wait_ge(slots_filled, 3 * n + 2)
                        if g >= 2:
                            pe.wait_ge(topped, 4 * n + g - 1)
                        elif keys > P:
                            pe.wait_ge(topped, 4 * n + g - 1)
                        lo = DH * (g % 2)
                        for j in range(G4):
                            mm = pe.matmul(scores(g % 2)[:, j, 0:keys], q_blk[lo:lo + DH, 4 * (g // 2) + j, :],
                                           k_blk[lo:lo + DH, g // 2, 0:keys], start=True, stop=True)
                        mm.then_inc(scored, 1)

                    def turn(n, g, keys):
                        pe.wait_ge(exped, 4 * n + g + 1)
                        if g or keys > P:
                            pe.wait_ge(probs_kept, 4 * n + g)
                        if g == 0 and keys > P:
                            pe.wait_ge(o_kept, n)
                        for j in range(G4):
                            for c in range(keys // P):
                                mm = pe.transpose(turned[:, 2 * j + c, :], probs[:, g % 2, j, c * P:(c + 1) * P], ident[:, :])
                        mm.then_inc(probs_turned, 1)

                    def mixing(n, g, keys):
                        pe.wait_ge(probs_kept, 4 * n + g + 1)
                        if g == 0:
                            pe.wait_ge(sink_ready, 1)
                            if keys > P:
                                pe.wait_ge(normed, n)
                        for j in range(G4):
                            h = G4 * g + j
                            for c in range(keys // P):
                                rows = v_rows[:, ds(n - c, 1), g * DH:(g + 1) * DH].rearrange("p t d -> p (t d)")
                                mm = pe.matmul(mix[:, h * DH:(h + 1) * DH], p_T[:, 2 * j + c, :], rows,
                                               start=(c == 0), stop=(c == keys // P - 1))
                        mm.then_inc(mixed, 1)

                    def attend(n, keys):
                        score(n, 0, keys)
                        score(n, 1, keys)
                        turn(n, 0, keys)
                        for g in range(HKV):
                            if g + 2 < HKV:
                                score(n, g + 2, keys)
                            mixing(n, g, keys)
                            if g + 1 < HKV:
                                turn(n, g + 1, keys)
                        pe.wait_ge(normed, n + 1)
                        for k in range(KT):
                            mm = pe.transpose(turned[:, k, :], o_blk[:, k * P:(k + 1) * P], ident[:, :])
                        mm.then_inc(o_turned, 1)

                    attend(0, P)
                    with pe.Fori(1, 4) as n:
                        attend(n, 2 * P)

                @block.scalar
                def _(act):
                    def attend(n, keys):
                        for g in range(HKV):
                            act.wait_ge(topped, 4 * n + g + 1)
                            for j in range(G4):
                                h = G4 * g + j
                                e = nc.scalar.activation(probs[:, g % 2, j, 0:keys], probs[:, g % 2, j, 0:keys], ACT.Exp,
                                                         bias=nbias[:, h:h + 1], scale=0.125,
                                                         accum_out=total[:, h:h + 1])
                            e.then_inc(exped, 1)
                            if g >= 1:
                                keep(n, g - 1, keys)
                        keep(n, HKV - 1, keys)
                        act.wait_ge(sunk, n + 1)
                        nc.scalar.activation(gap, gap, ACT.Exp, scale=0.125).then_inc(sunk_exped, 1)

                    def keep(n, g, keys):
                        act.wait_ge(probs_turned, 4 * n + g + 1)
                        if g or keys > P:
                            act.wait_ge(mixed, 4 * n + g)
                        c = keys // P
                        to = p_T.rearrange("p (j c) q -> p j c q", c=2)[:, :, 0:c, :]
                        of = turned.rearrange("p (j c) q -> p j c q", c=2)[:, :, 0:c, :]
                        nc.scalar.activation(to, of, ACT.Copy).then_inc(probs_kept, 1)

                    attend(0, P)
                    with act.Fori(1, 4) as n:
                        attend(n, 2 * P)

                @block.vector
                def _(v):
                    v.wait_ge(sink_spread, 1)
                    v.tensor_scalar(sink8, mix[:, 0:H], 8.0, None, ALU.mult).then_inc(sink_ready, 1)
                    v.wait_ge(sink_ready, 1)

                    def attend(n, keys):
                        first = keys == P
                        for g in range(HKV):
                            v.wait_ge(scored, 4 * n + g + 1)
                            if g >= 2 or not first:
                                v.wait_ge(probs_turned, 4 * n + g - 1)
                            if not first:
                                settle(v, scores_seen)
                            v.wait_ge(biased, H)
                            for j in range(G4):
                                h = G4 * g + j
                                t = v.tensor_tensor_reduce(out=probs[:, g % 2, j, 0:keys], in0=scores(g % 2)[:, j, 0:keys],
                                                           in1=bias[:, h, 0:keys], scale=1.0, scalar=sink8[:, h:h + 1],
                                                           op0=ALU.add, op1=ALU.max, accum_out=top[:, h:h + 1])
                            t.then_inc(top_step, 1)
                            v.wait_ge(top_step, 4 * n + g + 1)
                            hs = slice(G4 * g, G4 * g + G4)
                            v.tensor_scalar(nbias[:, hs], top[:, hs], -0.125, None, ALU.mult).then_inc(topped, 1)
                        v.tensor_tensor(gap, sink8, top, ALU.subtract).then_inc(sunk, 1)
                        v.wait_ge(sunk_exped, n + 1)
                        s = Steps(v, norm_step, 2 * n)
                        s.link(v.tensor_tensor(total, total, gap, ALU.add))
                        s.link(v.reciprocal(inv, total))
                        v.wait_ge(mixed, 4 * n + 4)
                        if not first:
                            v.wait_ge(o_turned, n)
                        v.tensor_tensor(o_blk.rearrange("p (h d) -> p h d", h=H), mix.rearrange("p (h d) -> p h d", h=H),
                                        inv.unsqueeze(2).to_broadcast([P, H, DH]),
                                        ALU.mult).then_inc(normed, 1)
                        v.wait_ge(o_turned, n + 1)
                        v.tensor_copy(o_T[:, :, ds(n * P, P)], turned).then_inc(o_kept, 1)

                    attend(0, P)
                    with v.Fori(1, 4) as n:
                        attend(n, 2 * P)

        def sample_attention_stage():
            NK = WIN + NS
            head_of_row = np.full(P, -1)
            for r in range(P):
                g, j = r // 32, r % 32 // 4
                if j // 4 == g // 2:
                    head_of_row[r] = G4 * g + j % G4
            pick = (np.arange(H)[:, None] == head_of_row[None, :]).astype(np.float32)
            row_vals = np.stack([np.arange(P) % NQ, np.where(head_of_row >= 0, -8.0 * 2.0 ** (-8.0 * (head_of_row + 1) / H), 0.0)],
                                axis=1).astype(np.float32)
            pick_dram = nc.inline_tensor(pick, "head_pick").ap()
            row_dram = nc.inline_tensor(row_vals, "row_values").ap()

            key_rows = areaB[:, 0:2048].rearrange("p (b n) -> p b n", b=NB)
            val_rows = areaB[:, 2048:4096].rearrange("p (b n) -> p b n", b=NB)
            keys_T = areaB[:, 4096:6144].rearrange("p (b m s) -> p b m s", b=NB, m=2)
            bias = h_flat[:, 0:NB * NK].rearrange("p (b s) -> p b s", b=NB)
            probs = h_flat[:, NB * NK:2 * NB * NK].rearrange("p (b s) -> p b s", b=NB)
            p_T = h_flat[:, 2560:3584].rearrange("p (b r) -> p b r", b=NB)
            pn_T = areaS[0:NS, 0:1024].rearrange("p (b r) -> p b r", b=NB)
            o_twice = areaS[:, 1024:2048].rearrange("p (b a d) -> p b a d", b=NB, a=2)
            pick_sb, sink_col, row_sb, sink8 = areaS[0:H, 2048:2176], small[0:H, 32:33], small[:, 34:36], small[:, 36:37]
            dist = areaS[:, 2176:2176 + NK]
            q_new = areaS[:, 2336:2336 + KT * NS].rearrange("p (b k t) -> p b k t", b=NB, k=KT)
            top, total, gap, inv = (small[:, 40 + 8 * i:48 + 8 * i] for i in range(4))
            k_out = h_flat[:, 3584:3840]
            ks_out = h_flat[0:NS, 3840:4096]

            cache_landed, vcache_landed, const_landed = sem("cache_landed"), sem("vcache_landed"), sem("row_const_landed")
            q_ready = sem("sample_q_ready")
            mask_step, step = sem("sample_mask_step"), sem("sample_step")
            keys_turned, keys_kept, scored = sem("keys_turned"), sem("keys_kept"), sem("sample_scored")
            picked, sink_kept = sem("sink_picked"), sem("sink_kept")
            shifted, exped, ready = sem("sample_shifted"), sem("sample_exped"), sem("sample_probs_ready")
            turned, kept, mixed = sem("sample_turned"), sem("sample_kept"), sem("sample_mixed")
            o_ready, o_turned, stored = sem("sample_o_ready"), sem("sample_o_turned"), sem("kv_stored")
            k_turned, k_kept, o_kept = sem("k_out_turned"), sem("k_out_kept"), sem("sample_o_kept")
            score_tile = lambda g: ps[32 * g:32 * g + 32, 4 * (g % 2):4 * (g % 2) + 4, :]\
                .rearrange("p c (b s) -> p (c b) s", s=256)[:, :, 0:NK]

            with nc.Block() as block:
                @block.sync
                def _(sp):
                    sp.dma_start(key_rows, cache_k[0].rearrange("b s g d -> s b (g d)")).then_inc(cache_landed, 16)
                    sp.dma_start(pick_sb, pick_dram).then_inc(const_landed, 16)
                    sp.dma_start(sink_col, attn_sinks.rearrange("l h -> h l")).then_inc(const_landed, 16)
                    sp.dma_start(row_sb, row_dram).then_inc(const_landed, 16)
                    sp.dma_start(val_rows, cache_v[0].rearrange("b s g d -> s b (g d)")).then_inc(vcache_landed, 16)
                    for new, old in ((k_sample, cache_k), (v_sample, cache_v)):
                        sp.dma_start(new[0, :, 0:WIN - NQ].rearrange("b s g d -> b s (g d)"),
                                     old[0, :, NQ:WIN].rearrange("b s g d -> b s (g d)")).then_inc(stored, 16)
                    sp.dma_start(v_prompt[0, 0].rearrange("s g d -> s (g d)"), v_rows[:, 3, :]).then_inc(stored, 16)
                    for b in range(NB):
                        sp.dma_start(v_sample[0, b, WIN - NQ:WIN].rearrange("s g d -> s (g d)"),
                                     v_rows[NQ * b:NQ * b + NQ, 4, :]).then_inc(stored, 16)
                    sp.wait_ge(k_kept, 2)
                    sp.dma_start(k_prompt[0, 0].rearrange("s g d -> s (g d)"), k_out).then_inc(stored, 16)
                    for b in range(NB):
                        sp.dma_start(k_sample[0, b, WIN - NQ:WIN].rearrange("s g d -> s (g d)"),
                                     ks_out[NQ * b:NQ * b + NQ, :]).then_inc(stored, 16)
                    sp.wait_ge(stored, 16 * (4 + 2 * NB))

                @block.gpsimd
                def _(gp):
                    gp.tensor_copy(q_new, q_T[:, :, NP:T].rearrange("p k (b t) -> p b k t", b=NB)).then_inc(q_ready, 1)
                    c = Steps(gp, mask_step)
                    c.done(gp.iota(dist[:, 0:WIN], [[-1, WIN]], base=WIN, channel_multiplier=0,
                                   allow_small_or_imprecise_dtypes=True))
                    c.done(gp.iota(dist[:, WIN:NK], [[0, NB], [-1, NQ]], base=0, channel_multiplier=0,
                                   allow_small_or_imprecise_dtypes=True))
                    c.wait()
                    gp.wait_ge(const_landed, 48)
                    c.link(gp.tensor_scalar(dist, dist, row_sb[:, 0:1], None, ALU.add))
                    hidden = bias[:, 0, :]
                    c.done(gp.tensor_scalar(hidden[:, 0:WIN], dist[:, 0:WIN], float(WIN), HIDE, ALU.is_ge, ALU.mult))
                    c.link(gp.tensor_scalar(hidden[:, WIN:NK], dist[:, WIN:NK], 0.0, HIDE, ALU.is_lt, ALU.mult))
                    c.link(gp.tensor_tensor(dist, dist, hidden, ALU.add))
                    c.done(gp.tensor_copy(bias[:, :, 0:WIN], dist[:, 0:WIN].unsqueeze(1).to_broadcast([P, NB, WIN])))
                    c.link(gp.tensor_copy(bias[:, :, WIN:NK], dist[:, WIN:NK].unsqueeze(1).to_broadcast([P, NB, NS])))
                    for t in range(NQ):
                        view = bias[:, :, WIN:NK].rearrange("p b (c t) -> p b c t", t=NQ)[:, :, :, t]
                        c.done(gp.affine_select(view, view, [[1, NB], [-1, NB]], ALU.is_equal, HIDE,
                                                base=0, channel_multiplier=0))
                    c.wait()
                    c.link(gp.tensor_scalar(bias, bias, row_sb[:, 1:2], None, ALU.mult))

                @block.tensor
                def _(pe):
                    pe.wait_ge(cache_landed, 16)
                    for b in range(NB):
                        for m in range(2):
                            n = 2 * b + m
                            mm = pe.transpose(ps[:, n // 4, (n % 4) * P:(n % 4 + 1) * P],
                                              key_rows[:, b, m * P:(m + 1) * P], ident[:, :])
                    mm.then_inc(keys_turned, 1)
                    for m in range(2):
                        pe.transpose(ps[:, 4, m * P:(m + 1) * P], k_T[:, m, NP - P:NP], ident[:, :])
                        mm = pe.transpose(ps[0:NS, 5, m * P:(m + 1) * P], k_T[:, m, NP:T], ident[:, :])
                    mm.then_inc(k_turned, 1)
                    pe.wait_ge(const_landed, 48)
                    pe.matmul(ps[:, 6, 0:1], pick_sb, sink_col, start=True, stop=True).then_inc(picked, 1)
                    pe.wait_ge(keys_kept, 1)
                    pe.wait_ge(q_ready, 1)
                    pe.wait_ge(k_kept, 2)
                    pe.wait_ge(sink_kept, 1)
                    for g in range(HKV):
                        lo, m = DH * (g % 2), g // 2
                        for b in range(NB):
                            q = q_new[lo:lo + DH, b].rearrange("p k t -> p (k t)")
                            out = score_tile(g)[:, b, :]
                            pe.matmul(out[:, 0:WIN], q, keys_T[lo:lo + DH, b, m, :], start=True, stop=True)
                            mm = pe.matmul(out[:, WIN:NK], q, k_T[lo:lo + DH, m, NP:T], start=True, stop=True)
                        mm.then_inc(scored, 1)
                    pe.wait_ge(ready, 1)
                    for b in range(NB):
                        pe.transpose(ps[:, b // 4, (b % 4) * P:(b % 4 + 1) * P], probs[:, b, 0:WIN], ident[:, :])
                        mm = pe.transpose(ps[0:NS, 2 + b // 4, (b % 4) * P:(b % 4 + 1) * P], probs[:, b, WIN:NK], ident[:, :])
                    mm.then_inc(turned, 1)
                    pe.wait_ge(kept, 2)
                    pe.wait_ge(vcache_landed, 16)
                    for b in range(NB):
                        for g in range(HKV):
                            out = ps[32 * g:32 * g + 32, 4, b * DH:(b + 1) * DH]
                            pe.matmul(out, p_T[:, b, 32 * g:32 * g + 32], val_rows[:, b, g * DH:(g + 1) * DH],
                                      start=True, stop=False)
                            mm = pe.matmul(out, pn_T[:, b, 32 * g:32 * g + 32], v_rows[0:NS, 4, g * DH:(g + 1) * DH],
                                           start=False, stop=True)
                    mm.then_inc(mixed, 1)
                    pe.wait_ge(o_ready, 2)
                    for b in range(NB):
                        mm = pe.transpose(ps[:, 6 + b // 4, (b % 4) * P:(b % 4 + 1) * P],
                                          o_twice[:, b].rearrange("p a d -> p (a d)"), ident[:, :])
                    mm.then_inc(o_turned, 1)

                @block.scalar
                def _(act):
                    act.wait_ge(keys_turned, 1)
                    nc.scalar.activation(keys_T.rearrange("p b m s -> p (b m s)"),
                                         ps[:, 0:4, :].rearrange("p c n -> p (c n)"), ACT.Copy).then_inc(keys_kept, 1)
                    act.wait_ge(shifted, 2)
                    nc.scalar.activation(probs, probs, ACT.Exp, scale=0.125).then_inc(exped, 1)
                    nc.scalar.activation(gap, gap, ACT.Exp, scale=0.125).then_inc(exped, 1)
                    act.wait_ge(turned, 1)
                    nc.scalar.activation(p_T.rearrange("p b r -> p (b r)"), ps[:, 0:2, :].rearrange("p c n -> p (c n)"),
                                         ACT.Copy).then_inc(kept, 1)

                @block.vector
                def _(v):
                    v.wait_ge(k_turned, 1)
                    v.tensor_copy(k_out, ps[:, 4, 0:256]).then_inc(k_kept, 1)
                    v.tensor_copy(ks_out, ps[0:NS, 5, 0:256]).then_inc(k_kept, 1)
                    v.wait_ge(picked, 1)
                    v.tensor_scalar(sink8, ps[:, 6, 0:1], 8.0, None, ALU.mult).then_inc(sink_kept, 1)
                    v.wait_ge(sink_kept, 1)
                    v.wait_ge(mask_step, 13)
                    s = Steps(v, step)
                    for g in range(HKV):
                        v.wait_ge(scored, g + 1)
                        q = slice(32 * g, 32 * g + 32)
                        s.done(v.tensor_tensor(probs[q], score_tile(g), bias[q], ALU.add))
                    s.wait()
                    s.link(v.tensor_reduce(top, probs, AX_X, ALU.max))
                    s.link(v.tensor_scalar(top, top, sink8, None, ALU.max))
                    v.tensor_tensor(probs, probs, top.unsqueeze(2).to_broadcast([P, NB, NK]), ALU.subtract).then_inc(shifted, 1)
                    v.tensor_scalar(gap, top, -1.0, sink8, ALU.mult, ALU.add).then_inc(shifted, 1)
                    v.wait_ge(exped, 2)
                    s.link(v.tensor_reduce(total, probs, AX_X, ALU.add))
                    s.link(v.tensor_tensor(total, total, gap, ALU.add))
                    s.link(v.reciprocal(inv, total))
                    v.tensor_tensor(probs, probs, inv.unsqueeze(2).to_broadcast([P, NB, NK]), ALU.mult).then_inc(ready, 1)
                    v.wait_ge(turned, 1)
                    v.tensor_copy(pn_T.rearrange("p b r -> p (b r)"), ps[0:NS, 2:4, :].rearrange("p c n -> p (c n)")).then_inc(kept, 1)
                    v.wait_ge(mixed, 1)
                    for a in range(2):
                        v.tensor_copy(o_twice[:, :, a, :], ps[:, 4, :].rearrange("p (b d) -> p b d", d=DH)).then_inc(o_ready, 1)
                    v.wait_ge(o_turned, 1)
                    spread = ps[:, 6:8, :].rearrange("p c (b r) -> p (c b) r", r=P)
                    for g in range(HKV):
                        for a in range(2):
                            first = 32 * g + 16 * (g // 2) + NQ * a
                            for i in range(2):
                                src = spread[DH * a:DH * a + DH, :, first + 8 * i:first + 8 * i + NQ]
                                dst = o_T[DH * a:DH * a + DH, 2 * g + i, NP:T].rearrange("p (b t) -> p b t", t=NQ)
                                v.tensor_copy(dst, src).then_inc(o_kept, 1)
                    v.wait_ge(o_kept, 16)

        def project_back_stage(name, w, operand, offset):
            landed = [sem(f"{name}_weights_landed{s}") for s in range(2)]
            projected = [sem(f"{name}_projected{s}") for s in range(2)]
            added = [sem(f"{name}_added{s}") for s in range(2)]
            with nc.Block() as block:
                @block.sync
                def _(sp):
                    for s in range(2):
                        sp.dma_start(wring[:, s], columns(w, s * P)).then_inc(landed[s], 16)
                    with sp.Fori(1, 4) as n:
                        for s in range(2):
                            sp.wait_ge(projected[s], n)
                            sp.dma_start(wring[:, s], columns(w, (2 * n + s) * P)).then_inc(landed[s], 16)

                @block.tensor
                def _(pe):
                    for s in range(2):
                        pe.wait_ge(landed[s], 16)
                        matmul_block(pe, s, operand).then_inc(projected[s], 1)
                    with pe.Fori(1, 4) as n:
                        for s in range(2):
                            pe.wait_ge(landed[s], 16 * n + 16)
                            pe.wait_ge(added[s], n)
                            matmul_block(pe, s, operand).then_inc(projected[s], 1)

                @block.vector
                def _(v):
                    with v.Fori(0, 4) as n:
                        for s in range(2):
                            v.wait_ge(projected[s], n + 1)
                            xs = half(x_T[:, ds(2 * n + s, 1), :].rearrange("p k t -> p (k t)"))
                            off = 0.0 if offset is None else \
                                chan[:, ds(2 * n + s, 1), offset:offset + 1].rearrange("p k n -> p (k n)")
                            v.scalar_tensor_tensor(xs, ps[:, 2 * s:2 * s + 2, 0:TH], off, xs,
                                                   ALU.add, ALU.add).then_inc(added[s], 1)

        def conv_stage():
            u_T = areaB[:, :].rearrange("p (k n) -> p k n", k=KT)
            u_seg = u_T[:, :, HIST + NP:UW].rearrange("p k (b n) -> p k b n", b=NB)
            state_rows = areaS[0:4 * HIST, 0:2048].rearrange("p (i n) -> p i n", i=2)
            sig = areaS[:, 2048:2048 + T]
            prod = areaS[:, 2592:2592 + NS * CW].rearrange("p (r w) -> p r w", w=CW)
            diag = areaS[:, 3584:3584 + 2 * PE_TAPS * P].rearrange("p (b w c) -> p b w c", b=2, w=PE_TAPS)
            w = w_pw1[0]
            state_landed, state_turned, hist_ready = sem("state_landed"), sem("state_turned"), sem("hist_ready")
            landed = [sem(f"pw1_landed{s}") for s in range(2)]
            val_done, gate_done = sem("pw1_value_done"), sem("pw1_gate_done")
            sig_done, u_done, diag_ready = sem("sigmoid_done"), sem("u_done"), sem("diag_ready")
            taps_done, conv_done = sem("pe_taps_done"), sem("conv_done")
            product_ready, product_added = sem("product_ready"), sem("product_added")
            hist_copied, u_part = sem("hist_copied"), sem("u_part")
            tap_step, seg_step = sem("tap_step"), sem("seg_step")
            stored = sem("conv_stored")
            products = areaC[:, 0:2048].rearrange("p (b n) -> p b n", b=4)
            product_sum = areaC[:, 2048:2560]
            VEC_FIRST = PE_TAPS + ACT_TAPS
            VEC_STEPS = CW - VEC_FIRST + 1
            acc = lambda b: ps[:, 4 + b, :]
            acc2 = lambda b: ps[:, 6 + b, :]
            col = lambda k, n: chan[:, ds(k, 1), n:n + 1].rearrange("p k n -> p (k n)")
            shifted = lambda k, j: u_T[:, ds(k, 1), j:j + NP].rearrange("p k n -> p (k n)")

            with nc.Block() as block:
                @block.sync
                def _(sp):
                    sp.dma_start(state_rows, state_conv[0].rearrange("(i b) r n -> (b r) i n", i=2)).then_inc(state_landed, 16)
                    for s in range(2):
                        sp.dma_start(wring[:, s], columns(w, s * D)).then_inc(landed[s], 16)
                    sp.dma_start(conv_sample[0, :, 0:HIST - NQ], state_conv[0, :, NQ:HIST]).then_inc(stored, 16)
                    with sp.Fori(1, KT) as k:
                        sp.wait_ge(val_done, k)
                        sp.dma_start(wring[:, 0], columns(w, k * P)).then_inc(landed[0], 16)
                        sp.wait_ge(gate_done, k)
                        sp.dma_start(wring[:, 1], columns(w, k * P + D)).then_inc(landed[1], 16)
                    sp.wait_ge(stored, 16)

                @block.tensor
                def _(pe):
                    pe.wait_ge(state_landed, 16)
                    for i in range(2):
                        for k in range(KT):
                            mm = pe.transpose(ps[:, 4 * i + k // 4, (k % 4) * P:(k % 4) * P + 4 * HIST],
                                              state_rows[:, i, k * P:(k + 1) * P], ident[0:4 * HIST, 0:4 * HIST])
                    mm.then_inc(state_turned, 1)
                    pe.wait_ge(hist_ready, 1)

                    def value(k):
                        pe.wait_ge(landed[0], 16 * k + 16)
                        after(pe, u_done, 2 * k)
                        matmul_block(pe, 0, h_T).then_inc(val_done, 1)

                    def gate(k):
                        pe.wait_ge(landed[1], 16 * k + 16)
                        after(pe, sig_done, k)
                        matmul_block(pe, 1, h_T).then_inc(gate_done, 1)

                    def taps(k, b, early):
                        pe.wait_ge(diag_ready, k + 1)
                        pe.wait_ge(u_done, 2 * k + 2)
                        if not early:
                            pe.wait_ge(conv_done, k - 1)
                        for j in range(PE_TAPS):
                            mm = pe.matmul(acc(b), diag[:, b, j, :],
                                           u_T[:, ds(k, 1), j:j + NP].rearrange("p k n -> p (k n)"),
                                           start=(j == 0), stop=(j == PE_TAPS - 1))
                        mm.then_inc(taps_done, 1)

                    value(0)
                    gate(0)
                    for k in (1, 2):
                        value(k)
                        taps(k - 1, (k - 1) % 2, True)
                        gate(k)
                    with pe.Fori(1, 3) as i:
                        for j in (1, 2):
                            k = 2 * i + j
                            value(k)
                            taps(k - 1, (j - 1) % 2, False)
                            gate(k)
                    value(7)
                    taps(6, 0, False)
                    gate(7)
                    taps(7, 1, False)

                @block.scalar
                def _(act):
                    def diags(k, b):
                        for j in range(PE_TAPS):
                            d = nc.scalar.activation(diag[:, b, j, :], ident[:, :], ACT.Copy,
                                                     scale=chan[:, ds(k, 1), V_DW + j:V_DW + j + 1].rearrange("p k n -> p (k n)"))
                        d.then_inc(diag_ready, 1)

                    def sigmoid(k):
                        act.wait_ge(gate_done, k + 1)
                        after(act, u_done, 2 * k)
                        nc.scalar.activation(half(sig), ps[:, 2:4, 0:TH], ACT.Sigmoid,
                                             bias=chan[:, ds(k, 1), V_BG:V_BG + 1].rearrange("p k n -> p (k n)")).then_inc(sig_done, 1)

                    def multiply(k, first):
                        act.wait_ge(u_done, 2 * k + 2)
                        for m in range(ACT_TAPS):
                            if m >= 4:
                                act.wait_ge(product_added, (ACT_TAPS - 1) * k + max(m - 4, 1))
                            elif not first:
                                act.wait_ge(product_added, (ACT_TAPS - 1) * (k - 1) + m + 4)
                            nc.scalar.activation(products[:, m % 4, :], shifted(k, PE_TAPS + m), ACT.Copy,
                                                 scale=col(k, V_DW + PE_TAPS + m)).then_inc(product_ready, 1)

                    diags(0, 0)
                    sigmoid(0)
                    diags(1, 1)
                    multiply(0, True)
                    sigmoid(1)
                    with act.Fori(1, 4) as i:
                        for j in range(2):
                            k = 2 * i + j
                            act.wait_ge(taps_done, k - 1)
                            diags(k, j)
                            multiply(k - 1, False)
                            sigmoid(k)
                    multiply(7, False)

                @block.vector
                def _(v):
                    v.wait_ge(state_turned, 1)
                    for i in range(2):
                        for c in range(2):
                            v.tensor_copy(u_seg[:, 4 * c:4 * c + 4, 4 * i:4 * i + 4, 0:HIST],
                                          ps[:, 4 * i + c, :].rearrange("p (k t) -> p k t", k=4)[:, :, 0:4 * HIST]
                                          .rearrange("p k (b r) -> p k b r", b=4)).then_inc(hist_copied, 1)
                    v.wait_ge(hist_copied, 4)
                    v.memset(u_T[:, :, 0:HIST], 0.0).then_inc(hist_ready, 1)

                    def glu(k):
                        v.wait_ge(sig_done, k + 1)
                        ba = chan[:, ds(k, 1), V_BA:V_BA + 1].rearrange("p k n -> p (k n)")
                        uk = u_T[:, ds(k, 1), HIST:HIST + NP].rearrange("p k n -> p (k n)")
                        v.scalar_tensor_tensor(uk[:, 0:TH], ps[:, 0, 0:TH], ba, sig[:, 0:TH],
                                               ALU.add, ALU.mult).then_inc(u_part, 1)
                        v.scalar_tensor_tensor(u_seg[:, ds(k, 1), :, HIST:SEG].rearrange("p k b t -> p (k b) t"),
                                               ps[:, 1, NP - TH:TH].rearrange("p (b t) -> p b t", t=NQ), ba,
                                               sig[:, NP:T].rearrange("p (b t) -> p b t", t=NQ),
                                               ALU.add, ALU.mult).then_inc(u_done, 1)
                        v.wait_ge(u_part, k + 1)
                        v.scalar_tensor_tensor(uk[:, TH:NP], ps[:, 1, 0:NP - TH], ba, sig[:, TH:NP],
                                               ALU.add, ALU.mult).then_inc(u_done, 1)

                    def taps(k, b, js, steps):
                        for j in js:
                            if j == VEC_FIRST:
                                o = v.tensor_scalar(acc2(b), shifted(k, j), col(k, V_DW + j), None, ALU.mult)
                            else:
                                a = (acc2, acc)[(j - VEC_FIRST) % 2](b)
                                if j > VEC_FIRST + 1:
                                    steps.wait_before_last()
                                o = v.scalar_tensor_tensor(a, shifted(k, j), col(k, V_DW + j), a, ALU.mult, ALU.add)
                            steps.done(o)
                    split = CW - 6

                    def conv(k, b, last):
                        steps = Steps(v, tap_step, k * VEC_STEPS)
                        v.wait_ge(taps_done, k + 1)
                        taps(k, b, range(VEC_FIRST, split), steps)
                        if not last:
                            glu(k + 1)
                        taps(k, b, range(split, CW), steps)
                        steps.wait()
                        out = c_T[:, ds(k, 1), 0:NP].rearrange("p k n -> p (k n)")
                        v.wait_ge(product_added, (ACT_TAPS - 1) * (k + 1))
                        steps.link(v.scalar_tensor_tensor(out, acc2(b), col(k, V_BDW), product_sum, ALU.add, ALU.add))
                        v.tensor_tensor(out, acc(b), out, ALU.add).then_inc(conv_done, 1)

                    glu(0)
                    with v.Fori(0, 3) as i:
                        for j in range(2):
                            conv(2 * i + j, j, False)
                    conv(6, 0, False)
                    conv(7, 1, True)

                @block.gpsimd
                def _(gp):
                    def samples(k):
                        s = Steps(gp, seg_step, 7 * k)
                        gp.wait_ge(u_done, 2 * k + 2)
                        taps = chan[:, ds(k, 1), V_DW:NV]
                        for t in range(NQ):
                            windows = u_seg[:, ds(k, 1), :, t:t + CW].rearrange("p k b w -> p (k b) w")
                            m = gp.tensor_tensor(prod.rearrange("p (b t) w -> p b t w", t=NQ)[:, :, t, :], windows,
                                                 taps.to_broadcast([P, NB, CW]), ALU.mult)
                        s.link(m)
                        out = c_T[:, ds(k, 1), NP:T].rearrange("p k n -> p (k n)")
                        for n in (15, 8, 4, 2):
                            up = CW - n if n == 15 else n
                            s.link(gp.tensor_tensor(prod[:, :, 0:n], prod[:, :, 0:n], prod[:, :, up:up + n], ALU.add))
                        s.link(gp.tensor_tensor(out, prod[:, :, 0], prod[:, :, 1], ALU.add))
                        s.done(gp.tensor_tensor(out, out, col(k, V_BDW).to_broadcast([P, NS]), ALU.add))

                    def add(k):
                        after(gp, conv_done, k)
                        for m in range(1, ACT_TAPS):
                            gp.wait_ge(product_ready, ACT_TAPS * k + m + 1)
                            if m > 1:
                                gp.wait_ge(product_added, (ACT_TAPS - 1) * k + m - 1)
                            gp.tensor_tensor(product_sum, products[:, 0, :] if m == 1 else product_sum,
                                             products[:, m % 4, :], ALU.add).then_inc(product_added, 1)

                    samples(0)
                    add(0)
                    with gp.Fori(1, KT) as k:
                        samples(k)
                        add(k)

            u_turned, u_kept, u_stored = sem("u_turned"), sem("u_rows_kept"), sem("u_rows_stored")
            tail = areaS[0:HIST, 0:1024]
            fresh = areaS[0:NS, 1024:2048]
            fresh_T = areaS[:, 2048:2048 + KT * NS].rearrange("p (k t) -> p k t", k=KT)
            fresh_ready = sem("u_fresh_ready")
            with nc.Block() as block:
                @block.tensor
                def _(pe):
                    pe.wait_ge(fresh_ready, 1)
                    for k in range(KT):
                        pe.transpose(ps[0:HIST, k // 4, (k % 4) * P:(k % 4 + 1) * P], u_T[:, k, NP:NP + HIST], ident[:, :])
                        mm = pe.transpose(ps[0:NS, 2 + k // 4, (k % 4) * P:(k % 4 + 1) * P],
                                          fresh_T[:, k, :], ident[:, :])
                    mm.then_inc(u_turned, 1)

                @block.vector
                def _(v):
                    v.tensor_copy(fresh_T.rearrange("p k (b t) -> p k b t", b=NB), u_seg[:, :, :, HIST:SEG]).then_inc(fresh_ready, 1)
                    v.wait_ge(u_turned, 1)
                    v.tensor_copy(tail, ps[0:HIST, 0:2, :].rearrange("p c n -> p (c n)")).then_inc(u_kept, 1)
                    v.tensor_copy(fresh, ps[0:NS, 2:4, :].rearrange("p c n -> p (c n)")).then_inc(u_kept, 1)

                @block.sync
                def _(sp):
                    sp.wait_ge(u_kept, 2)
                    sp.dma_start(conv_prompt[0, 0], tail).then_inc(u_stored, 16)
                    for b in range(NB):
                        sp.dma_start(conv_sample[0, b, HIST - NQ:HIST, :], fresh[NQ * b:NQ * b + NQ, :]).then_inc(u_stored, 16)
                    sp.wait_ge(u_stored, 16 * (1 + NB))

        def layernorm_stage():
            sq = areaS[:, 2048:2048 + 2 * T].rearrange("p (b t) -> p b t", b=2)
            rstd = areaS[:, 2048 + 2 * T:2048 + 3 * T]
            meaned, centred, squared, summed = sem("ln_meaned"), sem("ln_centred"), sem("ln_squared"), sem("ln_summed")
            rooted, inverted, scaled, out = sem("ln_rooted"), sem("ln_inverted"), sem("ln_scaled"), sem("ln_out")
            with nc.Block() as block:
                @block.tensor
                def _(pe):
                    for k in range(KT):
                        for c in range(2):
                            mm = pe.matmul(ps[:, c, 0:TH], ones[:, :], c_T[:, k, c * TH:(c + 1) * TH],
                                           start=(k == 0), stop=(k == KT - 1))
                    mm.then_inc(meaned, 1)
                    for k in range(KT):
                        pe.wait_ge(squared, k + 1)
                        for c in range(2):
                            mm = pe.matmul(ps[:, 2 + c, 0:TH], ones[:, :], sq[:, k % 2, c * TH:(c + 1) * TH],
                                           start=(k == 0), stop=(k == KT - 1))
                        mm.then_inc(summed, 1)

                @block.vector
                def _(v):
                    v.wait_ge(meaned, 1)
                    for k in range(KT):
                        v.scalar_tensor_tensor(half(c_T[:, k, :]), ps[:, 0:2, 0:TH], -1.0 / D, half(c_T[:, k, :]),
                                               ALU.mult, ALU.add).then_inc(centred, 1)
                    v.wait_ge(rooted, 1)
                    v.reciprocal(rstd, rstd).then_inc(inverted, 1)
                    v.wait_ge(inverted, 1)
                    for k in range(KT):
                        v.tensor_tensor(c_T[:, k, :], c_T[:, k, :], rstd, ALU.mult).then_inc(scaled, 1)

                @block.scalar
                def _(act):
                    for k in range(KT):
                        act.wait_ge(centred, k + 1)
                        if k >= 2:
                            act.wait_ge(summed, k - 1)
                        nc.scalar.activation(sq[:, k % 2, :], c_T[:, k, :], ACT.Square).then_inc(squared, 1)
                    act.wait_ge(summed, KT)
                    nc.scalar.activation(half(rstd), ps[:, 2:4, 0:TH], ACT.Sqrt, scale=1.0 / D, bias=eps_col).then_inc(rooted, 1)
                    for k in range(KT):
                        act.wait_ge(scaled, k + 1)
                        nc.scalar.activation(h_T[:, k, :], c_T[:, k, :], ACT.Silu, scale=chan[:, k, V_LNG:V_LNG + 1],
                                             bias=chan[:, k, V_LNB:V_LNB + 1]).then_inc(out, 1)

        area_route = areaS[:, :]
        off = [0]

        def part(n):
            off[0] += n
            return area_route[:, off[0] - n:off[0]]

        logits = part(NT * (NG + NE)).rearrange("p (t e) -> p t e", t=NT)
        picked = [part(NT * NE).rearrange("p (t e) -> p t e", t=NT) for _ in range(2)]
        tagged = [part(NT * NE).rearrange("p (t e) -> p t e", t=NT) for _ in range(2)]
        taken = part(NT * NE).rearrange("p (t e) -> p t e", t=NT)
        hot = part(NT * NE).rearrange("p (t e) -> p t e", t=NT)
        match = part(2 * NT * CAP).rearrange("p (c s) -> p c s", s=CAP)
        far, tok_of, pair_of = part(NE)[0:CAP], part(NE)[0:CAP], part(NE)[0:CAP]
        pair_no, rank, weight = part(2 * NT), part(2 * NT), part(2 * NT)
        g_top, g_sum, e_top, e_next, tie = part(NT), part(NT), part(NT), part(NT), part(NT)
        g_exp, g_hot, g_rev = part(NT * NG).rearrange("p (t g) -> p t g", t=NT), part(NT * NG).rearrange("p (t g) -> p t g", t=NT), part(NE)
        most = part(1)
        most_int = part(1).bitcast(I32)
        assert off[0] <= 5120, off[0]
        rows_in = areaC[:, 0:3 * D].rearrange("p (s n) -> p s n", s=3)
        rows_T = areaA[:, 0:3 * KT * CAP].rearrange("p (s k r) -> p s k r", s=3, k=KT)
        rows_out = areaB[:, 0:3 * D].rearrange("p (s n) -> p s n", s=3)
        hid_buf = areaB[:, 3072:3072 + 3 * F].rearrange("p (a f) -> p a f", a=3)
        gated, hid, hid_T = hid_buf[0:CAP, 0], hid_buf[0:CAP, 1], hid_buf[:, 2, 0:2 * CAP].rearrange("p (k r) -> p k r", k=2)

        def make_table(v, steps, match_ready, table_made, n):
            for c in range(2 * NT):
                m = v.tensor_scalar(match[:, c, :], slot_no[:, 0:CAP], rank[:, c:c + 1], None, ALU.is_equal)
            m.then_inc(match_ready, 1)
            v.wait_ge(table_made, n + 1)
            number = ps[0:CAP, 3, 0:NE]
            steps.link(v.tensor_scalar(far, number, 0.0, FAR, ALU.is_equal, ALU.mult))
            steps.link(v.scalar_tensor_tensor(pair_of, number, -1.0, far, ALU.add, ALU.add))
            steps.link(v.tensor_scalar(far, pair_of, float(T), -float(T), ALU.is_ge, ALU.mult))
            steps.link(v.tensor_tensor(tok_of, pair_of, far, ALU.add))

        TABLE_STEPS = 4

        def table_matmuls(pe, table_made):
            for c in range(2 * NT):
                mm = pe.matmul(ps[0:CAP, 3, 0:NE], match[:, c, :], tagged[c // NT][:, c % NT, :],
                               start=(c == 0), stop=(c == 2 * NT - 1))
            mm.then_inc(table_made, 1)

        def route_stage(l):
            b_row = small[0:1, 80:80 + NG + NE]
            h_out = areaB[:, 0:2 * D].rearrange("p (b n) -> p b n", b=2)
            bias_landed, stored = sem(f"route_bias_landed{l}"), sem(f"h_rows_stored{l}")
            logits_done, turned, kept = sem(f"logits_done{l}"), sem(f"h_turned{l}"), sem(f"h_kept{l}")
            filled, step, exped = sem(f"route_filled{l}"), sem(f"route_step{l}"), sem(f"route_exped{l}")
            dif_ready, choice_ready, ranked = sem(f"route_dif_ready{l}"), sem(f"choice_ready{l}"), sem(f"ranked{l}")
            match_ready, table_made, landed = sem(f"match_ready{l}"), sem(f"table_made{l}"), sem(f"w_route_landed{l}")
            h_stored = [sem(f"h_rows_stored{l}{b}") for b in range(2)]
            with nc.Block() as block:
                @block.sync
                def _(sp):
                    sp.dma_start(w_route[:, :, 0:NG], w_group_router[l].rearrange("(k p) g -> p k g", p=P)).then_inc(landed, 16)
                    sp.dma_start(w_route[:, :, NG:NG + NE], w_expert_router[l].rearrange("(k p) g -> p k g", p=P)).then_inc(landed, 16)
                    sp.dma_start(b_row[:, 0:NG], b_group_router[l:l + 1, :]).then_inc(bias_landed, 16)
                    sp.dma_start(b_row[:, NG:NG + NE], b_expert_router[l:l + 1, :]).then_inc(bias_landed, 16)
                    for t in range(NT):
                        r = rows_of(t)
                        sp.wait_ge(kept, t + 1)
                        sp.dma_start(h_rows[t * P:t * P + r, :], h_out[0:r, t % 2, :]).then_inc(h_stored[t % 2], 16)
                    sp.wait_ge(h_stored[0], 48)
                    sp.wait_ge(h_stored[1], 32)

                @block.gpsimd
                def _(gp):
                    gp.iota(pair_no, [[T, 2], [P, NT]], base=1, channel_multiplier=1,
                            allow_small_or_imprecise_dtypes=True).then_inc(filled, 1)
                    gp.iota(g_rev, [[-1, NE]], base=NE, channel_multiplier=0,
                            allow_small_or_imprecise_dtypes=True).then_inc(filled, 1)
                    gp.memset(logits, 0.0).then_inc(filled, 1)

                @block.tensor
                def _(pe):
                    pe.wait_ge(landed, 32)
                    pe.wait_ge(bias_landed, 32)
                    for t in range(NT):
                        r = rows_of(t)
                        out = ps[0:r, 2, t * (NG + NE):(t + 1) * (NG + NE)]
                        pe.matmul(out, ones[0:1, 0:r], b_row, start=True, stop=False)
                        for k in range(KT):
                            mm = pe.matmul(out, h_T[:, k, t * P:t * P + r], w_route[:, k, :], start=False, stop=(k == KT - 1))
                    mm.then_inc(logits_done, 1)
                    for t in range(NT):
                        r, b = rows_of(t), 2 * (t % 2)
                        if t >= 2:
                            pe.wait_ge(kept, t - 1)
                        for k in range(KT):
                            mm = pe.transpose(ps[0:r, 4 + b + k // 4, (k % 4) * P:(k % 4 + 1) * P],
                                              h_T[:, k, t * P:t * P + r], ident[:, :])
                        mm.then_inc(turned, 1)
                    pe.wait_ge(choice_ready, 1)
                    for t in range(NT):
                        out = ps[:, 0, t * NE:(t + 1) * NE]
                        for u in range(t + 1):
                            pe.matmul(out, (before if u == t else ones)[:, :], taken[:, u, :], start=(u == 0), stop=(u == t))
                    for u in range(NT):
                        mm = pe.matmul(ps[:, 1, 0:NE], ones[:, :], taken[:, u, :], start=(u == 0), stop=(u == NT - 1))
                    mm.then_inc(ranked, 1)
                    pe.wait_ge(match_ready, 1)
                    table_matmuls(pe, table_made)

                @block.scalar
                def _(act):
                    for t in range(NT):
                        r, b = rows_of(t), 2 * (t % 2)
                        act.wait_ge(turned, t + 1)
                        if t >= 2:
                            act.wait_ge(h_stored[t % 2], 16 * (t // 2))
                        nc.scalar.activation(h_out[0:r, t % 2, :], ps[0:r, 4 + b:6 + b, :].rearrange("p c n -> p (c n)"),
                                             ACT.Copy).then_inc(kept, 1)
                    act.wait_ge(dif_ready, 1)
                    nc.scalar.activation(g_exp, g_exp, ACT.Exp).then_inc(exped, 1)
                    nc.scalar.activation(tie, tie, ACT.Exp).then_inc(exped, 1)

                @block.vector
                def _(v):
                    s = Steps(v, step)
                    wide = lambda a, n: a.unsqueeze(2).to_broadcast([P, NT, n])
                    rev = lambda n: g_rev[:, NE - n:NE].unsqueeze(1).to_broadcast([P, NT, n])
                    v.wait_ge(logits_done, 1)
                    v.wait_ge(filled, 3)
                    s.done(v.tensor_copy(logits[:, 0:4, :], ps[:, 2, 0:4 * (NG + NE)].rearrange("p (t e) -> p t e", t=4)))
                    s.link(v.tensor_copy(logits[0:NS, 4, :], ps[0:NS, 2, 4 * (NG + NE):NT * (NG + NE)]))
                    group, expert = logits[:, :, 0:NG], logits[:, :, NG:NG + NE]
                    s.link(v.tensor_reduce(g_top, group, AX_X, ALU.max))
                    s.link(v.tensor_tensor(g_hot, group, wide(g_top, NG), ALU.is_equal))
                    s.link(v.tensor_tensor(g_hot, g_hot, rev(NG), ALU.mult))
                    s.link(v.tensor_reduce(tie, g_hot, AX_X, ALU.max))
                    s.link(v.tensor_tensor(g_hot, g_hot, wide(tie, NG), ALU.is_equal))
                    s.link(v.tensor_tensor(g_exp, group, wide(g_top, NG), ALU.subtract))
                    by_group = lambda a: a.rearrange("p t (g e) -> p (t g) e", g=NG)
                    g_flat = g_hot.rearrange("p t g -> p (t g)").unsqueeze(2).to_broadcast([P, NT * NG, EG])
                    s.link(v.tensor_scalar(by_group(hot), g_flat, -1.0, -LOW, ALU.add, ALU.mult))
                    s.link(v.tensor_copy(taken, expert))
                    s.link(v.tensor_tensor(by_group(taken), by_group(taken), g_flat, ALU.mult))
                    s.link(v.tensor_tensor(taken, taken, hot, ALU.add))
                    for c, top in enumerate((e_top, e_next)):
                        s.link(v.tensor_reduce(top, taken, AX_X, ALU.max))
                        s.link(v.tensor_tensor(hot, taken, wide(top, NE), ALU.is_equal))
                        s.link(v.tensor_tensor(hot, hot, rev(NE), ALU.mult))
                        s.link(v.tensor_reduce(tie, hot, AX_X, ALU.max))
                        s.link(v.tensor_tensor(picked[c], hot, wide(tie, NE), ALU.is_equal))
                        if c == 0:
                            s.link(v.scalar_tensor_tensor(taken, picked[0], LOW, taken, ALU.mult, ALU.add))
                    for c in range(2):
                        s.done(v.memset(picked[c][32:64, 4, :], 0.0))
                        s.done(v.memset(picked[c][64:P, 4, :], 0.0))
                    s.wait()
                    v.tensor_tensor(taken, picked[0], picked[1], ALU.add).then_inc(choice_ready, 1)
                    v.tensor_tensor(tie, e_next, e_top, ALU.subtract).then_inc(dif_ready, 1)
                    for c in range(2):
                        s.link(v.tensor_tensor(tagged[c], picked[c], wide(pair_no[:, c * NT:(c + 1) * NT], NE), ALU.mult))
                    v.wait_ge(exped, 2)
                    s.link(v.tensor_reduce(g_sum, g_exp, AX_X, ALU.add))
                    s.link(v.tensor_scalar(e_top, tie, 1.0, None, ALU.add))
                    s.link(v.tensor_tensor(g_sum, g_sum, e_top, ALU.mult))
                    s.link(v.reciprocal(weight[:, 0:NT], g_sum))
                    s.link(v.tensor_tensor(weight[:, NT:2 * NT], weight[:, 0:NT], tie, ALU.mult))
                    v.wait_ge(ranked, 1)
                    ranks = ps[:, 0, 0:NT * NE].rearrange("p (t e) -> p t e", t=NT)
                    for c in range(2):
                        s.link(v.tensor_tensor(hot, picked[c], ranks, ALU.mult))
                        s.link(v.tensor_reduce(rank[:, c * NT:(c + 1) * NT], hot, AX_X, ALU.add))
                    s.link(v.tensor_reduce(most, ps[:, 1, 0:NE], AX_X, ALU.max))
                    s.link(v.tensor_copy(most_int, most))
                    make_table(v, s, match_ready, table_made, 0)

        class Nth:

            def __init__(self, i, c):
                self.i, self.c = i, c
                self.e, self.s, self.q = 3 * i + c, c % 3, i + c // 3

            def shift(self, d):
                return Nth(self.i, self.c + d)

        def expert_stage(l):
            gathered = [sem(f"rows_gathered{l}{s}") for s in range(3)]
            scattered = [sem(f"rows_scattered{l}{s}") for s in range(3)]
            cleared, tok_ready, pair_ready = sem(f"rows_cleared{l}"), sem(f"tok_ready{l}"), sem(f"pair_ready{l}")
            turned, turned_kept = sem(f"rows_turned{l}"), sem(f"rows_T_kept{l}")
            gateup_done, silued, hid_ready = sem(f"gateup_done{l}"), sem(f"silued{l}"), sem(f"hid_ready{l}")
            hid_turned, hid_kept = sem(f"hid_turned{l}"), sem(f"hid_T_kept{l}")
            down_done, out_kept = sem(f"down_done{l}"), sem(f"out_kept{l}")
            pool_settled = sem(f"pool_settled{l}")
            last = NE - 1

            def everywhere(eng, step):
                for e in range(1 + RING):
                    step(Nth(0, e), e == 0, False)
                with eng.Fori(1, (NE - 2) // RING) as i:
                    for u in range(RING):
                        step(Nth(i, 1 + u), False, False)
                step(Nth((NE - 2) // RING, 1), False, True)

            def turn_rows(pe, s):
                for k in range(KT):
                    mm = pe.transpose(ps[:, k // 4, (k % 4) * P:(k % 4) * P + CAP], rows_in[0:CAP, s, k * P:(k + 1) * P], ident[0:CAP, 0:CAP])
                return mm

            def gate_and_up(pe, s, w):
                for a, wt in ((0, ring_gate(w)), (1, ring_up(w))):
                    for k in range(KT):
                        mm = pe.matmul(ps[0:CAP, 2, a * F:(a + 1) * F], rows_T[:, s, k, :], wt[:, k, :],
                                       start=(k == 0), stop=(k == KT - 1))
                return mm

            def turn_hidden(pe):
                for k in range(2):
                    mm = pe.transpose(ps[:, 3, k * P:k * P + CAP], hid[:, k * P:(k + 1) * P], ident[0:CAP, 0:CAP])
                return mm

            def down(pe, w):
                for k in range(2):
                    for c in range(2):
                        mm = pe.matmul(ps[0:CAP, 4 + c, :], hid_T[:, k, :], ring_down(w)[:, k, c * 512:(c + 1) * 512],
                                       start=(k == 0), stop=(k == 1))
                return mm

            def keep_turned(act, s):
                return nc.scalar.activation(rows_T[:, s], ps[:, 0:2, :].rearrange("p c (k r) -> p (c k) r", r=P)[:, :, 0:CAP], ACT.Copy)

            def silu_gate():
                return nc.scalar.activation(gated, ps[0:CAP, 2, 0:F], ACT.Silu)

            def keep_hidden_T():
                return nc.scalar.activation(hid_T, ps[:, 3, 0:F].rearrange("p (k r) -> p k r", k=2)[:, :, 0:CAP], ACT.Copy)

            def fill_idx(gp, s, e, sem_, of, at):
                gp.tensor_copy(idx[0:CAP, at + s:at + s + 1], of[:, ds(e, 1)]).then_inc(sem_, 1)

            def gather(gp, s):
                settle(gp, pool_settled)
                return gp.indirect_dma_start(rows_in[0:CAP, s, :], None, h_rows, bass.IndirectOffsetOnAxis(idx[0:CAP, s:s + 1], 0),
                                             bounds_check=T - 1, oob_is_err=False)

            def scatter(gp, s):
                settle(gp, pool_settled)
                return gp.indirect_dma_start(pair_rows, bass.IndirectOffsetOnAxis(idx[0:CAP, 3 + s:4 + s], 0), rows_out[0:CAP, s, :],
                                             None, bounds_check=PAIRS - 1, oob_is_err=False)

            gateup_landed[l] = [sem(f"gateup_landed{l}{s}") for s in range(RING)]
            down_landed[l] = [sem(f"down_landed{l}{s}") for s in range(RING)]
            with nc.Block() as block:
                @block.sync
                def _(sp):
                    for s in range(RING):
                        load_gateup(sp, l, s, s)
                        load_down(sp, l, s, s)

                    def load(x):
                        sp.wait_ge(gateup_done, x.e - 2)
                        load_gateup(sp, l, x.e, x.s)
                        y = x.shift(-1)
                        if not (isinstance(y.e, int) and y.e < RING):
                            sp.wait_ge(down_done, y.e - 2)
                            load_down(sp, l, y.e, y.s)

                    for e in range(RING, 2 * RING):
                        load(Nth(0, e))
                    with sp.Fori(2, NE // RING) as i:
                        for u in range(RING):
                            load(Nth(i, u))
                    for e in range(NE // RING * RING, NE):
                        load(Nth(0, e))
                    sp.wait_ge(down_done, NE - RING)
                    load_down(sp, l, NE - 1, (NE - 1) % RING)

                @block.gpsimd
                def _(gp):
                    gp.memset(rows_in, 0.0).then_inc(cleared, 1)
                    def fetch(x):
                        after(gp, gathered[x.s], 16 * x.q)
                        fill_idx(gp, x.s, x.e, tok_ready, tok_of, 0)
                        after(gp, turned, x.e - 2)
                        gp.wait_ge(tok_ready, x.e + 1)
                        gather(gp, x.s).then_inc(gathered[x.s], 16)

                    def store(x):
                        after(gp, scattered[x.s], 16 * x.q)
                        fill_idx(gp, x.s, x.e, pair_ready, pair_of, 3)
                        gp.wait_ge(pair_ready, x.e + 1)
                        gp.wait_ge(out_kept, 2 * x.e + 2)
                        scatter(gp, x.s).then_inc(scattered[x.s], 16)

                    gp.wait_ge(cleared, 1)
                    for e in range(5):
                        fetch(Nth(0, e))
                    for e in range(3):
                        fetch(Nth(0, e + 5))
                        store(Nth(0, e))
                    with gp.Fori(1, (NE - 5) // RING) as i:
                        for u in range(RING):
                            fetch(Nth(i, u + 5))
                            store(Nth(i, u))
                    for e in range(NE - 5, NE):
                        store(Nth(0, e))
                    for s in range(3):
                        gp.wait_ge(scattered[s], 16 * len(range(s, NE, 3)))

                @block.tensor
                def _(pe):
                    def turn(x, first):
                        pe.wait_ge(gathered[x.s], 16 * x.q + 16)
                        if not first:
                            pe.wait_ge(turned_kept, x.e)
                        turn_rows(pe, x.s).then_inc(turned, 1)

                    def hidden(x):
                        pe.wait_ge(hid_ready, x.e + 1)
                        turn_hidden(pe).then_inc(hid_turned, 1)

                    def out(x):
                        pe.wait_ge(hid_kept, x.e + 1)
                        pe.wait_ge(down_landed[l][x.s], 16 * x.q + 16)
                        after(pe, out_kept, 2 * x.e)
                        down(pe, x.s).then_inc(down_done, 1)

                    def step(x, first, final):
                        if not final:
                            turn(x.shift(1), False)
                        if not first:
                            hidden(x.shift(-1))
                        pe.wait_ge(turned_kept, x.e + 1)
                        pe.wait_ge(gateup_landed[l][x.s], 32 * x.q + 32)
                        if not first:
                            pe.wait_ge(hid_ready, x.e)
                        gate_and_up(pe, x.s, x.s).then_inc(gateup_done, 1)
                        if not first:
                            out(x.shift(-1))

                    turn(Nth(0, 0), True)
                    everywhere(pe, step)
                    hidden(Nth(0, last))
                    out(Nth(0, last))

                @block.scalar
                def _(act):
                    def turned_rows(x):
                        act.wait_ge(turned, x.e + 1)
                        keep_turned(act, x.s).then_inc(turned_kept, 1)

                    def hidden(x):
                        act.wait_ge(hid_turned, x.e + 1)
                        keep_hidden_T().then_inc(hid_kept, 1)

                    def out(x):
                        act.wait_ge(down_done, x.e + 1)
                        after(act, scattered[x.s], 16 * x.q)
                        nc.scalar.activation(rows_out[0:CAP, x.s, 0:512], ps[0:CAP, 4, :], ACT.Copy).then_inc(out_kept, 1)

                    def step(x, first, final):
                        if not final:
                            turned_rows(x.shift(1))
                        if not first:
                            hidden(x.shift(-1))
                        act.wait_ge(gateup_done, x.e + 1)
                        silu_gate().then_inc(silued, 1)
                        if not first:
                            out(x.shift(-1))

                    turned_rows(Nth(0, 0))
                    everywhere(act, step)
                    hidden(Nth(0, last))
                    out(Nth(0, last))

                @block.vector
                def _(v):
                    def out(x):
                        v.wait_ge(down_done, x.e + 1)
                        after(v, scattered[x.s], 16 * x.q)
                        v.tensor_copy(rows_out[0:CAP, x.s, 512:D], ps[0:CAP, 5, :]).then_inc(out_kept, 1)

                    def step(x, first, final):
                        v.wait_ge(silued, x.e + 1)
                        if not first:
                            v.wait_ge(hid_turned, x.e)
                        v.tensor_tensor(hid, gated, ps[0:CAP, 2, F:2 * F], ALU.mult).then_inc(hid_ready, 1)
                        if not first:
                            out(x.shift(-1))

                    everywhere(v, step)
                    out(Nth(0, last))

            overflow_stage(l, turn_rows, gate_and_up, turn_hidden, down, keep_turned, silu_gate, keep_hidden_T,
                           fill_idx, gather, scatter)

        def overflow_stage(l, turn_rows, gate_and_up, turn_hidden, down, keep_turned, silu_gate, keep_hidden_T,
                           fill_idx, gather, scatter):
            names = ("idle match_ready table_made table_ready table_step landed idx_ready gathered turned turned_kept gateup_done "
                     "silued hid_ready hid_turned hid_kept down_done out_kept scattered").split()
            o = {n: sem(f"more_{n}{l}") for n in names}
            with nc.Block() as block:
                def over(eng, body, before_round=None, before=None):
                    most = eng.value_load(most_int[0:1, 0:1], min_val=0, max_val=T)
                    with eng.If(most > CAP):
                        if before:
                            before()
                        with eng.Fori(0, CHUNKS - 1) as j:
                            if before_round:
                                before_round(j)
                            with eng.Fori(0, NE) as e:
                                body(e, NE * j + e, j)

                @block.sync
                def _(sp):
                    def body(e, n, j):
                        sp.wait_ge(o["idle"], n + 1)
                        for dst, src in ((ring_gate(0), w_gate), (ring_up(0), w_up)):
                            sp.dma_start(dst, src[l, ds(e, 1)].rearrange("e (k p) f -> p (e k) f", p=P)).then_inc(o["landed"], 16)
                        sp.dma_start(ring_down(0), w_down[l, ds(e, 1)].rearrange("e (k p) n -> p (e k) n", p=P)).then_inc(o["landed"], 16)
                    over(sp, body)

                @block.gpsimd
                def _(gp):
                    def body(e, n, j):
                        gp.wait_ge(o["table_ready"], j + 1)
                        fill_idx(gp, 0, e, o["idx_ready"], tok_of, 0)
                        fill_idx(gp, 0, e, o["idx_ready"], pair_of, 3)
                        gp.wait_ge(o["idx_ready"], 2 * n + 2)
                        gather(gp, 0).then_inc(o["gathered"], 16)
                        gp.wait_ge(o["out_kept"], 2 * n + 2)
                        scatter(gp, 0).then_inc(o["scattered"], 16)
                        gp.wait_ge(o["scattered"], 16 * n + 16)
                        gp.sem_inc(o["idle"], 1)
                    over(gp, body, before=lambda: gp.sem_inc(o["idle"], 1))

                @block.tensor
                def _(pe):
                    def table(j):
                        pe.wait_ge(o["match_ready"], j + 1)
                        table_matmuls(pe, o["table_made"])

                    def body(e, n, j):
                        pe.wait_ge(o["gathered"], 16 * n + 16)
                        turn_rows(pe, 0).then_inc(o["turned"], 1)
                        pe.wait_ge(o["turned_kept"], n + 1)
                        pe.wait_ge(o["landed"], 48 * n + 48)
                        gate_and_up(pe, 0, 0).then_inc(o["gateup_done"], 1)
                        pe.wait_ge(o["hid_ready"], n + 1)
                        turn_hidden(pe).then_inc(o["hid_turned"], 1)
                        pe.wait_ge(o["hid_kept"], n + 1)
                        down(pe, 0).then_inc(o["down_done"], 1)
                        pe.wait_ge(o["out_kept"], 2 * n + 2)
                    over(pe, body, table)

                @block.scalar
                def _(act):
                    def body(e, n, j):
                        act.wait_ge(o["turned"], n + 1)
                        keep_turned(act, 0).then_inc(o["turned_kept"], 1)
                        act.wait_ge(o["gateup_done"], n + 1)
                        silu_gate().then_inc(o["silued"], 1)
                        act.wait_ge(o["hid_turned"], n + 1)
                        keep_hidden_T().then_inc(o["hid_kept"], 1)
                        act.wait_ge(o["down_done"], n + 1)
                        nc.scalar.activation(rows_out[0:CAP, 0, 0:512], ps[0:CAP, 4, :], ACT.Copy).then_inc(o["out_kept"], 1)
                    over(act, body)

                @block.vector
                def _(v):
                    def table(j):
                        v.wait_ge(o["idle"], NE * j + 1)
                        s = Steps(v, o["table_step"], (TABLE_STEPS + 1) * j)
                        s.link(v.tensor_scalar(rank, rank, -float(CAP), None, ALU.add))
                        make_table(v, s, o["match_ready"], o["table_made"], j)
                        v.sem_inc(o["table_ready"], 1)

                    def body(e, n, j):
                        v.wait_ge(o["silued"], n + 1)
                        v.tensor_tensor(hid, gated, ps[0:CAP, 2, F:2 * F], ALU.mult).then_inc(o["hid_ready"], 1)
                        v.wait_ge(o["down_done"], n + 1)
                        v.tensor_copy(rows_out[0:CAP, 0, 512:D], ps[0:CAP, 5, :]).then_inc(o["out_kept"], 1)
                    over(v, body, table)

        def combine_stage(l):
            final = l == 1
            pairs = areaB[:, 0:4 * D].rearrange("p (b c n) -> p b c n", b=2, c=2)
            mixed_rows = areaA[:, 0:2 * D].rearrange("p (b n) -> p b n", b=2)
            x_rows = areaA[:, 2 * D:4 * D].rearrange("p (b n) -> p b n", b=2)
            gain = areaC[:, 0:D]
            square = areaC[:, D:2 * D]
            y_rows = areaC[:, 2 * D:4 * D].rearrange("p (b n) -> p b n", b=2)
            ssq, rstd = small[:, 120:125], small[:, 125:130]
            landed = [sem(f"pairs_landed{l}{b}") for b in range(2)]
            first_scaled, mixed, turned, added = sem(f"first_scaled{l}"), sem(f"pairs_mixed{l}"), sem(f"mixed_turned{l}"), sem(f"mixed_added{l}")
            gain_landed, x_kept, summed = sem(f"gain_landed{l}"), sem(f"x_rows_kept{l}"), sem(f"final_summed{l}")
            rooted, inverted, y_ready = sem(f"final_rooted{l}"), sem(f"final_inverted{l}"), sem(f"y_ready{l}")
            squared = sem(f"final_squared{l}")
            y_stored = [sem(f"y_stored{l}{b}") for b in range(2)]
            with nc.Block() as block:
                @block.sync
                def _(sp):
                    if final:
                        sp.dma_start(gain, final_norm_g.rearrange("(a n) -> a n", a=1).to_broadcast([P, D])).then_inc(gain_landed, 16)
                    by_choice = pair_rows.rearrange("(c t) n -> t c n", c=2)
                    for t in range(NT):
                        r = rows_of(t)
                        if t >= 2:
                            sp.wait_ge(mixed, t - 1)
                        sp.dma_start(pairs[0:r, t % 2], by_choice[t * P:t * P + r]).then_inc(landed[t % 2], 16)
                    if final:
                        for t in range(NT):
                            r = rows_of(t)
                            dst = y_prompt.rearrange("b t d -> (b t) d")[t * P:(t + 1) * P, :] if t < 4 \
                                else y_sample.rearrange("b t d -> (b t) d")
                            sp.wait_ge(y_ready, t + 1)
                            sp.dma_start(dst, y_rows[0:r, t % 2, :]).then_inc(y_stored[t % 2], 16)
                        sp.wait_ge(y_stored[0], 48)
                        sp.wait_ge(y_stored[1], 32)

                @block.scalar
                def _(act):
                    for t in range(NT):
                        r, b = rows_of(t), t % 2
                        act.wait_ge(landed[b], 16 * (t // 2) + 16)
                        if t >= 2:
                            act.wait_ge(summed if final else turned, t - 1)
                        nc.scalar.activation(mixed_rows[0:r, b, :], pairs[0:r, b, 0, :], ACT.Copy,
                                             scale=weight[0:r, t:t + 1]).then_inc(first_scaled, 1)
                        if final:
                            act.wait_ge(summed, t + 1)
                            nc.scalar.activation(square[0:r, :], x_rows[0:r, b, :], ACT.Square,
                                                 accum_out=ssq[0:r, t:t + 1]).then_inc(squared, 1)
                            act.wait_ge(squared, t + 1)
                            nc.scalar.activation(rstd[0:r, t:t + 1], ssq[0:r, t:t + 1], ACT.Sqrt, scale=1.0 / D,
                                                 bias=eps_col[0:r]).then_inc(rooted, 1)

                @block.vector
                def _(v):
                    if final:
                        v.wait_ge(gain_landed, 16)
                    for t in range(NT):
                        r, b = rows_of(t), t % 2
                        v.wait_ge(first_scaled, t + 1)
                        v.scalar_tensor_tensor(mixed_rows[0:r, b, :], pairs[0:r, b, 1, :], weight[0:r, NT + t:NT + t + 1],
                                               mixed_rows[0:r, b, :], ALU.mult, ALU.add).then_inc(mixed, 1)
                        v.wait_ge(turned, t + 1)
                        if not final:
                            xs = x_T[:, :, t * P:t * P + r]
                            v.tensor_tensor(xs, ps[:, 2 * b:2 * b + 2, :].rearrange("p c (k t) -> p (c k) t", t=P)[:, :, 0:r],
                                            xs, ALU.add).then_inc(added, 1)
                            continue
                        v.wait_ge(mixed, t + 1)
                        if t >= 2:
                            v.wait_ge(y_ready, t - 1)
                        v.tensor_tensor(x_rows[0:r, b, :], ps[0:r, 2 * b:2 * b + 2, :].rearrange("p c n -> p (c n)"),
                                        mixed_rows[0:r, b, :], ALU.add).then_inc(summed, 1)
                        v.wait_ge(rooted, t + 1)
                        v.reciprocal(rstd[0:r, t:t + 1], rstd[0:r, t:t + 1]).then_inc(inverted, 1)
                        v.wait_ge(inverted, t + 1)
                        if t >= 2:
                            v.wait_ge(y_stored[b], 16 * (t // 2))
                        v.scalar_tensor_tensor(y_rows[0:r, b, :], x_rows[0:r, b, :], rstd[0:r, t:t + 1], gain[0:r, :],
                                               ALU.mult, ALU.mult).then_inc(y_ready, 1)

                @block.tensor
                def _(pe):
                    for t in range(NT):
                        r, b = rows_of(t), t % 2
                        if t >= 2:
                            pe.wait_ge(summed if final else added, t - 1)
                        if not final:
                            pe.wait_ge(mixed, t + 1)
                        for k in range(KT):
                            at = (k % 4) * P
                            if final:
                                mm = pe.transpose(ps[0:r, 2 * b + k // 4, at:at + P], x_T[:, k, t * P:t * P + r], ident[:, :])
                            else:
                                mm = pe.transpose(ps[:, 2 * b + k // 4, at:at + r], mixed_rows[0:r, b, k * P:(k + 1) * P],
                                                  ident[0:r, 0:r])
                        mm.then_inc(turned, 1)

        load_stage()
        norm_stage("mix0", V_MIX)
        qkv_stage()
        prompt_attention_stage()
        sample_attention_stage()
        project_back_stage("w_o", w_o[0], o_T, None)
        norm_stage("ffn0", V_FFN)
        route_stage(0)
        expert_stage(0)
        combine_stage(0)
        semaphores_back()
        norm_stage("mix1", V_MIX + 1)
        conv_stage()
        layernorm_stage()
        project_back_stage("w_pw2", w_pw2[0], h_T, V_BPW2)
        norm_stage("ffn1", V_FFN + 1)
        route_stage(1)
        expert_stage(1)
        combine_stage(1)


_INS = ["x_prompt", "x_sample", "cache_k", "cache_v", "state_conv", "w_qkv", "w_o", "attn_sinks",
        "w_pw1", "b_pw1", "w_dw", "b_dw", "conv_ln_g", "conv_ln_b", "w_pw2", "b_pw2", "norm_mix_g", "norm_ffn_g",
        "w_group_router", "b_group_router", "w_expert_router", "b_expert_router",
        "w_gate", "w_up", "w_down", "final_norm_g"]
_OUTS = [(1, NP, D), (NB, NQ, D), (1, 1, WIN, HKV, DH), (1, 1, WIN, HKV, DH), (1, 1, HIST, D),
         (1, NB, WIN, HKV, DH), (1, NB, WIN, HKV, DH), (1, NB, HIST, D)]


def kernel(**inputs):
    import concourse.bacc as bacc
    from concourse.bass_utils import run_bass_kernel_spmd

    nc = bacc.Bacc("TRN2", target_bir_lowering=False, num_devices=1)
    arrays, args = {}, []
    for name in _INS:
        a = np.ascontiguousarray(inputs[name])
        arrays[f"in_{name}"] = a
        args.append(nc.dram_tensor(f"in_{name}", a.shape, mybir.dt.from_np(a.dtype), kind="ExternalInput").ap())
    for i, shape in enumerate(_OUTS):
        args.append(nc.dram_tensor(f"out_{i}", shape, F32, kind="ExternalOutput").ap())
    hybrid_step(nc, *args)
    r = run_bass_kernel_spmd(nc, [arrays], core_ids=[0])
    return tuple(r.results[0][f"out_{i}"] for i in range(len(_OUTS)))
```

```python
from contextlib import ExitStack

import numpy as np

import concourse.bass as bass
from concourse import mybir
from concourse.alu_op_type import AluOpType as ALU

F32 = mybir.dt.float32
I32 = mybir.dt.int32
U32 = mybir.dt.uint32
ACT = mybir.ActivationFunctionType
AX_X = mybir.AxisListType.X
ds = bass.ds

P = 128
D = 1024
KT = D // P
NP, NB, NQ = 512, 8, 4
NS = NB * NQ
T = NP + NS
TH = T // 2
NT = 5
H, HKV, DH = 16, 4, 64
G4 = H // HKV
WIN = 128
CW = 31
HIST = CW - 1
SEG = HIST + NQ
UW = HIST + NP + NB * SEG
NG, EG, NE = 4, 8, 32
NR = NG + NE
F = 256
CAP = 80
CHUNKS = -(-T // CAP)
PAIRS = 2 * T
FAR = 1.0e6
LOW = -3.0e38
HIDE = 1.0e31
EPS = 1e-6
RING = 3
V_MIX, V_FFN, V_BA, V_BG, V_BDW, V_LNG, V_LNB, V_BPW2, V_DW = 0, 2, 4, 5, 6, 7, 8, 9, 10
NV = V_DW + CW
PE_TAPS = 3
ACT_TAPS = 8


def rows_of(t):
    return P if t < 4 else NS


class Steps:

    def __init__(self, eng, sem, start=0):
        self.eng, self.sem, self.start, self.n = eng, sem, start, 0

    def wait_before_last(self):
        self.eng.wait_ge(self.sem, self.start + self.n - 1)

    def done(self, ins):
        ins.then_inc(self.sem, 1)
        self.n += 1

    def wait(self):
        self.eng.wait_ge(self.sem, self.start + self.n)

    def link(self, ins):
        self.done(ins)
        self.wait()


def after(eng, sem, n):
    if not (isinstance(n, int) and n <= 0):
        eng.wait_ge(sem, n)


def settle(eng, sem):
    eng.sem_inc(sem, 1)


def hybrid_step(nc, x_prompt, x_sample, cache_k, cache_v, state_conv, w_qkv, w_o, attn_sinks,
                w_pw1, b_pw1, w_dw, b_dw, conv_ln_g, conv_ln_b, w_pw2, b_pw2, norm_mix_g, norm_ffn_g,
                w_group_router, b_group_router, w_expert_router, b_expert_router,
                w_gate, w_up, w_down, final_norm_g,
                y_prompt, y_sample, k_prompt, v_prompt, conv_prompt, k_sample, v_sample, conv_sample):
    ctx = ExitStack()

    def sb(name, shape, dt=F32):
        return ctx.enter_context(nc.sbuf_tensor(name, shape, dt))

    in_use = []

    def sem(name):
        in_use.append(nc.alloc_semaphore(name))
        return in_use[-1]

    def semaphores_back():
        nc.clear_and_free_semaphores(in_use)
        in_use.clear()
        nc.all_engine_barrier()

    with ctx:
        ps = ctx.enter_context(nc.psum_tensor("ps", [P, 8, 512], F32))
        x_T = sb("x_T", [P, KT, T])
        h_T = sb("h_T", [P, KT, T])
        ring = sb("ring", [P, RING, 6144])
        wring = sb("wring", [P, 2, KT, P])
        areaA = sb("areaA", [P, KT * T])
        areaB = sb("areaB", [P, KT * UW])
        areaC = sb("areaC", [P, KT * T])
        areaS = sb("areaS", [P, 5120])
        ident = sb("ident", [P, P])
        ones = sb("ones", [P, P])
        before = sb("before", [P, P])
        slot_no = sb("slot_no", [P, P])
        chan = sb("chan", [P, KT, NV])
        w_route = sb("w_route", [P, KT, NG + NE])
        small = sb("small", [P, 160])
        idx = sb("idx", [P, 12], U32)
        h_rows = nc.dram_tensor("h_rows", [T, D], F32, kind="Internal").ap()
        pair_rows = nc.dram_tensor("pair_rows", [PAIRS, D], F32, kind="Internal").ap()

        h_flat = h_T[:, :, :].rearrange("p k t -> p (k t)")
        q_T = areaA[:, :].rearrange("p (k t) -> p k t", t=T)
        c_T = q_T
        o_T = areaC[:, :].rearrange("p (k t) -> p k t", t=T)
        v_rows = areaS[:, 2752:2752 + NT * 256].rearrange("p (t n) -> p t n", t=NT)
        k_T = areaS[:, 4032:4032 + 2 * T].rearrange("p (m t) -> p m t", m=2)
        eps_col = small[:, 0:1]
        alibi = areaB[:, 0:H * 256].rearrange("p (h s) -> p h s", h=H)
        sink8, sink_row = areaB[:, 4096:4112], small[0:1, 16:32]
        scratch = ring[:, :, :].rearrange("p s n -> p (s n)")
        s_key_rows = scratch[:, 0:2048].rearrange("p (b n) -> p b n", b=NB)
        s_val_rows = scratch[:, 2048:4096].rearrange("p (b n) -> p b n", b=NB)
        s_keys_T = scratch[:, 4096:6144].rearrange("p (b m s) -> p b m s", b=NB, m=2)
        NK = WIN + NS
        s_bias = scratch[:, 6144:6144 + NB * NK].rearrange("p (b s) -> p b s", b=NB)
        s_q_new = scratch[:, 7424:7424 + KT * NS].rearrange("p (b k t) -> p b k t", b=NB, k=KT)
        s_pick, s_sink_col, s_row = scratch[0:H, 7680:7808], small[0:H, 32:33], small[:, 34:36]
        s_sink8 = small[:, 36:37]
        half = lambda a: a.rearrange("p (c t) -> p c t", c=2)
        x_prompt2 = x_prompt.rearrange("b t d -> (b t) d")
        x_sample2 = x_sample.rearrange("b t d -> (b t) d")

        ring_gate = lambda s: ring[:, s, 0:2048].rearrange("p (k f) -> p k f", f=F)
        ring_up = lambda s: ring[:, s, 2048:4096].rearrange("p (k f) -> p k f", f=F)
        ring_down = lambda s: ring[:, s, 4096:6144].rearrange("p (k n) -> p k n", n=D)

        columns_landed = {}

        def columns(w, at):
            return w.rearrange("(k p) n -> p k n", p=P)[:, :, ds(at, P)]

        def first_columns(sp, name, w, at):
            columns_landed[name] = [nc.alloc_semaphore(f"{name}_weights_landed{s}") for s in range(2)]
            for s in range(2):
                sp.dma_start(wring[:, s], columns(w, at[s])).then_inc(columns_landed[name][s], 16)

        gateup_landed, down_landed = {}, {}
        route_landed = {}
        b_col = small[0:NR, 80:81]

        def load_gateup(sp, l, e, s):
            sp.dma_start(ring_gate(s), w_gate[l, e].rearrange("(k p) f -> p k f", p=P)).then_inc(gateup_landed[l][s], 16)
            sp.dma_start(ring_up(s), w_up[l, e].rearrange("(k p) f -> p k f", p=P)).then_inc(gateup_landed[l][s], 16)

        def load_down(sp, l, e, s):
            sp.dma_start(ring_down(s), w_down[l, e].rearrange("(k p) n -> p k n", p=P)).then_inc(down_landed[l][s], 16)

        w_v = areaB[:, 4352:6400].rearrange("p (k n) -> p k n", k=KT)
        qk_landed, v_landed = [sem(f"qk_weights_landed{s}") for s in range(2)], sem("v_weights_landed")
        w_q = w_qkv[0][:, 0:1024].rearrange("(k p) (m a i c) -> m a i p k c", p=P, m=2, a=2, i=G4)

        def load_queries(sp, j):
            for a in range(2):
                sp.dma_start(wring[:, j % 2, :, a * DH:(a + 1) * DH], w_q[j // 4, a, j % 4]).then_inc(qk_landed[j % 2], 16)

        def load_stage():
            x_in = areaS[:, :].rearrange("p (t d) -> p t d", t=NT)
            vals = areaA[0:NV, 0:D]
            landed = [sem(f"x_landed{t}") for t in range(NT)]
            vals_landed = sem("vals_landed")
            const_step = sem("const_step")
            turned = sem("x_turned")
            copied = sem("x_copied")
            with nc.Block() as block:
                @block.sync
                def _(sp):
                    for t in range(NT):
                        src = x_prompt2[t * P:(t + 1) * P, :] if t < 4 else x_sample2
                        sp.dma_start(x_in[0:rows_of(t), t, :], src).then_inc(landed[t], 16)
                    sp.dma_start(w_v, w_qkv[0][:, 1280:1536].rearrange("(k p) n -> p k n", p=P)).then_inc(v_landed, 16)

                @block.scalar
                def _(act):
                    one = lambda a: a.rearrange("(a n) -> a n", a=1)
                    rows = [(V_MIX, norm_mix_g), (V_FFN, norm_ffn_g), (V_BA, b_pw1.rearrange("l (a n) -> (l a) n", a=2)),
                            (V_BDW, b_dw), (V_LNG, conv_ln_g), (V_LNB, conv_ln_b), (V_BPW2, b_pw2), (V_DW, w_dw[0])]
                    for at, src in rows:
                        act.dma_start(vals[at:at + src.shape[0], :], src).then_inc(vals_landed, 16)

                @block.gpsimd
                def _(gp):
                    c = Steps(gp, const_step)
                    c.done(gp.memset(ident[:, :], 0.0))
                    c.done(gp.memset(ones[:, :], 1.0))
                    c.done(gp.memset(eps_col, EPS))
                    c.done(gp.iota(slot_no[:, :], [[1, P]], base=0, channel_multiplier=0,
                                   allow_small_or_imprecise_dtypes=True))
                    c.wait()
                    c.done(gp.affine_select(ident[:, :], ident[:, :], [[-1, P]], ALU.not_equal, 1.0,
                                            base=0, channel_multiplier=1))
                    c.link(gp.affine_select(before[:, :], ones[:, :], [[1, P]], ALU.is_gt, 0.0,
                                            base=0, channel_multiplier=-1))

                @block.tensor
                def _(pe):
                    pe.wait_ge(const_step, 6)
                    pe.wait_ge(vals_landed, 8 * 16)
                    for k in range(KT):
                        mm = pe.transpose(ps[:, 7, k * NV:(k + 1) * NV], vals[:, k * P:(k + 1) * P], ident[0:NV, 0:NV])
                    mm.then_inc(turned, 1)
                    for t in range(NT):
                        r, b = rows_of(t), 2 * (t % 3)
                        pe.wait_ge(landed[t], 16)
                        if t >= 3:
                            pe.wait_ge(copied, t - 1)
                        for k in range(KT):
                            mm = pe.transpose(ps[:, b + k // 4, (k % 4) * P:(k % 4) * P + r],
                                              x_in[0:r, t, k * P:(k + 1) * P], ident[0:r, 0:r])
                        mm.then_inc(turned, 1)

                @block.vector
                def _(v):
                    v.wait_ge(turned, 1)
                    v.tensor_copy(chan[:, :, :].rearrange("p k n -> p (k n)"), ps[:, 7, 0:KT * NV]).then_inc(copied, 1)
                    for t in range(NT):
                        r, b = rows_of(t), 2 * (t % 3)
                        v.wait_ge(turned, t + 2)
                        v.tensor_copy(x_T[:, :, t * P:t * P + r],
                                      ps[:, b:b + 2, :].rearrange("p b (k t) -> p (b k) t", t=P)[:, :, 0:r]).then_inc(copied, 1)

        std, rstd = areaS[:, 0:T], areaS[:, T:2 * T]

        def norm_stage(name):
            sq = areaS[:, 2 * T:4 * T].rearrange("p (b t) -> p b t", b=2)
            squared, used, rooted = sem(name + "_squared"), sem(name + "_used"), sem(name + "_rooted")
            with nc.Block() as block:
                @block.scalar
                def _(act):
                    for k in range(KT):
                        if k >= 2:
                            act.wait_ge(used, k - 1)
                        nc.scalar.activation(sq[:, k % 2, :], x_T[:, k, :], ACT.Square).then_inc(squared, 1)
                    act.wait_ge(used, KT)
                    nc.scalar.activation(half(std), ps[:, 0:2, 0:TH], ACT.Sqrt, scale=1.0 / D,
                                         bias=eps_col).then_inc(rooted, 1)
                    act.wait_ge(rooted, 1)

                @block.tensor
                def _(pe):
                    for k in range(KT):
                        pe.wait_ge(squared, k + 1)
                        for c in range(2):
                            mm = pe.matmul(ps[:, c, 0:TH], ones[:, :], sq[:, k % 2, c * TH:(c + 1) * TH],
                                           start=(k == 0), stop=(k == KT - 1))
                        mm.then_inc(used, 1)

        def scale_rows(v, gain, inverted, scaled):
            v.reciprocal(rstd, std).then_inc(inverted, 1)
            v.wait_ge(inverted, 1)
            for k in range(KT):
                v.scalar_tensor_tensor(h_T[:, k, :], x_T[:, k, :], chan[:, k, gain:gain + 1], rstd,
                                       ALU.mult, ALU.mult).then_inc(scaled, 1)

        def matmul_block(pe, s, operand, ready=None):
            for k in range(KT):
                if ready is not None:
                    pe.wait_ge(ready, k + 1)
                for c in range(2):
                    mm = pe.matmul(ps[:, 2 * s + c, 0:TH], wring[:, s, k, :], operand[:, k, c * TH:(c + 1) * TH],
                                   start=(k == 0), stop=(k == KT - 1))
            return mm

        def qkv_stage():
            projected = [sem(f"qk_projected{s}") for s in range(2)]
            kept = [sem(f"qk_kept{s}") for s in range(2)]
            v_projected, v_kept = sem("v_projected"), sem("v_kept")
            inverted, scaled = sem("mix0_inverted"), sem("mix0_scaled")
            tables, masks = sem("alibi_step"), sem("sample_mask_step")
            keys_turned, keys_kept = sem("keys_turned"), sem("keys_kept")
            dist = areaC[:, 0:256]
            s_dist = areaC[:, 256:256 + NK]

            head_of_row = np.full(P, -1)
            for r in range(P):
                g, j = r // 32, r % 32 // 4
                if j // 4 == g // 2:
                    head_of_row[r] = G4 * g + j % G4
            pick = (np.arange(H)[:, None] == head_of_row[None, :]).astype(np.float32)
            row_vals = np.stack([np.arange(P) % NQ, np.where(head_of_row >= 0, -8.0 * 2.0 ** (-8.0 * (head_of_row + 1) / H), 0.0)],
                                axis=1).astype(np.float32)
            pick_dram = nc.inline_tensor(pick, "head_pick").ap()
            row_dram = nc.inline_tensor(row_vals, "row_values").ap()

            with nc.Block() as block:
                @block.gpsimd
                def _(gp):
                    c = Steps(gp, tables)
                    c.link(gp.iota(dist, [[-1, 2 * P]], base=WIN, channel_multiplier=1,
                                   allow_small_or_imprecise_dtypes=True))
                    c.link(gp.affine_select(dist, dist, [[-1, 2 * P]], ALU.is_ge, HIDE, base=WIN, channel_multiplier=1))
                    c.link(gp.affine_select(dist, dist, [[1, 2 * P]], ALU.is_gt, HIDE, base=0, channel_multiplier=-1))
                    for h in range(H):
                        c.done(gp.tensor_scalar(alibi[:, h, :], dist, -8.0 * 2.0 ** (-8.0 * (h + 1) / H), None, ALU.mult))
                    d = Steps(gp, masks)
                    d.done(gp.iota(s_dist[:, 0:WIN], [[-1, WIN]], base=WIN, channel_multiplier=0,
                                   allow_small_or_imprecise_dtypes=True))
                    d.done(gp.iota(s_dist[:, WIN:NK], [[0, NB], [-1, NQ]], base=0, channel_multiplier=0,
                                   allow_small_or_imprecise_dtypes=True))
                    d.wait()
                    gp.wait_ge(sink_landed, 64)
                    d.link(gp.tensor_scalar(s_dist, s_dist, s_row[:, 0:1], None, ALU.add))
                    hidden = s_bias[:, 0, :]
                    d.done(gp.tensor_scalar(hidden[:, 0:WIN], s_dist[:, 0:WIN], float(WIN), HIDE, ALU.is_ge, ALU.mult))
                    d.link(gp.tensor_scalar(hidden[:, WIN:NK], s_dist[:, WIN:NK], 0.0, HIDE, ALU.is_lt, ALU.mult))
                    d.link(gp.tensor_tensor(s_dist, s_dist, hidden, ALU.add))
                    d.done(gp.tensor_copy(s_bias[:, :, 0:WIN], s_dist[:, 0:WIN].unsqueeze(1).to_broadcast([P, NB, WIN])))
                    d.link(gp.tensor_copy(s_bias[:, :, WIN:NK], s_dist[:, WIN:NK].unsqueeze(1).to_broadcast([P, NB, NS])))
                    for t in range(NQ):
                        view = s_bias[:, :, WIN:NK].rearrange("p b (c t) -> p b c t", t=NQ)[:, :, :, t]
                        d.done(gp.affine_select(view, view, [[1, NB], [-1, NB]], ALU.is_equal, HIDE,
                                                base=0, channel_multiplier=0))
                    d.wait()
                    d.link(gp.tensor_scalar(s_bias, s_bias, s_row[:, 1:2], None, ALU.mult))
                    c.wait()

                @block.sync
                def _(sp):
                    load_queries(sp, 0)
                    load_queries(sp, 1)
                    sp.dma_start(sink_row, attn_sinks).then_inc(sink_landed, 16)
                    sp.dma_start(s_pick, pick_dram).then_inc(sink_landed, 16)
                    sp.dma_start(s_sink_col, attn_sinks.rearrange("l h -> h l")).then_inc(sink_landed, 16)
                    sp.dma_start(s_row, row_dram).then_inc(sink_landed, 16)
                    sp.dma_start(s_key_rows, cache_k[0].rearrange("b s g d -> s b (g d)")).then_inc(cache_landed, 16)
                    for j in range(2, 8):
                        sp.wait_ge(projected[j % 2], j // 2)
                        load_queries(sp, j)
                    for m in range(2):
                        sp.wait_ge(projected[m], 4)
                        sp.dma_start(wring[:, m], columns(w_qkv[0], 1024 + m * P)).then_inc(qk_landed[m], 32)
                    sp.dma_start(s_val_rows, cache_v[0].rearrange("b s g d -> s b (g d)")).then_inc(vcache_landed, 16)

                @block.tensor
                def _(pe):
                    for s in range(2):
                        pe.wait_ge(qk_landed[s], 32)
                        matmul_block(pe, s, h_T, scaled if s == 0 else None).then_inc(projected[s], 1)
                    pe.wait_ge(v_landed, 16)
                    for t in range(NT):
                        r, b = rows_of(t), 4 + t % 4
                        if t >= 4:
                            pe.wait_ge(v_kept, t - 3)
                        for k in range(KT):
                            mm = pe.matmul(ps[0:r, b, 0:256], h_T[:, k, t * P:t * P + r], w_v[:, k, :],
                                           start=(k == 0), stop=(k == KT - 1))
                        mm.then_inc(v_projected, 1)
                    pe.wait_ge(cache_landed, 16)
                    pe.wait_ge(v_kept, NT)
                    for b in range(NB):
                        for m in range(2):
                            n = 2 * b + m
                            mm = pe.transpose(ps[:, 4 + n // 4, (n % 4) * P:(n % 4 + 1) * P],
                                              s_key_rows[:, b, m * P:(m + 1) * P], ident[:, :])
                    mm.then_inc(keys_turned, 1)
                    with pe.Fori(1, 5) as n:
                        for s in range(2):
                            pe.wait_ge(qk_landed[s], 32 * n + 32)
                            pe.wait_ge(kept[s], n)
                            matmul_block(pe, s, h_T).then_inc(projected[s], 1)

                @block.scalar
                def _(act):
                    def keep(n):
                        act.wait_ge(projected[0], n + 1)
                        nc.scalar.activation(half(q_T[:, ds(2 * n, 1), :].rearrange("p k t -> p (k t)")),
                                             ps[:, 0:2, 0:TH], ACT.Copy).then_inc(kept[0], 1)

                    keep(0)
                    act.wait_ge(keys_turned, 1)
                    nc.scalar.activation(s_keys_T.rearrange("p b m s -> p (b m s)"),
                                         ps[:, 4:8, :].rearrange("p c n -> p (c n)"), ACT.Copy).then_inc(keys_kept, 1)
                    with act.Fori(1, 4) as n:
                        keep(n)
                    act.wait_ge(projected[0], 5)
                    nc.scalar.activation(half(k_T[:, 0, :]), ps[:, 0:2, 0:TH], ACT.Copy).then_inc(kept[0], 1)
                    act.wait_ge(keys_kept, 1)

                @block.vector
                def _(v):
                    scale_rows(v, V_MIX, inverted, scaled)

                    def keep(n):
                        v.wait_ge(projected[1], n + 1)
                        v.tensor_copy(half(q_T[:, ds(2 * n + 1, 1), :].rearrange("p k t -> p (k t)")),
                                      ps[:, 2:4, 0:TH]).then_inc(kept[1], 1)

                    keep(0)
                    for t in range(NT):
                        r, b = rows_of(t), 4 + t % 4
                        v.wait_ge(v_projected, t + 1)
                        v.tensor_copy(v_rows[0:r, t, :], ps[0:r, b, 0:256]).then_inc(v_kept, 1)
                    with v.Fori(1, 4) as n:
                        keep(n)
                    v.wait_ge(projected[1], 5)
                    v.tensor_copy(half(k_T[:, 1, :]), ps[:, 2:4, 0:TH]).then_inc(kept[1], 1)

        def prompt_attention_stage():
            q_blk = h_flat[:, 0:1024].rearrange("p (k t) -> p k t", k=KT)
            k_blk = h_flat[:, 1024:1536].rearrange("p (m s) -> p m s", m=2)
            p_T = h_flat[:, 1536:3584].rearrange("p (b j c q) -> p b j c q", b=2, j=G4, c=2)
            o_blk = areaB[:, 4352:5376]
            probs = areaS[:, 0:2048].rearrange("p (b h s) -> p b h s", b=2, h=G4)
            top, nbias, total, gap, inv = (areaB[:, 4112 + 16 * i:4128 + 16 * i] for i in range(5))
            slots_filled = sem("slots_filled")
            scored, topped, exped = sem("scored"), sem("topped"), sem("exped")
            probs_turned, probs_kept = sem("probs_turned"), sem("probs_kept")
            mixed, sunk, normed = sem("mixed"), sem("sunk"), sem("normed")
            o_turned, o_kept = sem("o_turned"), sem("o_kept")
            scores_seen = sem("scores_seen")
            top_step, norm_step = sem("top_step"), sem("norm_step")
            sunk_exped, total_taken = sem("sunk_exped"), sem("total_taken")
            sink_spread, sink_ready = sem("sink_spread"), sem("sink_ready")
            scores = lambda b: ps[:, 2 * b:2 * b + 2, :].rearrange("p c (h s) -> p (c h) s", s=256)
            turned = ps[:, 4:6, :].rearrange("p c (h s) -> p (c h) s", s=P)
            mix = ps[:, 6:8, :].rearrange("p c n -> p (c n)")

            NBLK = NP // P
            keys_of = lambda n: (slice(P, 2 * P), (1,)) if isinstance(n, int) and n == 0 else (slice(0, 2 * P), (0, 1))

            def blocks(eng, attend):
                attend(0, True, False)
                with eng.Fori(1, NBLK - 1) as n:
                    attend(n, False, False)
                attend(NBLK - 1, False, True)

            with nc.Block() as block:
                @block.gpsimd
                def _(gp):
                    gp.tensor_copy(s_q_new, q_T[:, :, NP:T].rearrange("p k (b t) -> p b k t", b=NB)).then_inc(s_q_ready, 1)

                    def fill(n, first):
                        for m in range(2):
                            if not first:
                                gp.wait_ge(scored, 4 * n + 2 * m - 2)
                            gp.tensor_copy(q_blk[:, 4 * m:4 * m + 4, :],
                                           q_T[:, 4 * m:4 * m + 4, ds(n * P, P)]).then_inc(slots_filled, 1)
                            gp.tensor_copy(k_blk[:, m, :], k_T[:, m, ds(n * P - P, 2 * P)]).then_inc(slots_filled, 1)

                    fill(1, True)
                    with gp.Fori(2, NBLK) as n:
                        fill(n, False)
                    gp.wait_ge(s_q_ready, 1)

                @block.tensor
                def _(pe):
                    pe.wait_ge(sink_landed, 16 * 4)
                    pe.matmul(mix[:, 0:H], ones[0:1, :], sink_row, start=True, stop=True)
                    pe.matmul(mix[:, H:H + 1], s_pick, s_sink_col, start=True, stop=True).then_inc(sink_spread, 1)

                    def score(n, g, early=False):
                        keys, _ = keys_of(n)
                        fixed = isinstance(n, int) and n in (0, NBLK - 1)
                        if fixed:
                            q, keys_at = q_T[:, :, n * P:(n + 1) * P], k_T[:, :, max(n * P - P, 0):(n + 1) * P]
                        else:
                            q, keys_at = q_blk, k_blk
                            if g % 2 == 0:
                                pe.wait_ge(slots_filled, 4 * (n - 1) + 2 * (g // 2) + 2)
                        after(pe, topped, 4 * n + g - 1)
                        lo = DH * (g % 2)
                        for j in range(G4):
                            mm = pe.matmul(scores(g % 2)[:, j, keys], q[lo:lo + DH, 4 * (g // 2) + j, :],
                                           keys_at[lo:lo + DH, g // 2, :], start=True, stop=True)
                        mm.then_inc(scored, 1)

                    def turn(n, g):
                        keys, halves = keys_of(n)
                        pe.wait_ge(exped, 4 * n + g + 1)
                        after(pe, probs_kept, 2 * (4 * n + g))
                        if g == 1:
                            after(pe, o_kept, n)
                        for j in range(G4):
                            for c in halves:
                                mm = pe.transpose(turned[:, 2 * j + c, :], probs[:, g % 2, j, c * P:(c + 1) * P], ident[:, :])
                        mm.then_inc(probs_turned, 1)

                    def mixing(n, g):
                        keys, halves = keys_of(n)
                        pe.wait_ge(probs_kept, 2 * (4 * n + g) + 2)
                        if g == 0:
                            pe.wait_ge(sink_ready, 1)
                            after(pe, normed, n)
                        for j in range(G4):
                            h = G4 * g + j
                            for c in halves:
                                rows = v_rows[:, ds(n - 1 + c, 1), g * DH:(g + 1) * DH].rearrange("p t d -> p (t d)")
                                mm = pe.matmul(mix[:, h * DH:(h + 1) * DH], p_T[:, g % 2, j, c, :], rows,
                                               start=(c == halves[0]), stop=(c == 1))
                        mm.then_inc(mixed, 1)

                    def turn_out(n):
                        pe.wait_ge(normed, n + 1)
                        pe.wait_ge(probs_kept, 2 * min(4 * n + 5, 4 * NBLK) if isinstance(n, int) else 2 * (4 * n + 5))
                        for k in range(KT):
                            mm = pe.transpose(turned[:, k, :], o_blk[:, k * P:(k + 1) * P], ident[:, :])
                        mm.then_inc(o_turned, 1)

                    def attend(n, first, last):
                        if first:
                            score(0, 0)
                            score(0, 1)
                            turn(0, 0)
                        score(n, 2)
                        mixing(n, 0)
                        if not first:
                            turn_out(n - 1)
                        score(n, 3)
                        turn(n, 1)
                        mixing(n, 1)
                        turn(n, 2)
                        if not last:
                            score(n + 1, 0)
                        mixing(n, 2)
                        turn(n, 3)
                        if not last:
                            score(n + 1, 1)
                        mixing(n, 3)
                        if not last:
                            turn(n + 1, 0)
                        else:
                            turn_out(n)

                    blocks(pe, attend)

                @block.scalar
                def _(act):
                    def exps(n, g):
                        keys, _ = keys_of(n)
                        act.wait_ge(topped, 4 * n + g + 1)
                        if g == 0:
                            after(act, total_taken, n)
                        for j in range(G4):
                            h = G4 * g + j
                            e = nc.scalar.activation(probs[:, g % 2, j, keys], probs[:, g % 2, j, keys], ACT.Exp,
                                                     bias=nbias[:, h:h + 1], scale=0.125,
                                                     accum_out=total[:, h:h + 1])
                        e.then_inc(exped, 1)

                    def keep(n, g):
                        _, halves = keys_of(n)
                        act.wait_ge(probs_turned, 4 * n + g + 1)
                        after(act, mixed, 4 * n + g - 1)
                        of = turned[:, 0:4, :].rearrange("p (j c) q -> p j c q", c=2)
                        nc.scalar.activation(p_T[:, g % 2, 0:2, halves[0]:2, :], of[:, :, halves[0]:2, :],
                                             ACT.Copy).then_inc(probs_kept, 1)

                    def attend(n, first, last):
                        if first:
                            exps(0, 0)
                        for g in range(HKV - 1):
                            exps(n, g + 1)
                            if g == HKV - 2:
                                act.wait_ge(sunk, n + 1)
                                nc.scalar.activation(gap, gap, ACT.Exp, scale=0.125).then_inc(sunk_exped, 1)
                            keep(n, g)
                        if not last:
                            exps(n + 1, 0)
                        keep(n, HKV - 1)

                    blocks(act, attend)

                @block.vector
                def _(v):
                    v.wait_ge(sink_spread, 1)
                    v.tensor_scalar(sink8, mix[:, 0:H], 8.0, None, ALU.mult).then_inc(sink_ready, 1)
                    v.tensor_scalar(s_sink8, mix[:, H:H + 1], 8.0, None, ALU.mult).then_inc(sink_ready, 1)
                    v.wait_ge(sink_ready, 2)

                    def tops(n, g):
                        keys, _ = keys_of(n)
                        v.wait_ge(scored, 4 * n + g + 1)
                        after(v, probs_turned, 4 * n + g - 1)
                        settle(v, scores_seen)
                        for j in range(G4):
                            h = G4 * g + j
                            t = v.tensor_tensor_reduce(out=probs[:, g % 2, j, keys], in0=scores(g % 2)[:, j, keys],
                                                       in1=alibi[:, h, keys], scale=1.0, scalar=sink8[:, h:h + 1],
                                                       op0=ALU.add, op1=ALU.max, accum_out=top[:, h:h + 1])
                        t.then_inc(top_step, 1)
                        v.wait_ge(top_step, 4 * n + g + 1)
                        hs = slice(G4 * g, G4 * g + G4)
                        v.tensor_scalar(nbias[:, hs], top[:, hs], -0.125, None, ALU.mult).then_inc(topped, 1)

                    def keep(n, g):
                        _, halves = keys_of(n)
                        v.wait_ge(probs_turned, 4 * n + g + 1)
                        after(v, mixed, 4 * n + g - 1)
                        of = turned[:, 4:8, :].rearrange("p (j c) q -> p j c q", c=2)
                        v.tensor_copy(p_T[:, g % 2, 2:4, halves[0]:2, :], of[:, :, halves[0]:2, :]).then_inc(probs_kept, 1)

                    def keep_out(n):
                        v.wait_ge(o_turned, n + 1)
                        v.tensor_copy(o_T[:, :, ds(n * P, P)], turned).then_inc(o_kept, 1)

                    def attend(n, first, last):
                        if first:
                            tops(0, 0)
                            tops(0, 1)
                        keep(n, 0)
                        tops(n, 2)
                        if not first:
                            keep_out(n - 1)
                        keep(n, 1)
                        tops(n, 3)
                        v.tensor_tensor(gap, sink8, top, ALU.subtract).then_inc(sunk, 1)
                        keep(n, 2)
                        v.wait_ge(exped, 4 * n + 4)
                        v.wait_ge(sunk_exped, n + 1)
                        v.tensor_tensor(total, total, gap, ALU.add).then_inc(total_taken, 1)
                        v.wait_ge(total_taken, n + 1)
                        v.reciprocal(inv, total).then_inc(norm_step, 1)
                        if not last:
                            tops(n + 1, 0)
                        keep(n, 3)
                        if not last:
                            tops(n + 1, 1)
                        v.wait_ge(norm_step, n + 1)
                        v.wait_ge(mixed, 4 * n + 4)
                        v.tensor_tensor(o_blk.rearrange("p (h d) -> p h d", h=H), mix.rearrange("p (h d) -> p h d", h=H),
                                        inv.unsqueeze(2).to_broadcast([P, H, DH]),
                                        ALU.mult).then_inc(normed, 1)
                        if last:
                            keep_out(n)

                    blocks(v, attend)

        def sample_attention_stage():
            probs = h_flat[:, NB * NK:2 * NB * NK].rearrange("p (b s) -> p b s", b=NB)
            p_T = h_flat[:, 2560:3584].rearrange("p (b r) -> p b r", b=NB)
            pn_T = areaS[0:NS, 0:1024].rearrange("p (b r) -> p b r", b=NB)
            o_twice = areaS[:, 1024:2048].rearrange("p (b a d) -> p b a d", b=NB, a=2)
            top, total, gap, inv = (small[:, 40 + 8 * i:48 + 8 * i] for i in range(4))
            k_out = h_flat[:, 3584:3840]
            ks_out = h_flat[0:NS, 3840:4096]

            step, scored = sem("sample_step"), sem("sample_scored")
            shifted, exped, ready = sem("sample_shifted"), sem("sample_exped"), sem("sample_probs_ready")
            turned, kept, mixed = sem("sample_turned"), sem("sample_kept"), sem("sample_mixed")
            o_ready, o_turned = sem("sample_o_ready"), sem("sample_o_turned")
            k_turned, k_kept, o_kept = sem("k_out_turned"), sem("k_out_kept"), sem("sample_o_kept")
            score_tile = lambda g: ps[32 * g:32 * g + 32, 4 * (g % 2):4 * (g % 2) + 4, :]\
                .rearrange("p c (b s) -> p (c b) s", s=256)[:, :, 0:NK]

            with nc.Block() as block:
                @block.sync
                def _(sp):
                    for new, old in ((k_sample, cache_k), (v_sample, cache_v)):
                        sp.dma_start(new[0, :, 0:WIN - NQ].rearrange("b s g d -> b s (g d)"),
                                     old[0, :, NQ:WIN].rearrange("b s g d -> b s (g d)")).then_inc(kv_stored, 16)
                    sp.dma_start(v_prompt[0, 0].rearrange("s g d -> s (g d)"), v_rows[:, 3, :]).then_inc(kv_stored, 16)
                    for b in range(NB):
                        sp.dma_start(v_sample[0, b, WIN - NQ:WIN].rearrange("s g d -> s (g d)"),
                                     v_rows[NQ * b:NQ * b + NQ, 4, :]).then_inc(kv_stored, 16)
                    first_columns(sp, "w_o", w_o[0], (0, P))
                    sp.wait_ge(k_kept, 2)
                    sp.dma_start(k_prompt[0, 0].rearrange("s g d -> s (g d)"), k_out).then_inc(kv_stored, 16)
                    for b in range(NB):
                        sp.dma_start(k_sample[0, b, WIN - NQ:WIN].rearrange("s g d -> s (g d)"),
                                     ks_out[NQ * b:NQ * b + NQ, :]).then_inc(kv_stored, 16)

                @block.tensor
                def _(pe):
                    for g in range(HKV):
                        lo, m = DH * (g % 2), g // 2
                        for b in range(NB):
                            q = s_q_new[lo:lo + DH, b].rearrange("p k t -> p (k t)")
                            out = score_tile(g)[:, b, :]
                            pe.matmul(out[:, 0:WIN], q, s_keys_T[lo:lo + DH, b, m, :], start=True, stop=True)
                            mm = pe.matmul(out[:, WIN:NK], q, k_T[lo:lo + DH, m, NP:T], start=True, stop=True)
                        mm.then_inc(scored, 1)
                    pe.wait_ge(ready, 1)
                    for b in range(NB):
                        pe.transpose(ps[:, b // 4, (b % 4) * P:(b % 4 + 1) * P], probs[:, b, 0:WIN], ident[:, :])
                        mm = pe.transpose(ps[0:NS, 2 + b // 4, (b % 4) * P:(b % 4 + 1) * P], probs[:, b, WIN:NK], ident[:, :])
                    mm.then_inc(turned, 1)
                    for m in range(2):
                        pe.transpose(ps[:, 5, m * P:(m + 1) * P], k_T[:, m, NP - P:NP], ident[:, :])
                        mm = pe.transpose(ps[0:NS, 5, 256 + m * P:256 + (m + 1) * P], k_T[:, m, NP:T], ident[:, :])
                    mm.then_inc(k_turned, 1)
                    pe.wait_ge(kept, 2)
                    pe.wait_ge(vcache_landed, 16)
                    for b in range(NB):
                        for g in range(HKV):
                            out = ps[32 * g:32 * g + 32, 4, b * DH:(b + 1) * DH]
                            pe.matmul(out, p_T[:, b, 32 * g:32 * g + 32], s_val_rows[:, b, g * DH:(g + 1) * DH],
                                      start=True, stop=False)
                            mm = pe.matmul(out, pn_T[:, b, 32 * g:32 * g + 32], v_rows[0:NS, 4, g * DH:(g + 1) * DH],
                                           start=False, stop=True)
                    mm.then_inc(mixed, 1)
                    pe.wait_ge(o_ready, 2)
                    for b in range(NB):
                        mm = pe.transpose(ps[:, 6 + b // 4, (b % 4) * P:(b % 4 + 1) * P],
                                          o_twice[:, b].rearrange("p a d -> p (a d)"), ident[:, :])
                    mm.then_inc(o_turned, 1)

                @block.scalar
                def _(act):
                    act.wait_ge(shifted, 2)
                    nc.scalar.activation(probs, probs, ACT.Exp, scale=0.125).then_inc(exped, 1)
                    nc.scalar.activation(gap, gap, ACT.Exp, scale=0.125).then_inc(exped, 1)
                    act.wait_ge(turned, 1)
                    nc.scalar.activation(p_T.rearrange("p b r -> p (b r)"), ps[:, 0:2, :].rearrange("p c n -> p (c n)"),
                                         ACT.Copy).then_inc(kept, 1)

                @block.vector
                def _(v):
                    s = Steps(v, step)
                    for g in range(HKV):
                        v.wait_ge(scored, g + 1)
                        q = slice(32 * g, 32 * g + 32)
                        s.done(v.tensor_tensor(probs[q], score_tile(g), s_bias[q], ALU.add))
                    s.wait()
                    s.link(v.tensor_reduce(top, probs, AX_X, ALU.max))
                    s.link(v.tensor_scalar(top, top, s_sink8, None, ALU.max))
                    v.tensor_tensor(probs, probs, top.unsqueeze(2).to_broadcast([P, NB, NK]), ALU.subtract).then_inc(shifted, 1)
                    v.tensor_scalar(gap, top, -1.0, s_sink8, ALU.mult, ALU.add).then_inc(shifted, 1)
                    v.wait_ge(exped, 2)
                    s.link(v.tensor_reduce(total, probs, AX_X, ALU.add))
                    s.link(v.tensor_tensor(total, total, gap, ALU.add))
                    s.link(v.reciprocal(inv, total))
                    v.tensor_tensor(probs, probs, inv.unsqueeze(2).to_broadcast([P, NB, NK]), ALU.mult).then_inc(ready, 1)
                    v.wait_ge(turned, 1)
                    v.tensor_copy(pn_T.rearrange("p b r -> p (b r)"), ps[0:NS, 2:4, :].rearrange("p c n -> p (c n)")).then_inc(kept, 1)
                    v.wait_ge(k_turned, 1)
                    v.tensor_copy(k_out, ps[:, 5, 0:256]).then_inc(k_kept, 1)
                    v.tensor_copy(ks_out, ps[0:NS, 5, 256:512]).then_inc(k_kept, 1)
                    v.wait_ge(mixed, 1)
                    for a in range(2):
                        v.tensor_copy(o_twice[:, :, a, :], ps[:, 4, :].rearrange("p (b d) -> p b d", d=DH)).then_inc(o_ready, 1)
                    v.wait_ge(o_turned, 1)
                    spread = ps[:, 6:8, :].rearrange("p c (b r) -> p (c b) r", r=P)
                    for g in range(HKV):
                        for a in range(2):
                            first = 32 * g + 16 * (g // 2) + NQ * a
                            for i in range(2):
                                src = spread[DH * a:DH * a + DH, :, first + 8 * i:first + 8 * i + NQ]
                                dst = o_T[DH * a:DH * a + DH, 2 * g + i, NP:T].rearrange("p (b t) -> p b t", t=NQ)
                                v.tensor_copy(dst, src).then_inc(o_kept, 1)
                    v.wait_ge(o_kept, 16)

        def project_back_stage(name, w, operand, offset, l, rows_stored, stores):
            sq = areaB[:, 0:2 * T].rearrange("p (b t) -> p b t", b=2)
            gateup_landed[l] = [sem(f"gateup_landed{l}{s}") for s in range(RING)]
            down_landed[l] = [sem(f"down_landed{l}{s}") for s in range(RING)]
            landed = columns_landed[name]
            projected = [sem(f"{name}_projected{s}") for s in range(2)]
            added = [sem(f"{name}_added{s}") for s in range(2)]
            squared, summed = sem(f"{name}_squared"), sem(f"{name}_summed")
            route_landed[l] = sem(f"route_weights_landed{l}")
            with nc.Block() as block:
                @block.sync
                def _(sp):
                    sp.dma_start(w_route[:, :, 0:NG], w_group_router[l].rearrange("(k p) g -> p k g", p=P)).then_inc(route_landed[l], 16)
                    sp.dma_start(w_route[:, :, NG:NR], w_expert_router[l].rearrange("(k p) g -> p k g", p=P)).then_inc(route_landed[l], 16)
                    sp.dma_start(b_col[0:NG], b_group_router[l:l + 1, :].rearrange("l g -> g l")).then_inc(route_landed[l], 16)
                    sp.dma_start(b_col[NG:NR], b_expert_router[l:l + 1, :].rearrange("l g -> g l")).then_inc(route_landed[l], 16)
                    with sp.Fori(1, 4) as n:
                        for s in range(2):
                            sp.wait_ge(projected[s], n)
                            sp.dma_start(wring[:, s], columns(w, (2 * n + s) * P)).then_inc(landed[s], 16)
                    for s in range(RING):
                        load_gateup(sp, l, s, s)
                        load_down(sp, l, s, s)
                    sp.wait_ge(rows_stored, 16 * stores)

                @block.tensor
                def _(pe):
                    def sums(k, s, first, last):
                        pe.wait_ge(squared, k + 1)
                        for c in range(2):
                            mm = pe.matmul(ps[:, 4 + c, 0:TH], ones[:, :], sq[:, s, c * TH:(c + 1) * TH],
                                           start=first, stop=last)
                        mm.then_inc(summed, 1)

                    for s in range(2):
                        pe.wait_ge(landed[s], 16)
                        matmul_block(pe, s, operand).then_inc(projected[s], 1)

                    def turn(n):
                        for s in range(2):
                            pe.wait_ge(landed[s], 16 * n + 16)
                            pe.wait_ge(added[s], n)
                            matmul_block(pe, s, operand).then_inc(projected[s], 1)
                            sums(2 * n + s - 2, s, isinstance(n, int) and n == 1 and s == 0, False)

                    turn(1)
                    with pe.Fori(2, 4) as n:
                        turn(n)
                    for s in range(2):
                        sums(KT - 2 + s, s, False, s == 1)

                @block.vector
                def _(v):
                    with v.Fori(0, 4) as n:
                        for s in range(2):
                            v.wait_ge(projected[s], n + 1)
                            xs = half(x_T[:, ds(2 * n + s, 1), :].rearrange("p k t -> p (k t)"))
                            off = 0.0 if offset is None else \
                                chan[:, ds(2 * n + s, 1), offset:offset + 1].rearrange("p k n -> p (k n)")
                            v.scalar_tensor_tensor(xs, ps[:, 2 * s:2 * s + 2, 0:TH], off, xs,
                                                   ALU.add, ALU.add).then_inc(added[s], 1)

                @block.scalar
                def _(act):
                    def square(n, first):
                        for s in range(2):
                            act.wait_ge(added[s], n + 1)
                            if not first:
                                act.wait_ge(summed, 2 * n + s - 1)
                            nc.scalar.activation(sq[:, s, :], x_T[:, ds(2 * n + s, 1), :].rearrange("p k t -> p (k t)"),
                                                 ACT.Square).then_inc(squared, 1)

                    square(0, True)
                    with act.Fori(1, 4) as n:
                        square(n, False)

        def conv_stage():
            u_T = areaB[:, :].rearrange("p (k n) -> p k n", k=KT)
            u_seg = u_T[:, :, HIST + NP:UW].rearrange("p k (b n) -> p k b n", b=NB)
            state_rows = areaA[0:4 * HIST, 0:2048].rearrange("p (i n) -> p i n", i=2)
            sig = areaS[:, 2048:2048 + T]
            prod = areaS[:, 2592:2592 + NS * CW].rearrange("p (r w) -> p r w", w=CW)
            diag = areaS[:, 3584:3584 + 2 * PE_TAPS * P].rearrange("p (b w c) -> p b w c", b=2, w=PE_TAPS)
            w = w_pw1[0]
            inverted, scaled = sem("mix1_inverted"), sem("mix1_scaled")
            state_landed, state_turned, hist_ready = sem("state_landed"), sem("state_turned"), sem("hist_ready")
            landed = columns_landed["pw1"]
            val_done, gate_done = sem("pw1_value_done"), sem("pw1_gate_done")
            sig_done, u_done, diag_ready = sem("sigmoid_done"), sem("u_done"), sem("diag_ready")
            taps_done, conv_done = sem("pe_taps_done"), sem("conv_done")
            product_ready, product_added = sem("product_ready"), sem("product_added")
            hist_copied, u_part = sem("hist_copied"), sem("u_part")
            tap_step, seg_step = sem("tap_step"), sem("seg_step")
            stored = sem("conv_stored")
            products = areaC[:, 0:2048].rearrange("p (b n) -> p b n", b=4)
            product_sum = areaC[:, 2048:2560]
            VEC_FIRST = PE_TAPS + ACT_TAPS
            VEC_STEPS = CW - VEC_FIRST + 1
            acc = lambda b: ps[:, 4 + b, :]
            acc2 = lambda b: ps[:, 6 + b, :]
            col = lambda k, n: chan[:, ds(k, 1), n:n + 1].rearrange("p k n -> p (k n)")
            shifted = lambda k, j: u_T[:, ds(k, 1), j:j + NP].rearrange("p k n -> p (k n)")

            with nc.Block() as block:
                @block.sync
                def _(sp):
                    sp.dma_start(state_rows, state_conv[0].rearrange("(i b) r n -> (b r) i n", i=2)).then_inc(state_landed, 16)
                    sp.dma_start(conv_sample[0, :, 0:HIST - NQ], state_conv[0, :, NQ:HIST]).then_inc(stored, 16)
                    with sp.Fori(1, KT) as k:
                        sp.wait_ge(val_done, k)
                        sp.dma_start(wring[:, 0], columns(w, k * P)).then_inc(landed[0], 16)
                        sp.wait_ge(gate_done, k)
                        sp.dma_start(wring[:, 1], columns(w, k * P + D)).then_inc(landed[1], 16)
                    sp.wait_ge(stored, 16)

                @block.tensor
                def _(pe):
                    pe.wait_ge(state_landed, 16)
                    for i in range(2):
                        for k in range(KT):
                            mm = pe.transpose(ps[:, 4 + 2 * i + k // 4, (k % 4) * P:(k % 4) * P + 4 * HIST],
                                              state_rows[:, i, k * P:(k + 1) * P], ident[0:4 * HIST, 0:4 * HIST])
                    mm.then_inc(state_turned, 1)

                    def value(k, ready=None):
                        pe.wait_ge(landed[0], 16 * k + 16)
                        after(pe, u_done, 2 * k)
                        matmul_block(pe, 0, h_T, ready).then_inc(val_done, 1)

                    def gate(k):
                        pe.wait_ge(landed[1], 16 * k + 16)
                        after(pe, sig_done, k)
                        matmul_block(pe, 1, h_T).then_inc(gate_done, 1)

                    def taps(k, b, early):
                        pe.wait_ge(diag_ready, k + 1)
                        pe.wait_ge(u_done, 2 * k + 2)
                        if not early:
                            pe.wait_ge(conv_done, k - 1)
                        for j in range(PE_TAPS):
                            mm = pe.matmul(acc(b), diag[:, b, j, :],
                                           u_T[:, ds(k, 1), j:j + NP].rearrange("p k n -> p (k n)"),
                                           start=(j == 0), stop=(j == PE_TAPS - 1))
                        mm.then_inc(taps_done, 1)

                    value(0, scaled)
                    gate(0)
                    for k in (1, 2):
                        value(k)
                        gate(k)
                        if k == 1:
                            pe.wait_ge(hist_ready, 1)
                        taps(k - 1, (k - 1) % 2, True)
                    with pe.Fori(1, 3) as i:
                        for j in (1, 2):
                            k = 2 * i + j
                            value(k)
                            gate(k)
                            taps(k - 1, (j - 1) % 2, False)
                    value(7)
                    gate(7)
                    taps(6, 0, False)
                    taps(7, 1, False)
                    pe.wait_ge(u_done, 2 * KT)
                    for k in range(KT):
                        pe.wait_ge(conv_done, k + 1)
                        pe.wait_ge(seg_step, 7 * (k + 1))
                        for c in range(2):
                            pe.matmul(ps[:, c, 0:TH], ones[:, :], c_T[:, k, c * TH:(c + 1) * TH],
                                      start=(k == 0), stop=(k == KT - 1))

                @block.scalar
                def _(act):
                    def diags(k, b):
                        for j in range(PE_TAPS):
                            d = nc.scalar.activation(diag[:, b, j, :], ident[:, :], ACT.Copy,
                                                     scale=chan[:, ds(k, 1), V_DW + j:V_DW + j + 1].rearrange("p k n -> p (k n)"))
                        d.then_inc(diag_ready, 1)

                    def sigmoid(k):
                        act.wait_ge(gate_done, k + 1)
                        after(act, u_done, 2 * k)
                        nc.scalar.activation(half(sig), ps[:, 2:4, 0:TH], ACT.Sigmoid,
                                             bias=chan[:, ds(k, 1), V_BG:V_BG + 1].rearrange("p k n -> p (k n)")).then_inc(sig_done, 1)

                    def multiply(k, first, between=None):
                        act.wait_ge(u_done, 2 * k + 2)
                        for m in range(ACT_TAPS):
                            if m == ACT_TAPS - 2 and between is not None:
                                between()
                            if m >= 4:
                                act.wait_ge(product_added, (ACT_TAPS - 1) * k + max(m - 4, 1))
                            elif not first:
                                act.wait_ge(product_added, (ACT_TAPS - 1) * (k - 1) + m + 4)
                            nc.scalar.activation(products[:, m % 4, :], shifted(k, PE_TAPS + m), ACT.Copy,
                                                 scale=col(k, V_DW + PE_TAPS + m)).then_inc(product_ready, 1)

                    diags(0, 0)
                    sigmoid(0)
                    diags(1, 1)
                    multiply(0, True, lambda: sigmoid(1))
                    with act.Fori(1, 4) as i:
                        for j in range(2):
                            k = 2 * i + j
                            act.wait_ge(taps_done, k - 1)
                            diags(k, j)
                            multiply(k - 1, False, lambda: sigmoid(k))
                    multiply(7, False)

                @block.vector
                def _(v):
                    scale_rows(v, V_MIX + 1, inverted, scaled)
                    v.wait_ge(state_turned, 1)
                    for i in range(2):
                        for c in range(2):
                            v.tensor_copy(u_seg[:, 4 * c:4 * c + 4, 4 * i:4 * i + 4, 0:HIST],
                                          ps[:, 4 + 2 * i + c, :].rearrange("p (k t) -> p k t", k=4)[:, :, 0:4 * HIST]
                                          .rearrange("p k (b r) -> p k b r", b=4)).then_inc(hist_copied, 1)
                    v.wait_ge(hist_copied, 4)
                    v.memset(u_T[:, :, 0:HIST], 0.0).then_inc(hist_ready, 1)

                    def glu(k):
                        v.wait_ge(sig_done, k + 1)
                        ba = chan[:, ds(k, 1), V_BA:V_BA + 1].rearrange("p k n -> p (k n)")
                        uk = u_T[:, ds(k, 1), HIST:HIST + NP].rearrange("p k n -> p (k n)")
                        v.scalar_tensor_tensor(uk[:, 0:TH], ps[:, 0, 0:TH], ba, sig[:, 0:TH],
                                               ALU.add, ALU.mult).then_inc(u_part, 1)
                        v.scalar_tensor_tensor(u_seg[:, ds(k, 1), :, HIST:SEG].rearrange("p k b t -> p (k b) t"),
                                               ps[:, 1, NP - TH:TH].rearrange("p (b t) -> p b t", t=NQ), ba,
                                               sig[:, NP:T].rearrange("p (b t) -> p b t", t=NQ),
                                               ALU.add, ALU.mult).then_inc(u_done, 1)
                        v.wait_ge(u_part, k + 1)
                        v.scalar_tensor_tensor(uk[:, TH:NP], ps[:, 1, 0:NP - TH], ba, sig[:, TH:NP],
                                               ALU.add, ALU.mult).then_inc(u_done, 1)

                    def taps(k, b, js, steps):
                        for j in js:
                            if j == VEC_FIRST:
                                o = v.tensor_scalar(acc2(b), shifted(k, j), col(k, V_DW + j), None, ALU.mult)
                            else:
                                a = (acc2, acc)[(j - VEC_FIRST) % 2](b)
                                if j > VEC_FIRST + 1:
                                    steps.wait_before_last()
                                o = v.scalar_tensor_tensor(a, shifted(k, j), col(k, V_DW + j), a, ALU.mult, ALU.add)
                            steps.done(o)
                    def conv(k, b, last):
                        if not last:
                            glu(k + 1)
                        steps = Steps(v, tap_step, k * VEC_STEPS)
                        v.wait_ge(taps_done, k + 1)
                        taps(k, b, range(VEC_FIRST, CW), steps)
                        steps.wait()
                        out = c_T[:, ds(k, 1), 0:NP].rearrange("p k n -> p (k n)")
                        v.wait_ge(product_added, (ACT_TAPS - 1) * (k + 1))
                        steps.link(v.scalar_tensor_tensor(out, acc2(b), col(k, V_BDW), product_sum, ALU.add, ALU.add))
                        v.tensor_tensor(out, acc(b), out, ALU.add).then_inc(conv_done, 1)

                    glu(0)
                    with v.Fori(0, 3) as i:
                        for j in range(2):
                            conv(2 * i + j, j, False)
                    conv(6, 0, False)
                    conv(7, 1, True)

                @block.gpsimd
                def _(gp):
                    def samples(k):
                        s = Steps(gp, seg_step, 7 * k)
                        gp.wait_ge(u_done, 2 * k + 2)
                        taps = chan[:, ds(k, 1), V_DW:NV]
                        for t in range(NQ):
                            windows = u_seg[:, ds(k, 1), :, t:t + CW].rearrange("p k b w -> p (k b) w")
                            m = gp.tensor_tensor(prod.rearrange("p (b t) w -> p b t w", t=NQ)[:, :, t, :], windows,
                                                 taps.to_broadcast([P, NB, CW]), ALU.mult)
                        s.link(m)
                        out = c_T[:, ds(k, 1), NP:T].rearrange("p k n -> p (k n)")
                        for n in (15, 8, 4, 2):
                            up = CW - n if n == 15 else n
                            s.link(gp.tensor_tensor(prod[:, :, 0:n], prod[:, :, 0:n], prod[:, :, up:up + n], ALU.add))
                        s.link(gp.tensor_tensor(out, prod[:, :, 0], prod[:, :, 1], ALU.add))
                        s.done(gp.tensor_tensor(out, out, col(k, V_BDW).to_broadcast([P, NS]), ALU.add))

                    def add(k):
                        after(gp, conv_done, k)
                        for m in range(1, ACT_TAPS):
                            gp.wait_ge(product_ready, ACT_TAPS * k + m + 1)
                            if m > 1:
                                gp.wait_ge(product_added, (ACT_TAPS - 1) * k + m - 1)
                            gp.tensor_tensor(product_sum, products[:, 0, :] if m == 1 else product_sum,
                                             products[:, m % 4, :], ALU.add).then_inc(product_added, 1)

                    samples(0)
                    add(0)
                    with gp.Fori(1, KT) as k:
                        samples(k)
                        add(k)

        def layernorm_stage():
            u_T = areaB[:, :].rearrange("p (k n) -> p k n", k=KT)
            u_seg = u_T[:, :, HIST + NP:UW].rearrange("p k (b n) -> p k b n", b=NB)
            u_turned, u_kept = sem("u_turned"), sem("u_rows_kept")
            tail = areaS[0:HIST, 0:1024]
            fresh = areaS[0:NS, 1024:2048]
            fresh_T = areaS[:, 3680:3680 + KT * NS].rearrange("p (k t) -> p k t", k=KT)
            fresh_ready = sem("u_fresh_ready")
            sq = areaS[:, 2048:2048 + 2 * T].rearrange("p (b t) -> p b t", b=2)
            rstd = areaS[:, 2048 + 2 * T:2048 + 3 * T]
            centred, squared, summed = sem("ln_centred"), sem("ln_squared"), sem("ln_summed")
            rooted, inverted, scaled, out = sem("ln_rooted"), sem("ln_inverted"), sem("ln_scaled"), sem("ln_out")
            with nc.Block() as block:
                @block.tensor
                def _(pe):
                    pe.wait_ge(fresh_ready, 1)
                    for k in range(KT):
                        pe.transpose(ps[0:HIST, 4 + k // 4, (k % 4) * P:(k % 4 + 1) * P], u_T[:, k, NP:NP + HIST], ident[:, :])
                        mm = pe.transpose(ps[0:NS, 6 + k // 4, (k % 4) * P:(k % 4 + 1) * P],
                                          fresh_T[:, k, :], ident[:, :])
                    mm.then_inc(u_turned, 1)
                    for k in range(KT):
                        pe.wait_ge(squared, k + 1)
                        for c in range(2):
                            mm = pe.matmul(ps[:, 2 + c, 0:TH], ones[:, :], sq[:, k % 2, c * TH:(c + 1) * TH],
                                           start=(k == 0), stop=(k == KT - 1))
                        mm.then_inc(summed, 1)

                @block.vector
                def _(v):
                    v.tensor_copy(fresh_T.rearrange("p k (b t) -> p k b t", b=NB), u_seg[:, :, :, HIST:SEG]).then_inc(fresh_ready, 1)
                    for k in range(KT):
                        v.scalar_tensor_tensor(half(c_T[:, k, :]), ps[:, 0:2, 0:TH], -1.0 / D, half(c_T[:, k, :]),
                                               ALU.mult, ALU.add).then_inc(centred, 1)
                    v.wait_ge(u_turned, 1)
                    v.tensor_copy(tail, ps[0:HIST, 4:6, :].rearrange("p c n -> p (c n)")).then_inc(u_kept, 1)
                    v.tensor_copy(fresh, ps[0:NS, 6:8, :].rearrange("p c n -> p (c n)")).then_inc(u_kept, 1)
                    v.wait_ge(rooted, 1)
                    v.reciprocal(rstd, rstd).then_inc(inverted, 1)
                    v.wait_ge(inverted, 1)
                    for k in range(KT):
                        v.tensor_tensor(c_T[:, k, :], c_T[:, k, :], rstd, ALU.mult).then_inc(scaled, 1)

                @block.sync
                def _(sp):
                    first_columns(sp, "w_pw2", w_pw2[0], (0, P))
                    sp.wait_ge(u_kept, 2)
                    sp.dma_start(conv_prompt[0, 0], tail).then_inc(u_stored, 16)
                    for b in range(NB):
                        sp.dma_start(conv_sample[0, b, HIST - NQ:HIST, :], fresh[NQ * b:NQ * b + NQ, :]).then_inc(u_stored, 16)

                @block.scalar
                def _(act):
                    for k in range(KT):
                        act.wait_ge(centred, k + 1)
                        if k >= 2:
                            act.wait_ge(summed, k - 1)
                        nc.scalar.activation(sq[:, k % 2, :], c_T[:, k, :], ACT.Square).then_inc(squared, 1)
                    act.wait_ge(summed, KT)
                    nc.scalar.activation(half(rstd), ps[:, 2:4, 0:TH], ACT.Sqrt, scale=1.0 / D, bias=eps_col).then_inc(rooted, 1)
                    for k in range(KT):
                        act.wait_ge(scaled, k + 1)
                        nc.scalar.activation(h_T[:, k, :], c_T[:, k, :], ACT.Silu, scale=chan[:, k, V_LNG:V_LNG + 1],
                                             bias=chan[:, k, V_LNB:V_LNB + 1]).then_inc(out, 1)

        area_route = areaS[:, :]
        off = [0]

        def part(n):
            off[0] += n
            return area_route[:, off[0] - n:off[0]]

        logits = part(NT * (NG + NE)).rearrange("p (t e) -> p t e", t=NT)
        picked = [part(NT * NE).rearrange("p (t e) -> p t e", t=NT) for _ in range(2)]
        tagged = [part(NT * NE).rearrange("p (t e) -> p t e", t=NT) for _ in range(2)]
        taken = part(NT * NE).rearrange("p (t e) -> p t e", t=NT)
        hot = part(NT * NE).rearrange("p (t e) -> p t e", t=NT)
        match = part(2 * NT * CAP).rearrange("p (c s) -> p c s", s=CAP)
        far, tok_of, pair_of = part(NE)[0:CAP], part(NE)[0:CAP], part(NE)[0:CAP]
        pair_no, rank, weight = part(2 * NT), part(2 * NT), part(2 * NT)
        g_top, g_sum, e_top, e_next, tie = part(NT), part(NT), part(NT), part(NT), part(NT)
        g_exp, g_hot, g_rev = part(NT * NG).rearrange("p (t g) -> p t g", t=NT), part(NT * NG).rearrange("p (t g) -> p t g", t=NT), part(NE)
        most = part(1)
        most_int = part(1).bitcast(I32)
        assert off[0] <= 5120, off[0]
        rows_in = areaC[:, 0:3 * D].rearrange("p (s n) -> p s n", s=3)
        rows_T = areaA[:, 0:3 * KT * CAP].rearrange("p (s k r) -> p s k r", s=3, k=KT)
        rows_out = areaB[:, 0:3 * D].rearrange("p (s n) -> p s n", s=3)
        hid_buf = areaB[:, 3072:3072 + 3 * F].rearrange("p (a f) -> p a f", a=3)
        gated, hid, hid_T = hid_buf[0:CAP, 0], hid_buf[0:CAP, 1], hid_buf[:, 2, 0:2 * CAP].rearrange("p (k r) -> p k r", k=2)

        def make_table(v, steps, match_ready, table_made, n):
            for c in range(2 * NT):
                m = v.tensor_scalar(match[:, c, :], slot_no[:, 0:CAP], rank[:, c:c + 1], None, ALU.is_equal)
            m.then_inc(match_ready, 1)
            v.wait_ge(table_made, n + 1)
            number = ps[0:CAP, 3, 256:256 + NE]
            steps.link(v.tensor_scalar(far, number, 0.0, FAR, ALU.is_equal, ALU.mult))
            steps.link(v.scalar_tensor_tensor(pair_of, number, -1.0, far, ALU.add, ALU.add))
            steps.link(v.tensor_scalar(far, pair_of, float(T), -float(T), ALU.is_ge, ALU.mult))
            steps.link(v.tensor_tensor(tok_of, pair_of, far, ALU.add))

        TABLE_STEPS = 4

        def table_matmuls(pe, table_made):
            for c in range(2 * NT):
                mm = pe.matmul(ps[0:CAP, 3, 256:256 + NE], match[:, c, :], tagged[c // NT][:, c % NT, :],
                               start=(c == 0), stop=(c == 2 * NT - 1))
            mm.then_inc(table_made, 1)

        def route_stage(l):
            std, rstd = areaB[:, 0:T], areaB[:, T:2 * T]
            h_out = areaB[:, 2048:2048 + 3 * D].rearrange("p (b n) -> p b n", b=3)
            logits_T = areaB[0:NR, 5120:5120 + T]
            rooted, scaled, logits_T_done, logits_T_kept = sem(f"rooted{l}"), sem(f"h_scaled{l}"), sem(f"logits_T_done{l}"), sem(f"logits_T_kept{l}")
            logits_done, turned, kept = sem(f"logits_done{l}"), sem(f"h_turned{l}"), sem(f"h_kept{l}")
            filled, step, exped = sem(f"route_filled{l}"), sem(f"route_step{l}"), sem(f"route_exped{l}")
            dif_ready, choice_ready, ranked = sem(f"route_dif_ready{l}"), sem(f"choice_ready{l}"), sem(f"ranked{l}")
            match_ready, table_made = sem(f"match_ready{l}"), sem(f"table_made{l}")
            h_stored = [sem(f"h_rows_stored{l}{b}") for b in range(3)]
            h_banks = (4, 6, 0)
            route_rows = ps[:, 2, 0:NT * NR].rearrange("p (t e) -> p t e", t=NT)
            rank_cols, count_cols = ps[:, 3, 0:NT * NE], ps[:, 3, NT * NE:(NT + 1) * NE]
            with nc.Block() as block:
                @block.sync
                def _(sp):
                    for t in range(NT):
                        r = rows_of(t)
                        sp.wait_ge(kept, t + 1)
                        sp.dma_start(h_rows[t * P:t * P + r, :], h_out[0:r, t % 3, :]).then_inc(h_stored[t % 3], 16)
                    for b in range(3):
                        sp.wait_ge(h_stored[b], 16 * (2 if b < 2 else 1))

                @block.gpsimd
                def _(gp):
                    gp.iota(pair_no, [[T, 2], [P, NT]], base=1, channel_multiplier=1,
                            allow_small_or_imprecise_dtypes=True).then_inc(filled, 1)
                    gp.iota(g_rev, [[-1, NE]], base=NE, channel_multiplier=0,
                            allow_small_or_imprecise_dtypes=True).then_inc(filled, 1)
                    gp.memset(logits, 0.0).then_inc(filled, 1)
                    gp.memset(rows_in, 0.0).then_inc(filled, 1)
                    gp.wait_ge(filled, 4)

                @block.tensor
                def _(pe):
                    pe.wait_ge(route_landed[l], 64)
                    for k in range(KT):
                        pe.wait_ge(scaled, k + 1)
                        for c in range(2):
                            mm = pe.matmul(ps[0:NR, c, 0:TH], w_route[:, k, :], h_T[:, k, c * TH:(c + 1) * TH],
                                           start=(k == 0), stop=(k == KT - 1))
                    mm.then_inc(logits_T_done, 1)

                    def turn(t):
                        r, b = rows_of(t), h_banks[t % 3]
                        if t >= 3:
                            pe.wait_ge(kept, t - 2)
                        for k in range(KT):
                            mm = pe.transpose(ps[0:r, b + k // 4, (k % 4) * P:(k % 4 + 1) * P],
                                              h_T[:, k, t * P:t * P + r], ident[:, :])
                        mm.then_inc(turned, 1)

                    turn(0)
                    pe.wait_ge(logits_T_kept, 1)
                    for t in range(NT):
                        r = rows_of(t)
                        mm = pe.transpose(route_rows[0:r, t, :], logits_T[:, t * P:t * P + r], ident[0:NR, 0:NR])
                    mm.then_inc(logits_done, 1)
                    for t in range(1, NT):
                        turn(t)
                    pe.wait_ge(choice_ready, 1)
                    for t in range(NT):
                        out = rank_cols[:, t * NE:(t + 1) * NE]
                        for u in range(t + 1):
                            pe.matmul(out, (before if u == t else ones)[:, :], taken[:, u, :], start=(u == 0), stop=(u == t))
                    for u in range(NT):
                        mm = pe.matmul(count_cols, ones[:, :], taken[:, u, :], start=(u == 0), stop=(u == NT - 1))
                    mm.then_inc(ranked, 1)
                    pe.wait_ge(match_ready, 1)
                    table_matmuls(pe, table_made)

                @block.scalar
                def _(act):
                    nc.scalar.activation(half(std), ps[:, 4:6, 0:TH], ACT.Sqrt, scale=1.0 / D, bias=eps_col).then_inc(rooted, 1)

                    def keep(t):
                        r, b = rows_of(t), h_banks[t % 3]
                        act.wait_ge(turned, t + 1)
                        if t >= 3:
                            act.wait_ge(h_stored[t % 3], 16)
                        nc.scalar.activation(h_out[0:r, t % 3, :], ps[0:r, b:b + 2, :].rearrange("p c n -> p (c n)"),
                                             ACT.Copy).then_inc(kept, 1)

                    act.wait_ge(route_landed[l], 64)
                    act.wait_ge(logits_T_done, 1)
                    nc.scalar.activation(half(logits_T), ps[0:NR, 0:2, 0:TH], ACT.Identity, bias=b_col).then_inc(logits_T_kept, 1)
                    for t in range(4):
                        keep(t)
                    act.wait_ge(dif_ready, 1)
                    nc.scalar.activation(g_exp, g_exp, ACT.Exp).then_inc(exped, 1)
                    nc.scalar.activation(tie, tie, ACT.Exp).then_inc(exped, 1)
                    keep(4)

                @block.vector
                def _(v):
                    s = Steps(v, step)
                    wide = lambda a, n: a.unsqueeze(2).to_broadcast([P, NT, n])
                    rev = lambda n: g_rev[:, NE - n:NE].unsqueeze(1).to_broadcast([P, NT, n])
                    v.wait_ge(rooted, 1)
                    s.link(v.reciprocal(rstd, std))
                    for k in range(KT):
                        v.scalar_tensor_tensor(h_T[:, k, :], x_T[:, k, :], chan[:, k, V_FFN + l:V_FFN + l + 1], rstd,
                                               ALU.mult, ALU.mult).then_inc(scaled, 1)
                    v.wait_ge(logits_done, 1)
                    v.wait_ge(filled, 3)
                    s.done(v.tensor_copy(logits[:, 0:4, :], route_rows[:, 0:4, :]))
                    s.link(v.tensor_copy(logits[0:NS, 4, :], route_rows[0:NS, 4, :]))
                    group, expert = logits[:, :, 0:NG], logits[:, :, NG:NG + NE]
                    s.link(v.tensor_reduce(g_top, group, AX_X, ALU.max))
                    s.link(v.tensor_tensor(g_hot, group, wide(g_top, NG), ALU.is_equal))
                    s.link(v.tensor_tensor(g_hot, g_hot, rev(NG), ALU.mult))
                    s.link(v.tensor_reduce(tie, g_hot, AX_X, ALU.max))
                    s.link(v.tensor_tensor(g_hot, g_hot, wide(tie, NG), ALU.is_equal))
                    s.link(v.tensor_tensor(g_exp, group, wide(g_top, NG), ALU.subtract))
                    by_group = lambda a: a.rearrange("p t (g e) -> p (t g) e", g=NG)
                    g_flat = g_hot.rearrange("p t g -> p (t g)").unsqueeze(2).to_broadcast([P, NT * NG, EG])
                    s.link(v.tensor_scalar(by_group(hot), g_flat, -1.0, -LOW, ALU.add, ALU.mult))
                    s.link(v.tensor_copy(taken, expert))
                    s.link(v.tensor_tensor(by_group(taken), by_group(taken), g_flat, ALU.mult))
                    s.link(v.tensor_tensor(taken, taken, hot, ALU.add))
                    for c, top in enumerate((e_top, e_next)):
                        s.link(v.tensor_reduce(top, taken, AX_X, ALU.max))
                        s.link(v.tensor_tensor(hot, taken, wide(top, NE), ALU.is_equal))
                        s.link(v.tensor_tensor(hot, hot, rev(NE), ALU.mult))
                        s.link(v.tensor_reduce(tie, hot, AX_X, ALU.max))
                        s.link(v.tensor_tensor(picked[c], hot, wide(tie, NE), ALU.is_equal))
                        if c == 0:
                            s.link(v.scalar_tensor_tensor(taken, picked[0], LOW, taken, ALU.mult, ALU.add))
                    for c in range(2):
                        s.done(v.memset(picked[c][32:64, 4, :], 0.0))
                        s.done(v.memset(picked[c][64:P, 4, :], 0.0))
                    s.wait()
                    v.tensor_tensor(taken, picked[0], picked[1], ALU.add).then_inc(choice_ready, 1)
                    v.tensor_tensor(tie, e_next, e_top, ALU.subtract).then_inc(dif_ready, 1)
                    for c in range(2):
                        s.link(v.tensor_tensor(tagged[c], picked[c], wide(pair_no[:, c * NT:(c + 1) * NT], NE), ALU.mult))
                    v.wait_ge(exped, 2)
                    s.link(v.tensor_reduce(g_sum, g_exp, AX_X, ALU.add))
                    s.link(v.tensor_scalar(e_top, tie, 1.0, None, ALU.add))
                    s.link(v.tensor_tensor(g_sum, g_sum, e_top, ALU.mult))
                    s.link(v.reciprocal(weight[:, 0:NT], g_sum))
                    s.link(v.tensor_tensor(weight[:, NT:2 * NT], weight[:, 0:NT], tie, ALU.mult))
                    v.wait_ge(ranked, 1)
                    ranks = rank_cols.rearrange("p (t e) -> p t e", t=NT)
                    for c in range(2):
                        s.link(v.tensor_tensor(hot, picked[c], ranks, ALU.mult))
                        s.link(v.tensor_reduce(rank[:, c * NT:(c + 1) * NT], hot, AX_X, ALU.add))
                    s.link(v.tensor_reduce(most, count_cols, AX_X, ALU.max))
                    s.link(v.tensor_copy(most_int, most))
                    make_table(v, s, match_ready, table_made, 0)

        class Nth:

            def __init__(self, i, c):
                self.i, self.c = i, c
                self.e, self.s, self.q = 3 * i + c, c % 3, i + c // 3

            def shift(self, d):
                return Nth(self.i, self.c + d)

        def expert_stage(l):
            gathered = [sem(f"rows_gathered{l}{s}") for s in range(3)]
            scattered = [sem(f"rows_scattered{l}{s}") for s in range(3)]
            tok_ready, pair_ready = sem(f"tok_ready{l}"), sem(f"pair_ready{l}")
            turned, turned_kept = sem(f"rows_turned{l}"), sem(f"rows_T_kept{l}")
            gateup_done, silued, hid_ready = sem(f"gateup_done{l}"), sem(f"silued{l}"), sem(f"hid_ready{l}")
            hid_turned, hid_kept = sem(f"hid_turned{l}"), sem(f"hid_T_kept{l}")
            down_done, out_kept = sem(f"down_done{l}"), sem(f"out_kept{l}")
            pool_settled = sem(f"pool_settled{l}")
            last = NE - 1

            def everywhere(eng, step):
                for e in range(1 + RING):
                    step(Nth(0, e), e == 0, False)
                with eng.Fori(1, (NE - 2) // RING) as i:
                    for u in range(RING):
                        step(Nth(i, 1 + u), False, False)
                step(Nth((NE - 2) // RING, 1), False, True)

            def turn_rows(pe, s):
                for k in range(KT):
                    mm = pe.transpose(ps[:, k // 4, (k % 4) * P:(k % 4) * P + CAP], rows_in[0:CAP, s, k * P:(k + 1) * P], ident[0:CAP, 0:CAP])
                return mm

            def gate_and_up(pe, s, w):
                for a, wt in ((0, ring_gate(w)), (1, ring_up(w))):
                    for k in range(KT):
                        mm = pe.matmul(ps[0:CAP, 2, a * F:(a + 1) * F], rows_T[:, s, k, :], wt[:, k, :],
                                       start=(k == 0), stop=(k == KT - 1))
                return mm

            def turn_hidden(pe):
                for k in range(2):
                    mm = pe.transpose(ps[:, 3, k * P:k * P + CAP], hid[:, k * P:(k + 1) * P], ident[0:CAP, 0:CAP])
                return mm

            def down(pe, w):
                for k in range(2):
                    for c in range(2):
                        mm = pe.matmul(ps[0:CAP, 4 + c, :], hid_T[:, k, :], ring_down(w)[:, k, c * 512:(c + 1) * 512],
                                       start=(k == 0), stop=(k == 1))
                return mm

            def keep_turned(act, s):
                return nc.scalar.activation(rows_T[:, s], ps[:, 0:2, :].rearrange("p c (k r) -> p (c k) r", r=P)[:, :, 0:CAP], ACT.Copy)

            def silu_gate():
                return nc.scalar.activation(gated, ps[0:CAP, 2, 0:F], ACT.Silu)

            def keep_hidden_T():
                return nc.scalar.activation(hid_T, ps[:, 3, 0:F].rearrange("p (k r) -> p k r", k=2)[:, :, 0:CAP], ACT.Copy)

            def fill_idx(gp, s, e, sem_, of, at):
                gp.tensor_copy(idx[0:CAP, at + s:at + s + 1], of[:, ds(e, 1)]).then_inc(sem_, 1)

            def gather(gp, s):
                settle(gp, pool_settled)
                return gp.indirect_dma_start(rows_in[0:CAP, s, :], None, h_rows, bass.IndirectOffsetOnAxis(idx[0:CAP, s:s + 1], 0),
                                             bounds_check=T - 1, oob_is_err=False)

            def scatter(gp, s):
                settle(gp, pool_settled)
                return gp.indirect_dma_start(pair_rows, bass.IndirectOffsetOnAxis(idx[0:CAP, 3 + s:4 + s], 0), rows_out[0:CAP, s, :],
                                             None, bounds_check=PAIRS - 1, oob_is_err=False)

            with nc.Block() as block:
                @block.sync
                def _(sp):
                    def load(x):
                        sp.wait_ge(gateup_done, x.e - 2)
                        load_gateup(sp, l, x.e, x.s)
                        y = x.shift(-1)
                        if not (isinstance(y.e, int) and y.e < RING):
                            sp.wait_ge(down_done, y.e - 2)
                            load_down(sp, l, y.e, y.s)

                    for e in range(RING, 2 * RING):
                        load(Nth(0, e))
                    with sp.Fori(2, NE // RING) as i:
                        for u in range(RING):
                            load(Nth(i, u))
                    for e in range(NE // RING * RING, NE):
                        load(Nth(0, e))
                    sp.wait_ge(down_done, NE - RING)
                    load_down(sp, l, NE - 1, (NE - 1) % RING)

                @block.gpsimd
                def _(gp):
                    def fetch(x):
                        after(gp, gathered[x.s], 16 * x.q)
                        fill_idx(gp, x.s, x.e, tok_ready, tok_of, 0)
                        after(gp, turned, x.e - 2)
                        gp.wait_ge(tok_ready, x.e + 1)
                        gather(gp, x.s).then_inc(gathered[x.s], 16)

                    def store(x):
                        after(gp, scattered[x.s], 16 * x.q)
                        fill_idx(gp, x.s, x.e, pair_ready, pair_of, 3)
                        gp.wait_ge(pair_ready, x.e + 1)
                        gp.wait_ge(out_kept, 2 * x.e + 2)
                        scatter(gp, x.s).then_inc(scattered[x.s], 16)

                    for e in range(5):
                        fetch(Nth(0, e))
                    for e in range(3):
                        fetch(Nth(0, e + 5))
                        store(Nth(0, e))
                    with gp.Fori(1, (NE - 5) // RING) as i:
                        for u in range(RING):
                            fetch(Nth(i, u + 5))
                            store(Nth(i, u))
                    for e in range(NE - 5, NE):
                        store(Nth(0, e))
                    for s in range(3):
                        gp.wait_ge(scattered[s], 16 * len(range(s, NE, 3)))

                @block.tensor
                def _(pe):
                    def turn(x, first):
                        pe.wait_ge(gathered[x.s], 16 * x.q + 16)
                        if not first:
                            pe.wait_ge(turned_kept, x.e)
                        turn_rows(pe, x.s).then_inc(turned, 1)

                    def hidden(x):
                        pe.wait_ge(hid_ready, x.e + 1)
                        turn_hidden(pe).then_inc(hid_turned, 1)

                    def out(x):
                        pe.wait_ge(hid_kept, x.e + 1)
                        pe.wait_ge(down_landed[l][x.s], 16 * x.q + 16)
                        after(pe, out_kept, 2 * x.e)
                        down(pe, x.s).then_inc(down_done, 1)

                    def step(x, first, final):
                        if not final:
                            turn(x.shift(1), False)
                        if not first:
                            hidden(x.shift(-1))
                        pe.wait_ge(turned_kept, x.e + 1)
                        pe.wait_ge(gateup_landed[l][x.s], 32 * x.q + 32)
                        if not first:
                            pe.wait_ge(hid_ready, x.e)
                        gate_and_up(pe, x.s, x.s).then_inc(gateup_done, 1)
                        if not first:
                            out(x.shift(-1))

                    turn(Nth(0, 0), True)
                    everywhere(pe, step)
                    hidden(Nth(0, last))
                    out(Nth(0, last))

                @block.scalar
                def _(act):
                    def turned_rows(x):
                        act.wait_ge(turned, x.e + 1)
                        keep_turned(act, x.s).then_inc(turned_kept, 1)

                    def hidden(x):
                        act.wait_ge(hid_turned, x.e + 1)
                        keep_hidden_T().then_inc(hid_kept, 1)

                    def out(x):
                        act.wait_ge(down_done, x.e + 1)
                        after(act, scattered[x.s], 16 * x.q)
                        nc.scalar.activation(rows_out[0:CAP, x.s, 0:512], ps[0:CAP, 4, :], ACT.Copy).then_inc(out_kept, 1)

                    def step(x, first, final):
                        if not final:
                            turned_rows(x.shift(1))
                        if not first:
                            hidden(x.shift(-1))
                        act.wait_ge(gateup_done, x.e + 1)
                        silu_gate().then_inc(silued, 1)
                        if not first:
                            out(x.shift(-1))

                    turned_rows(Nth(0, 0))
                    everywhere(act, step)
                    hidden(Nth(0, last))
                    out(Nth(0, last))

                @block.vector
                def _(v):
                    def out(x):
                        v.wait_ge(down_done, x.e + 1)
                        after(v, scattered[x.s], 16 * x.q)
                        v.tensor_copy(rows_out[0:CAP, x.s, 512:D], ps[0:CAP, 5, :]).then_inc(out_kept, 1)

                    def step(x, first, final):
                        v.wait_ge(silued, x.e + 1)
                        if not first:
                            v.wait_ge(hid_turned, x.e)
                        v.tensor_tensor(hid, gated, ps[0:CAP, 2, F:2 * F], ALU.mult).then_inc(hid_ready, 1)
                        if not first:
                            out(x.shift(-1))

                    everywhere(v, step)
                    out(Nth(0, last))

            overflow_stage(l, turn_rows, gate_and_up, turn_hidden, down, keep_turned, silu_gate, keep_hidden_T,
                           fill_idx, gather, scatter)

        def overflow_stage(l, turn_rows, gate_and_up, turn_hidden, down, keep_turned, silu_gate, keep_hidden_T,
                           fill_idx, gather, scatter):
            names = ("idle match_ready table_made table_ready table_step landed idx_ready gathered turned turned_kept gateup_done "
                     "silued hid_ready hid_turned hid_kept down_done out_kept scattered").split()
            o = {n: sem(f"more_{n}{l}") for n in names}
            with nc.Block() as block:
                def over(eng, body, before_round=None, before=None):
                    most = eng.value_load(most_int[0:1, 0:1], min_val=0, max_val=T)
                    with eng.If(most > CAP):
                        if before:
                            before()
                        with eng.Fori(0, CHUNKS - 1) as j:
                            if before_round:
                                before_round(j)
                            with eng.Fori(0, NE) as e:
                                body(e, NE * j + e, j)

                @block.sync
                def _(sp):
                    def body(e, n, j):
                        sp.wait_ge(o["idle"], n + 1)
                        for dst, src in ((ring_gate(0), w_gate), (ring_up(0), w_up)):
                            sp.dma_start(dst, src[l, ds(e, 1)].rearrange("e (k p) f -> p (e k) f", p=P)).then_inc(o["landed"], 16)
                        sp.dma_start(ring_down(0), w_down[l, ds(e, 1)].rearrange("e (k p) n -> p (e k) n", p=P)).then_inc(o["landed"], 16)
                    over(sp, body)

                @block.gpsimd
                def _(gp):
                    def body(e, n, j):
                        gp.wait_ge(o["table_ready"], j + 1)
                        fill_idx(gp, 0, e, o["idx_ready"], tok_of, 0)
                        fill_idx(gp, 0, e, o["idx_ready"], pair_of, 3)
                        gp.wait_ge(o["idx_ready"], 2 * n + 2)
                        gather(gp, 0).then_inc(o["gathered"], 16)
                        gp.wait_ge(o["out_kept"], 2 * n + 2)
                        scatter(gp, 0).then_inc(o["scattered"], 16)
                        gp.wait_ge(o["scattered"], 16 * n + 16)
                        gp.sem_inc(o["idle"], 1)
                    over(gp, body, before=lambda: gp.sem_inc(o["idle"], 1))

                @block.tensor
                def _(pe):
                    def table(j):
                        pe.wait_ge(o["match_ready"], j + 1)
                        table_matmuls(pe, o["table_made"])

                    def body(e, n, j):
                        pe.wait_ge(o["gathered"], 16 * n + 16)
                        turn_rows(pe, 0).then_inc(o["turned"], 1)
                        pe.wait_ge(o["turned_kept"], n + 1)
                        pe.wait_ge(o["landed"], 48 * n + 48)
                        gate_and_up(pe, 0, 0).then_inc(o["gateup_done"], 1)
                        pe.wait_ge(o["hid_ready"], n + 1)
                        turn_hidden(pe).then_inc(o["hid_turned"], 1)
                        pe.wait_ge(o["hid_kept"], n + 1)
                        down(pe, 0).then_inc(o["down_done"], 1)
                        pe.wait_ge(o["out_kept"], 2 * n + 2)
                    over(pe, body, table)

                @block.scalar
                def _(act):
                    def body(e, n, j):
                        act.wait_ge(o["turned"], n + 1)
                        keep_turned(act, 0).then_inc(o["turned_kept"], 1)
                        act.wait_ge(o["gateup_done"], n + 1)
                        silu_gate().then_inc(o["silued"], 1)
                        act.wait_ge(o["hid_turned"], n + 1)
                        keep_hidden_T().then_inc(o["hid_kept"], 1)
                        act.wait_ge(o["down_done"], n + 1)
                        nc.scalar.activation(rows_out[0:CAP, 0, 0:512], ps[0:CAP, 4, :], ACT.Copy).then_inc(o["out_kept"], 1)
                    over(act, body)

                @block.vector
                def _(v):
                    def table(j):
                        v.wait_ge(o["idle"], NE * j + 1)
                        s = Steps(v, o["table_step"], (TABLE_STEPS + 1) * j)
                        s.link(v.tensor_scalar(rank, rank, -float(CAP), None, ALU.add))
                        make_table(v, s, o["match_ready"], o["table_made"], j)
                        v.sem_inc(o["table_ready"], 1)

                    def body(e, n, j):
                        v.wait_ge(o["silued"], n + 1)
                        v.tensor_tensor(hid, gated, ps[0:CAP, 2, F:2 * F], ALU.mult).then_inc(o["hid_ready"], 1)
                        v.wait_ge(o["down_done"], n + 1)
                        v.tensor_copy(rows_out[0:CAP, 0, 512:D], ps[0:CAP, 5, :]).then_inc(o["out_kept"], 1)
                    over(v, body, table)

        def combine_stage(l):
            final = l == 1
            flat = ring[:, :, :].rearrange("p s n -> p (s n)")
            pairs = flat[:, 0:NT * 2 * D].rearrange("p (t c n) -> p t c n", t=NT, c=2)
            x_rows = flat[:, NT * 2 * D:NT * 3 * D].rearrange("p (t n) -> p t n", t=NT)
            gain = areaC[:, 0:D]
            square = areaC[:, D:2 * D]
            ssq, rstd = small[:, 120:125], small[:, 125:130]
            landed = [sem(f"pairs_landed{l}{t}") for t in range(NT)]
            banks = lambda t: ps[:, 2 * (t % 4):2 * (t % 4) + 2, :]

            def load_pairs(sp):
                by_choice = pair_rows.rearrange("(c t) n -> t c n", c=2)
                for t in range(NT):
                    r = rows_of(t)
                    sp.dma_start(pairs[0:r, t], by_choice[t * P:t * P + r]).then_inc(landed[t], 16)

            def to_stream():
                first_scaled, mixed = sem("first_scaled"), sem("pairs_mixed")
                turned, added = sem("mixed_turned"), sem("mixed_added")
                with nc.Block() as block:
                    @block.sync
                    def _(sp):
                        load_pairs(sp)
                        first_columns(sp, "pw1", w_pw1[0], (0, D))

                    @block.scalar
                    def _(act):
                        for t in range(NT):
                            r = rows_of(t)
                            act.wait_ge(landed[t], 16)
                            nc.scalar.activation(x_rows[0:r, t, :], pairs[0:r, t, 0, :], ACT.Copy,
                                                 scale=weight[0:r, t:t + 1]).then_inc(first_scaled, 1)

                    @block.tensor
                    def _(pe):
                        for t in range(NT):
                            r = rows_of(t)
                            pe.wait_ge(mixed, t + 1)
                            if t >= 4:
                                pe.wait_ge(added, t - 3)
                            for k in range(KT):
                                mm = pe.transpose(banks(t)[:, k // 4, (k % 4) * P:(k % 4) * P + r],
                                                  x_rows[0:r, t, k * P:(k + 1) * P], ident[0:r, 0:r])
                            mm.then_inc(turned, 1)

                    @block.vector
                    def _(v):
                        def mix(t):
                            r = rows_of(t)
                            v.wait_ge(first_scaled, t + 1)
                            v.scalar_tensor_tensor(x_rows[0:r, t, :], pairs[0:r, t, 1, :], weight[0:r, NT + t:NT + t + 1],
                                                   x_rows[0:r, t, :], ALU.mult, ALU.add).then_inc(mixed, 1)

                        def add(t):
                            r = rows_of(t)
                            v.wait_ge(turned, t + 1)
                            xs = x_T[:, :, t * P:t * P + r]
                            v.tensor_tensor(xs, banks(t).rearrange("p c (k t) -> p (c k) t", t=P)[:, :, 0:r],
                                            xs, ALU.add).then_inc(added, 1)

                        for t in range(NT):
                            mix(t)
                            if t >= 1:
                                add(t - 1)
                        add(NT - 1)
                        v.wait_ge(added, NT)

            def to_outputs():
                turned, summed = sem("x_rows_turned"), sem("final_summed")
                first_added, squared, rooted, inverted = sem("first_added"), sem("final_squared"), sem("final_rooted"), sem("final_inverted")
                scaled, gain_landed, y_stored = sem("y_scaled"), sem("gain_landed"), sem("y_stored")
                y_ready = [sem(f"y_ready{t}") for t in range(NT)]
                on_pool = (1, 3)
                with nc.Block() as block:
                    @block.sync
                    def _(sp):
                        load_pairs(sp)
                        for t in range(NT):
                            r = rows_of(t)
                            dst = y_prompt.rearrange("b t d -> (b t) d")[t * P:(t + 1) * P, :] if t < 4 \
                                else y_sample.rearrange("b t d -> (b t) d")
                            sp.wait_ge(y_ready[t], 1)
                            sp.dma_start(dst, pairs[0:r, t, 1, :]).then_inc(y_stored, 16)
                        sp.wait_ge(y_stored, 16 * NT)

                    @block.tensor
                    def _(pe):
                        for t in range(NT):
                            r = rows_of(t)
                            if t >= 4:
                                pe.wait_ge(first_added, t - 3)
                            for k in range(KT):
                                mm = pe.transpose(banks(t)[0:r, k // 4, (k % 4) * P:(k % 4 + 1) * P],
                                                  x_T[:, k, t * P:t * P + r], ident[:, :])
                            mm.then_inc(turned, 1)

                    @block.gpsimd
                    def _(gp):
                        gp.dma_start(gain, final_norm_g.rearrange("(a n) -> a n", a=1).to_broadcast([P, D])).then_inc(gain_landed, 16)
                        gp.wait_ge(gain_landed, 16)
                        for n, t in enumerate(on_pool):
                            r = rows_of(t)
                            gp.wait_ge(scaled, n + 1)
                            gp.tensor_tensor(pairs[0:r, t, 1, :], pairs[0:r, t, 0, :], gain[0:r, :], ALU.mult).then_inc(y_ready[t], 1)

                    @block.scalar
                    def _(act):
                        def root(t):
                            r = rows_of(t)
                            act.wait_ge(summed, t + 1)
                            nc.scalar.activation(square[0:r, :], x_rows[0:r, t, :], ACT.Square,
                                                 accum_out=ssq[0:r, t:t + 1]).then_inc(squared, 1)
                            act.wait_ge(squared, t + 1)
                            nc.scalar.activation(rstd[0:r, t:t + 1], ssq[0:r, t:t + 1], ACT.Sqrt, scale=1.0 / D,
                                                 bias=eps_col[0:r]).then_inc(rooted, 1)

                        for t in range(NT):
                            root(t)
                            if t in on_pool:
                                act.wait_ge(inverted, t + 1)
                                r = rows_of(t)
                                nc.scalar.activation(pairs[0:r, t, 0, :], x_rows[0:r, t, :], ACT.Copy,
                                                     scale=rstd[0:r, t:t + 1]).then_inc(scaled, 1)

                    @block.vector
                    def _(v):
                        def add_up(t):
                            r = rows_of(t)
                            v.wait_ge(turned, t + 1)
                            v.wait_ge(landed[t], 16)
                            v.scalar_tensor_tensor(x_rows[0:r, t, :], pairs[0:r, t, 0, :], weight[0:r, t:t + 1],
                                                   banks(t)[0:r].rearrange("p c n -> p (c n)"), ALU.mult, ALU.add).then_inc(first_added, 1)
                            v.wait_ge(first_added, t + 1)
                            v.scalar_tensor_tensor(x_rows[0:r, t, :], pairs[0:r, t, 1, :], weight[0:r, NT + t:NT + t + 1],
                                                   x_rows[0:r, t, :], ALU.mult, ALU.add).then_inc(summed, 1)

                        def finish(t):
                            r = rows_of(t)
                            v.wait_ge(rooted, t + 1)
                            v.reciprocal(rstd[0:r, t:t + 1], rstd[0:r, t:t + 1]).then_inc(inverted, 1)
                            if t in on_pool:
                                return
                            v.wait_ge(inverted, t + 1)
                            v.wait_ge(gain_landed, 16)
                            v.scalar_tensor_tensor(pairs[0:r, t, 1, :], x_rows[0:r, t, :], rstd[0:r, t:t + 1], gain[0:r, :],
                                                   ALU.mult, ALU.mult).then_inc(y_ready[t], 1)

                        add_up(0)
                        for t in range(1, NT):
                            add_up(t)
                            finish(t - 1)
                        finish(NT - 1)

            if final:
                to_outputs()
            else:
                to_stream()

        kv_stored = sem("kv_stored")
        sink_landed, s_q_ready = sem("sink_landed"), sem("sample_q_ready")
        cache_landed, vcache_landed = sem("cache_landed"), sem("vcache_landed")
        load_stage()
        norm_stage("mix0")
        qkv_stage()
        prompt_attention_stage()
        sample_attention_stage()
        project_back_stage("w_o", w_o[0], o_T, None, 0, kv_stored, 4 + 2 * NB)
        route_stage(0)
        expert_stage(0)
        combine_stage(0)
        semaphores_back()
        norm_stage("mix1")
        u_stored = sem("u_rows_stored")
        conv_stage()
        layernorm_stage()
        project_back_stage("w_pw2", w_pw2[0], h_T, V_BPW2, 1, u_stored, 1 + NB)
        route_stage(1)
        expert_stage(1)
        combine_stage(1)


_INS = ["x_prompt", "x_sample", "cache_k", "cache_v", "state_conv", "w_qkv", "w_o", "attn_sinks",
        "w_pw1", "b_pw1", "w_dw", "b_dw", "conv_ln_g", "conv_ln_b", "w_pw2", "b_pw2", "norm_mix_g", "norm_ffn_g",
        "w_group_router", "b_group_router", "w_expert_router", "b_expert_router",
        "w_gate", "w_up", "w_down", "final_norm_g"]
_OUTS = [(1, NP, D), (NB, NQ, D), (1, 1, WIN, HKV, DH), (1, 1, WIN, HKV, DH), (1, 1, HIST, D),
         (1, NB, WIN, HKV, DH), (1, NB, WIN, HKV, DH), (1, NB, HIST, D)]


def kernel(**inputs):
    import concourse.bacc as bacc
    from concourse.bass_utils import run_bass_kernel_spmd

    nc = bacc.Bacc("TRN2", target_bir_lowering=False, num_devices=1)
    arrays, args = {}, []
    for name in _INS:
        a = np.ascontiguousarray(inputs[name])
        arrays[f"in_{name}"] = a
        args.append(nc.dram_tensor(f"in_{name}", a.shape, mybir.dt.from_np(a.dtype), kind="ExternalInput").ap())
    for i, shape in enumerate(_OUTS):
        args.append(nc.dram_tensor(f"out_{i}", shape, F32, kind="ExternalOutput").ap())
    hybrid_step(nc, *args)
    r = run_bass_kernel_spmd(nc, [arrays], core_ids=[0])
    return tuple(r.results[0][f"out_{i}"] for i in range(len(_OUTS)))
```

```python
from contextlib import ExitStack

import numpy as np

import concourse.bass as bass
from concourse import mybir
from concourse.alu_op_type import AluOpType as ALU

F32 = mybir.dt.float32
F32R = mybir.dt.float32r
I32 = mybir.dt.int32
U32 = mybir.dt.uint32
ACT = mybir.ActivationFunctionType
AX_X = mybir.AxisListType.X
ds = bass.ds

P = 128
D = 1024
KT = D // P
NP, NB, NQ = 512, 8, 4
NS = NB * NQ
T = NP + NS
TH = T // 2
NT = 5
H, HKV, DH = 16, 4, 64
G4 = H // HKV
WIN = 128
CW = 31
HIST = CW - 1
SEG = HIST + NQ
UW = HIST + NP + NB * SEG
NG, EG, NE = 4, 8, 32
NR = NG + NE
F = 256
CAP = 80
CHUNKS = -(-T // CAP)
PAIRS = 2 * T
FAR = 1.0e6
LOW = -3.0e38
HIDE = 1.0e31
EPS = 1e-6
RING = 3
V_MIX, V_FFN, V_BA, V_BG, V_BDW, V_LNG, V_LNB, V_BPW2, V_DW = 0, 2, 4, 5, 6, 7, 8, 9, 10
NV = V_DW + CW
PE_TAPS = 3
ACT_TAPS = 8
END_TAPS = 10
assert ACT_TAPS % 4 == 0


def rows_of(t):
    return P if t < 4 else NS


class Steps:

    def __init__(self, eng, sem, start=0):
        self.eng, self.sem, self.start, self.n = eng, sem, start, 0

    def wait_before_last(self):
        self.eng.wait_ge(self.sem, self.start + self.n - 1)

    def done(self, ins):
        ins.then_inc(self.sem, 1)
        self.n += 1

    def wait(self):
        self.eng.wait_ge(self.sem, self.start + self.n)

    def link(self, ins):
        self.done(ins)
        self.wait()


def after(eng, sem, n):
    if not (isinstance(n, int) and n <= 0):
        eng.wait_ge(sem, n)


def settle(eng, sem):
    eng.sem_inc(sem, 1)


def hybrid_step(nc, x_prompt, x_sample, cache_k, cache_v, state_conv, w_qkv, w_o, attn_sinks,
                w_pw1, b_pw1, w_dw, b_dw, conv_ln_g, conv_ln_b, w_pw2, b_pw2, norm_mix_g, norm_ffn_g,
                w_group_router, b_group_router, w_expert_router, b_expert_router,
                w_gate, w_up, w_down, final_norm_g,
                y_prompt, y_sample, k_prompt, v_prompt, conv_prompt, k_sample, v_sample, conv_sample):
    ctx = ExitStack()

    def sb(name, shape, dt=F32):
        return ctx.enter_context(nc.sbuf_tensor(name, shape, dt))

    in_use = []

    def sem(name):
        in_use.append(nc.alloc_semaphore(name))
        return in_use[-1]

    def semaphores_back():
        nc.clear_and_free_semaphores(in_use)
        in_use.clear()
        nc.all_engine_barrier()

    with ctx:
        ps = ctx.enter_context(nc.psum_tensor("ps", [P, 8, 512], F32))
        x_T = sb("x_T", [P, KT, T])
        at = {}
        at["h_T"] = nc.sbuf_base
        h_T = sb("h_T", [P, KT, T])
        at["ring"] = nc.sbuf_base
        ring = sb("ring", [P, RING, 6144])
        wring = sb("wring", [P, 2, KT, P])
        at["A"] = nc.sbuf_base
        areaA = sb("areaA", [P, KT * T])
        at["B"] = nc.sbuf_base
        areaB = sb("areaB", [P, KT * UW])
        at["C"] = nc.sbuf_base
        areaC = sb("areaC", [P, KT * T])
        areaS = sb("areaS", [P, 5120])
        ident = sb("ident", [P, P])
        ones = sb("ones", [P, P])
        before = sb("before", [P, P])
        slot_no = sb("slot_no", [P, P])
        chan = sb("chan", [P, KT, NV])
        w_route = sb("w_route", [P, KT, NG + NE])
        small = sb("small", [P, 160])
        idx = sb("idx", [P, 12], U32)
        h_rows = nc.dram_tensor("h_rows", [T, D], F32, kind="Internal").ap()
        pair_rows = nc.dram_tensor("pair_rows", [PAIRS, D], F32, kind="Internal").ap()

        def halves(name, shape, area, first=0):
            return nc.alloc_sbuf_tensor_at(name, shape, F32R, offset=at[area] + 4 * first)

        w_halves_C = halves("w_halves_C", [P, 2, 2, KT, P], "C")
        w_halves_A = halves("w_halves_A", [P, 2, 2, KT, P], "A")
        x_halves = halves("x_halves", [P, 2, KT, T], "ring", 9728)
        down_halves = halves("down_halves", [P, 2, 2, D], "h_T")
        hid_halves = halves("hid_T_halves", [P, 2, 2, CAP], "A", 4032)
        qkv_operand = (x_halves[:, 0], x_halves[:, 1])
        back_operand = (halves("x_high", [P, KT, T], "h_T")[:, :, :], halves("x_low", [P, KT, T], "B", 2048)[:, :, :])

        h_flat = h_T[:, :, :].rearrange("p k t -> p (k t)")
        q_T = areaA[:, :].rearrange("p (k t) -> p k t", t=T)
        c_T = q_T
        o_T = areaC[:, :].rearrange("p (k t) -> p k t", t=T)
        v_rows = areaS[:, 2752:2752 + NT * 256].rearrange("p (t n) -> p t n", t=NT)
        k_T = areaS[:, 4032:4032 + 2 * T].rearrange("p (m t) -> p m t", m=2)
        state_rows = areaA[0:4 * HIST, 0:2048].rearrange("p (i n) -> p i n", i=2)
        eps_col = small[:, 0:1]
        alibi = areaB[:, 0:H * 256].rearrange("p (h s) -> p h s", h=H)
        sink8, sink_row = areaB[:, 4096:4112], small[0:1, 16:32]
        scratch = ring[:, :, :].rearrange("p s n -> p (s n)")
        s_key_rows = scratch[:, 0:2048].rearrange("p (b n) -> p b n", b=NB)
        s_val_rows = scratch[:, 2048:4096].rearrange("p (b n) -> p b n", b=NB)
        s_keys_T = scratch[:, 4096:6144].rearrange("p (b m s) -> p b m s", b=NB, m=2)
        NK = WIN + NS
        s_bias = scratch[:, 6144:6144 + NB * NK].rearrange("p (b s) -> p b s", b=NB)
        s_q_new = scratch[:, 7424:7424 + KT * NS].rearrange("p (b k t) -> p b k t", b=NB, k=KT)
        s_pick, s_sink_col, s_row = scratch[0:H, 7680:7808], small[0:H, 32:33], small[:, 34:36]
        s_sink8 = small[:, 36:37]
        half = lambda a: a.rearrange("p (c t) -> p c t", c=2)
        x_prompt2 = x_prompt.rearrange("b t d -> (b t) d")
        x_sample2 = x_sample.rearrange("b t d -> (b t) d")

        ring_gate = lambda s: ring[:, s, 0:2048].rearrange("p (k f) -> p k f", f=F)
        ring_up = lambda s: ring[:, s, 2048:4096].rearrange("p (k f) -> p k f", f=F)
        ring_down = lambda s: ring[:, s, 4096:6144].rearrange("p (k n) -> p k n", n=D)

        columns_landed = {}

        def columns(w, at):
            return w.rearrange("(k p) n -> p k n", p=P)[:, :, ds(at, P)]

        def first_columns(sp, name, w, at):
            columns_landed[name] = [nc.alloc_semaphore(f"{name}_weights_landed{s}") for s in range(2)]
            for s in range(2):
                sp.dma_start(wring[:, s], columns(w, at[s])).then_inc(columns_landed[name][s], 16)

        gateup_landed, down_landed = {}, {}
        route_landed = {}
        b_rows = small[:, 84:84 + NR]
        route_scaled = {}

        def load_gateup(sp, l, e, s):
            sp.dma_start(ring_gate(s), w_gate[l, e].rearrange("(k p) f -> p k f", p=P)).then_inc(gateup_landed[l][s], 16)
            sp.dma_start(ring_up(s), w_up[l, e].rearrange("(k p) f -> p k f", p=P)).then_inc(gateup_landed[l][s], 16)

        def load_down(sp, l, e, s):
            sp.dma_start(ring_down(s), w_down[l, e].rearrange("(k p) n -> p k n", p=P)).then_inc(down_landed[l][s], 16)

        w_v = areaB[:, 4352:6400].rearrange("p (k n) -> p k n", k=KT)
        qk_landed, v_landed = [sem(f"qk_weights_landed{s}") for s in range(2)], sem("v_weights_landed")
        w_q = w_qkv[0][:, 0:1024].rearrange("(k p) (m a i c) -> m a i p k c", p=P, m=2, a=2, i=G4)

        def load_queries(sp, j):
            for a in range(2):
                sp.dma_start(wring[:, j % 2, :, a * DH:(a + 1) * DH], w_q[j // 4, a, j % 4]).then_inc(qk_landed[j % 2], 16)

        def load_stage():
            x_in = areaS[:, :].rearrange("p (t d) -> p t d", t=NT)
            vals = areaA[0:NV, 0:D]
            landed = [sem(f"x_landed{t}") for t in range(NT)]
            vals_landed = sem("vals_landed")
            const_step = sem("const_step")
            turned = sem("x_turned")
            copied = sem("x_copied")
            with nc.Block() as block:
                @block.sync
                def _(sp):
                    for t in range(NT):
                        src = x_prompt2[t * P:(t + 1) * P, :] if t < 4 else x_sample2
                        sp.dma_start(x_in[0:rows_of(t), t, :], src).then_inc(landed[t], 16)
                    sp.dma_start(w_v, w_qkv[0][:, 1280:1536].rearrange("(k p) n -> p k n", p=P)).then_inc(v_landed, 16)

                @block.scalar
                def _(act):
                    one = lambda a: a.rearrange("(a n) -> a n", a=1)
                    rows = [(V_MIX, norm_mix_g), (V_FFN, norm_ffn_g), (V_BA, b_pw1.rearrange("l (a n) -> (l a) n", a=2)),
                            (V_BDW, b_dw), (V_LNG, conv_ln_g), (V_LNB, conv_ln_b), (V_BPW2, b_pw2), (V_DW, w_dw[0])]
                    for at, src in rows:
                        act.dma_start(vals[at:at + src.shape[0], :], src).then_inc(vals_landed, 16)

                @block.gpsimd
                def _(gp):
                    c = Steps(gp, const_step)
                    c.done(gp.memset(ident[:, :], 0.0))
                    c.done(gp.memset(ones[:, :], 1.0))
                    c.done(gp.memset(eps_col, EPS))
                    c.done(gp.iota(slot_no[:, :], [[1, P]], base=0, channel_multiplier=0,
                                   allow_small_or_imprecise_dtypes=True))
                    c.wait()
                    c.done(gp.affine_select(ident[:, :], ident[:, :], [[-1, P]], ALU.not_equal, 1.0,
                                            base=0, channel_multiplier=1))
                    c.link(gp.affine_select(before[:, :], ones[:, :], [[1, P]], ALU.is_gt, 0.0,
                                            base=0, channel_multiplier=-1))

                @block.tensor
                def _(pe):
                    pe.wait_ge(const_step, 6)
                    for t in range(NT):
                        r, b = rows_of(t), 2 * (t % 3)
                        pe.wait_ge(landed[t], 16)
                        if t >= 3:
                            pe.wait_ge(copied, t - 2)
                        for k in range(KT):
                            mm = pe.transpose(ps[:, b + k // 4, (k % 4) * P:(k % 4) * P + r],
                                              x_in[0:r, t, k * P:(k + 1) * P], ident[0:r, 0:r])
                        mm.then_inc(turned, 1)
                    pe.wait_ge(vals_landed, 8 * 16)
                    for k in range(KT):
                        mm = pe.transpose(ps[:, 7, k * NV:(k + 1) * NV], vals[:, k * P:(k + 1) * P], ident[0:NV, 0:NV])
                    mm.then_inc(turned, 1)

                @block.vector
                def _(v):
                    for t in range(NT):
                        r, b = rows_of(t), 2 * (t % 3)
                        v.wait_ge(turned, t + 1)
                        v.tensor_copy(x_T[:, :, t * P:t * P + r],
                                      ps[:, b:b + 2, :].rearrange("p b (k t) -> p (b k) t", t=P)[:, :, 0:r]).then_inc(copied, 1)
                    v.wait_ge(turned, NT + 1)
                    v.tensor_copy(chan[:, :, :].rearrange("p k n -> p (k n)"), ps[:, 7, 0:KT * NV]).then_inc(copied, 1)

        std, rstd = areaS[:, 0:T], areaS[:, T:2 * T]

        def norm_stage(name, prefetch=None):
            sq = areaS[:, 2 * T:4 * T].rearrange("p (b t) -> p b t", b=2)
            squared, used, rooted = sem(name + "_squared"), sem(name + "_used"), sem(name + "_rooted")
            with nc.Block() as block:
                @block.sync
                def _(sp):
                    if prefetch:
                        prefetch(sp)

                @block.scalar
                def _(act):
                    for k in range(KT):
                        if k >= 2:
                            act.wait_ge(used, k - 1)
                        nc.scalar.activation(sq[:, k % 2, :], x_T[:, k, :], ACT.Square).then_inc(squared, 1)
                    act.wait_ge(used, KT)
                    nc.scalar.activation(half(std), ps[:, 0:2, 0:TH], ACT.Sqrt, scale=1.0 / D,
                                         bias=eps_col).then_inc(rooted, 1)
                    act.wait_ge(rooted, 1)

                @block.tensor
                def _(pe):
                    for k in range(KT):
                        pe.wait_ge(squared, k + 1)
                        for c in range(2):
                            mm = pe.matmul(ps[:, c, 0:TH], ones[:, :], sq[:, k % 2, c * TH:(c + 1) * TH],
                                           start=(k == 0), stop=(k == KT - 1))
                        mm.then_inc(used, 1)

        def scale_row(v, gain, scaled, k):
            v.scalar_tensor_tensor(h_T[:, k, :], x_T[:, k, :], chan[:, k, gain:gain + 1], rstd,
                                   ALU.mult, ALU.mult).then_inc(scaled, 1)

        def matmul_block(pe, s, operand, ready=None):
            for k in range(KT):
                if ready is not None:
                    pe.wait_ge(ready, k + 1)
                for c in range(2):
                    mm = pe.matmul(ps[:, 2 * s + c, 0:TH], wring[:, s, k, :], operand[:, k, c * TH:(c + 1) * TH],
                                   start=(k == 0), stop=(k == KT - 1))
            return mm

        class Columns:

            def __init__(self, name, w_halves, operand, landed, step):
                self.w, self.x, self.landed, self.step = w_halves, operand, landed, step
                self.high_ready = [sem(f"{name}_high_ready{s}") for s in range(2)]
                self.ready = [sem(f"{name}_weights_ready{s}") for s in range(2)]
                self.projected = [sem(f"{name}_projected{s}") for s in range(2)]
                self.x_high_ready = sem(f"{name}_x_high_ready")
                self.x_ready = [sem(f"{name}_x_ready{i}") for i in range(2)]

            def high(self, act, s, n):
                act.wait_ge(self.landed[s], self.step * n + self.step)
                after(act, self.projected[s], n)
                nc.scalar.activation(self.w[:, s, 0], wring[:, s], ACT.Copy).then_inc(self.high_ready[s], 1)

            def low(self, v, s, n):
                v.wait_ge(self.high_ready[s], n + 1)
                v.tensor_tensor(self.w[:, s, 1], wring[:, s], self.w[:, s, 0].bitcast(F32), ALU.subtract).then_inc(self.ready[s], 1)

            def x_high(self, source, k):
                nc.scalar.activation(self.x[0][:, k, :], source[:, k, :], ACT.Copy).then_inc(self.x_high_ready, 1)

            def x_low(self, eng, source, k):
                eng.wait_ge(self.x_high_ready, k + 1)
                eng.tensor_tensor(self.x[1][:, k, :], source[:, k, :], self.x[0][:, k, :].bitcast(F32),
                                  ALU.subtract).then_inc(self.x_ready[k % 2], 1)

            def x_lows(self, v, source, scale=None):
                for k in range(KT + 2):
                    if scale and k < KT:
                        scale(k)
                    if k == 1:
                        self.low(v, 0, 0)
                    if k >= 3 and k % 2:
                        self.x_low(v, source, k - 2)
                self.low(v, 1, 0)

            def multiply(self, pe, s, n, first=False):
                pe.wait_ge(self.ready[s], n + 1)
                for k in range(KT):
                    if first:
                        pe.wait_ge(self.x_ready[k % 2], k // 2 + 1)
                    for w, x in ((0, 0), (0, 1), (1, 0)):
                        for c in range(2):
                            mm = pe.matmul(ps[:, 2 * s + c, 0:TH], self.w[:, s, w, k, :], self.x[x][:, k, c * TH:(c + 1) * TH],
                                           start=(k == 0 and w == 0 and x == 0), stop=(k == KT - 1 and w == 1))
                mm.then_inc(self.projected[s], 1)

        def qkv_stage():
            cols = Columns("qk", w_halves_C, qkv_operand, qk_landed, 32)
            projected = cols.projected
            kept = [sem(f"qk_kept{s}") for s in range(2)]
            v_projected, v_kept = sem("v_projected"), sem("v_kept")
            inverted, scaled = sem("mix0_inverted"), sem("mix0_scaled")
            tables, masks = sem("alibi_step"), sem("sample_mask_step")
            keys_turned, keys_kept = sem("keys_turned"), sem("keys_kept")
            dist = scratch[:, 7808:8064]
            s_dist = scratch[:, 8064:8064 + NK]

            head_of_row = np.full(P, -1)
            for r in range(P):
                g, j = r // 32, r % 32 // 4
                if j // 4 == g // 2:
                    head_of_row[r] = G4 * g + j % G4
            pick = (np.arange(H)[:, None] == head_of_row[None, :]).astype(np.float32)
            row_vals = np.stack([np.arange(P) % NQ, np.where(head_of_row >= 0, -8.0 * 2.0 ** (-8.0 * (head_of_row + 1) / H), 0.0)],
                                axis=1).astype(np.float32)
            pick_dram = nc.inline_tensor(pick, "head_pick").ap()
            row_dram = nc.inline_tensor(row_vals, "row_values").ap()

            with nc.Block() as block:
                @block.gpsimd
                def _(gp):
                    for k in range(0, KT, 2):
                        cols.x_low(gp, h_T, k)
                    c = Steps(gp, tables)
                    c.link(gp.iota(dist, [[-1, 2 * P]], base=WIN, channel_multiplier=1,
                                   allow_small_or_imprecise_dtypes=True))
                    c.link(gp.affine_select(dist, dist, [[-1, 2 * P]], ALU.is_ge, HIDE, base=WIN, channel_multiplier=1))
                    c.link(gp.affine_select(dist, dist, [[1, 2 * P]], ALU.is_gt, HIDE, base=0, channel_multiplier=-1))
                    for h in range(H):
                        c.done(gp.tensor_scalar(alibi[:, h, :], dist, -8.0 * 2.0 ** (-8.0 * (h + 1) / H), None, ALU.mult))
                    d = Steps(gp, masks)
                    d.done(gp.iota(s_dist[:, 0:WIN], [[-1, WIN]], base=WIN, channel_multiplier=0,
                                   allow_small_or_imprecise_dtypes=True))
                    d.done(gp.iota(s_dist[:, WIN:NK], [[0, NB], [-1, NQ]], base=0, channel_multiplier=0,
                                   allow_small_or_imprecise_dtypes=True))
                    d.wait()
                    gp.wait_ge(sink_landed, 64)
                    d.link(gp.tensor_scalar(s_dist, s_dist, s_row[:, 0:1], None, ALU.add))
                    hidden = s_bias[:, 0, :]
                    d.done(gp.tensor_scalar(hidden[:, 0:WIN], s_dist[:, 0:WIN], float(WIN), HIDE, ALU.is_ge, ALU.mult))
                    d.link(gp.tensor_scalar(hidden[:, WIN:NK], s_dist[:, WIN:NK], 0.0, HIDE, ALU.is_lt, ALU.mult))
                    d.link(gp.tensor_tensor(s_dist, s_dist, hidden, ALU.add))
                    d.done(gp.tensor_copy(s_bias[:, :, 0:WIN], s_dist[:, 0:WIN].unsqueeze(1).to_broadcast([P, NB, WIN])))
                    d.link(gp.tensor_copy(s_bias[:, :, WIN:NK], s_dist[:, WIN:NK].unsqueeze(1).to_broadcast([P, NB, NS])))
                    for t in range(NQ):
                        view = s_bias[:, :, WIN:NK].rearrange("p b (c t) -> p b c t", t=NQ)[:, :, :, t]
                        d.done(gp.affine_select(view, view, [[1, NB], [-1, NB]], ALU.is_equal, HIDE,
                                                base=0, channel_multiplier=0))
                    d.wait()
                    d.link(gp.tensor_scalar(s_bias, s_bias, s_row[:, 1:2], None, ALU.mult))
                    c.wait()

                @block.sync
                def _(sp):
                    sp.dma_start(sink_row, attn_sinks).then_inc(sink_landed, 16)
                    sp.dma_start(s_pick, pick_dram).then_inc(sink_landed, 16)
                    sp.dma_start(s_sink_col, attn_sinks.rearrange("l h -> h l")).then_inc(sink_landed, 16)
                    sp.dma_start(s_row, row_dram).then_inc(sink_landed, 16)
                    sp.dma_start(s_key_rows, cache_k[0].rearrange("b s g d -> s b (g d)")).then_inc(cache_landed, 16)
                    for j in range(2, 8):
                        sp.wait_ge(cols.ready[j % 2], j // 2)
                        load_queries(sp, j)
                    for m in range(2):
                        sp.wait_ge(cols.ready[m], 4)
                        sp.dma_start(wring[:, m], columns(w_qkv[0], 1024 + m * P)).then_inc(qk_landed[m], 32)
                    sp.dma_start(s_val_rows, cache_v[0].rearrange("b s g d -> s b (g d)")).then_inc(vcache_landed, 16)

                @block.tensor
                def _(pe):
                    for s in range(2):
                        cols.multiply(pe, s, 0, first=s == 0)
                    pe.wait_ge(v_landed, 16)
                    for t in range(NT):
                        r, b = rows_of(t), 4 + t % 4
                        if t >= 4:
                            pe.wait_ge(v_kept, t - 3)
                        for k in range(KT):
                            mm = pe.matmul(ps[0:r, b, 0:256], h_T[:, k, t * P:t * P + r], w_v[:, k, :],
                                           start=(k == 0), stop=(k == KT - 1))
                        mm.then_inc(v_projected, 1)
                    pe.wait_ge(cache_landed, 16)
                    pe.wait_ge(v_kept, NT)
                    for b in range(NB):
                        for m in range(2):
                            n = 2 * b + m
                            mm = pe.transpose(ps[:, 4 + n // 4, (n % 4) * P:(n % 4 + 1) * P],
                                              s_key_rows[:, b, m * P:(m + 1) * P], ident[:, :])
                    mm.then_inc(keys_turned, 1)
                    with pe.Fori(1, 5) as n:
                        for s in range(2):
                            pe.wait_ge(kept[s], n)
                            cols.multiply(pe, s, n)

                @block.scalar
                def _(act):
                    def keep(n):
                        act.wait_ge(projected[0], n + 1)
                        nc.scalar.activation(half(q_T[:, ds(2 * n, 1), :].rearrange("p k t -> p (k t)")),
                                             ps[:, 0:2, 0:TH], ACT.Copy).then_inc(kept[0], 1)
                        for s in range(2):
                            cols.high(act, s, n + 1)

                    cols.high(act, 0, 0)
                    for k in range(KT):
                        act.wait_ge(scaled, k + 1)
                        cols.x_high(h_T, k)
                    cols.high(act, 1, 0)
                    keep(0)
                    act.wait_ge(keys_turned, 1)
                    nc.scalar.activation(s_keys_T.rearrange("p b m s -> p (b m s)"),
                                         ps[:, 4:8, :].rearrange("p c n -> p (c n)"), ACT.Copy).then_inc(keys_kept, 1)
                    with act.Fori(1, 4) as n:
                        keep(n)
                    act.wait_ge(projected[0], 5)
                    nc.scalar.activation(half(k_T[:, 0, :]), ps[:, 0:2, 0:TH], ACT.Copy).then_inc(kept[0], 1)
                    act.wait_ge(keys_kept, 1)

                @block.vector
                def _(v):
                    v.reciprocal(rstd, std).then_inc(inverted, 1)
                    v.wait_ge(inverted, 1)
                    cols.x_lows(v, h_T, lambda k: scale_row(v, V_MIX, scaled, k))

                    def keep(n):
                        cols.low(v, 0, n + 1)
                        v.wait_ge(projected[1], n + 1)
                        v.tensor_copy(half(q_T[:, ds(2 * n + 1, 1), :].rearrange("p k t -> p (k t)")),
                                      ps[:, 2:4, 0:TH]).then_inc(kept[1], 1)
                        cols.low(v, 1, n + 1)

                    keep(0)
                    for t in range(NT):
                        r, b = rows_of(t), 4 + t % 4
                        v.wait_ge(v_projected, t + 1)
                        v.tensor_copy(v_rows[0:r, t, :], ps[0:r, b, 0:256]).then_inc(v_kept, 1)
                    with v.Fori(1, 4) as n:
                        keep(n)
                    v.wait_ge(projected[1], 5)
                    v.tensor_copy(half(k_T[:, 1, :]), ps[:, 2:4, 0:TH]).then_inc(kept[1], 1)

        def prompt_attention_stage():
            q_blk = h_flat[:, 0:1024].rearrange("p (k t) -> p k t", k=KT)
            k_blk = h_flat[:, 1024:1536].rearrange("p (m s) -> p m s", m=2)
            p_T = h_flat[:, 1536:3584].rearrange("p (b j c q) -> p b j c q", b=2, j=G4, c=2)
            o_blk = areaB[:, 4352:5376]
            probs = areaS[:, 0:2048].rearrange("p (b h s) -> p b h s", b=2, h=G4)
            top, nbias, total, gap, inv = (areaB[:, 4112 + 16 * i:4128 + 16 * i] for i in range(5))
            slots_filled = sem("slots_filled")
            scored, topped, exped = sem("scored"), sem("topped"), sem("exped")
            probs_turned, probs_kept = sem("probs_turned"), sem("probs_kept")
            mixed, sunk, normed = sem("mixed"), sem("sunk"), sem("normed")
            o_turned, o_kept = sem("o_turned"), sem("o_kept")
            scores_seen = sem("scores_seen")
            top_step, norm_step = sem("top_step"), sem("norm_step")
            sunk_exped, total_taken = sem("sunk_exped"), sem("total_taken")
            sink_spread, sink_ready = sem("sink_spread"), sem("sink_ready")
            scores = lambda b: ps[:, 2 * b:2 * b + 2, :].rearrange("p c (h s) -> p (c h) s", s=256)
            turned = ps[:, 4:6, :].rearrange("p c (h s) -> p (c h) s", s=P)
            mix = ps[:, 6:8, :].rearrange("p c n -> p (c n)")

            NBLK = NP // P
            keys_of = lambda n: (slice(P, 2 * P), (1,)) if isinstance(n, int) and n == 0 else (slice(0, 2 * P), (0, 1))

            def blocks(eng, attend):
                attend(0, True, False)
                with eng.Fori(1, NBLK - 1) as n:
                    attend(n, False, False)
                attend(NBLK - 1, False, True)

            with nc.Block() as block:
                @block.gpsimd
                def _(gp):
                    gp.tensor_copy(s_q_new, q_T[:, :, NP:T].rearrange("p k (b t) -> p b k t", b=NB)).then_inc(s_q_ready, 1)

                    def fill(n, first):
                        for m in range(2):
                            if not first:
                                gp.wait_ge(scored, 4 * n + 2 * m - 2)
                            gp.tensor_copy(q_blk[:, 4 * m:4 * m + 4, :],
                                           q_T[:, 4 * m:4 * m + 4, ds(n * P, P)]).then_inc(slots_filled, 1)
                            gp.tensor_copy(k_blk[:, m, :], k_T[:, m, ds(n * P - P, 2 * P)]).then_inc(slots_filled, 1)

                    fill(1, True)
                    with gp.Fori(2, NBLK) as n:
                        fill(n, False)
                    gp.wait_ge(s_q_ready, 1)

                @block.tensor
                def _(pe):
                    pe.wait_ge(sink_landed, 16 * 4)
                    pe.matmul(mix[:, 0:H], ones[0:1, :], sink_row, start=True, stop=True)
                    pe.matmul(mix[:, H:H + 1], s_pick, s_sink_col, start=True, stop=True).then_inc(sink_spread, 1)

                    def score(n, g):
                        keys, _ = keys_of(n)
                        fixed = isinstance(n, int) and n in (0, NBLK - 1)
                        if fixed:
                            q, keys_at = q_T[:, :, n * P:(n + 1) * P], k_T[:, :, max(n * P - P, 0):(n + 1) * P]
                        else:
                            q, keys_at = q_blk, k_blk
                            if g % 2 == 0:
                                pe.wait_ge(slots_filled, 4 * (n - 1) + 2 * (g // 2) + 2)
                        after(pe, topped, 4 * n + g - 1)
                        lo = DH * (g % 2)
                        for j in range(G4):
                            mm = pe.matmul(scores(g % 2)[:, j, keys], q[lo:lo + DH, 4 * (g // 2) + j, :],
                                           keys_at[lo:lo + DH, g // 2, :], start=True, stop=True)
                        mm.then_inc(scored, 1)

                    def turn(n, g):
                        keys, halves = keys_of(n)
                        pe.wait_ge(exped, 4 * n + g + 1)
                        after(pe, probs_kept, 2 * (4 * n + g))
                        if g == 1:
                            after(pe, o_kept, n)
                        for j in range(G4):
                            for c in halves:
                                mm = pe.transpose(turned[:, 2 * j + c, :], probs[:, g % 2, j, c * P:(c + 1) * P], ident[:, :])
                        mm.then_inc(probs_turned, 1)

                    def mixing(n, g):
                        keys, halves = keys_of(n)
                        pe.wait_ge(probs_kept, 2 * (4 * n + g) + 2)
                        if g == 0:
                            pe.wait_ge(sink_ready, 1)
                            after(pe, normed, n)
                        for j in range(G4):
                            h = G4 * g + j
                            for c in halves:
                                rows = v_rows[:, ds(n - 1 + c, 1), g * DH:(g + 1) * DH].rearrange("p t d -> p (t d)")
                                mm = pe.matmul(mix[:, h * DH:(h + 1) * DH], p_T[:, g % 2, j, c, :], rows,
                                               start=(c == halves[0]), stop=(c == 1))
                        mm.then_inc(mixed, 1)

                    def turn_out(n):
                        pe.wait_ge(normed, n + 1)
                        pe.wait_ge(probs_kept, 2 * min(4 * n + 5, 4 * NBLK) if isinstance(n, int) else 2 * (4 * n + 5))
                        for k in range(KT):
                            mm = pe.transpose(turned[:, k, :], o_blk[:, k * P:(k + 1) * P], ident[:, :])
                        mm.then_inc(o_turned, 1)

                    def attend(n, first, last):
                        if first:
                            score(0, 0)
                            score(0, 1)
                            turn(0, 0)
                        score(n, 2)
                        mixing(n, 0)
                        if not first:
                            turn_out(n - 1)
                        score(n, 3)
                        turn(n, 1)
                        mixing(n, 1)
                        turn(n, 2)
                        if not last:
                            score(n + 1, 0)
                        mixing(n, 2)
                        turn(n, 3)
                        if not last:
                            score(n + 1, 1)
                        mixing(n, 3)
                        if not last:
                            turn(n + 1, 0)
                        else:
                            turn_out(n)

                    blocks(pe, attend)

                @block.scalar
                def _(act):
                    def exps(n, g):
                        keys, _ = keys_of(n)
                        act.wait_ge(topped, 4 * n + g + 1)
                        if g == 0:
                            after(act, total_taken, n)
                        for j in range(G4):
                            h = G4 * g + j
                            e = nc.scalar.activation(probs[:, g % 2, j, keys], probs[:, g % 2, j, keys], ACT.Exp,
                                                     bias=nbias[:, h:h + 1], scale=0.125,
                                                     accum_out=total[:, h:h + 1])
                        e.then_inc(exped, 1)

                    def keep(n, g):
                        _, halves = keys_of(n)
                        act.wait_ge(probs_turned, 4 * n + g + 1)
                        after(act, mixed, 4 * n + g - 1)
                        of = turned[:, 0:4, :].rearrange("p (j c) q -> p j c q", c=2)
                        nc.scalar.activation(p_T[:, g % 2, 0:2, halves[0]:2, :], of[:, :, halves[0]:2, :],
                                             ACT.Copy).then_inc(probs_kept, 1)

                    def attend(n, first, last):
                        if first:
                            exps(0, 0)
                        for g in range(HKV - 1):
                            exps(n, g + 1)
                            if g == HKV - 2:
                                act.wait_ge(sunk, n + 1)
                                nc.scalar.activation(gap, gap, ACT.Exp, scale=0.125).then_inc(sunk_exped, 1)
                            keep(n, g)
                        if not last:
                            exps(n + 1, 0)
                        keep(n, HKV - 1)

                    blocks(act, attend)

                @block.vector
                def _(v):
                    v.wait_ge(sink_spread, 1)
                    v.tensor_scalar(sink8, mix[:, 0:H], 8.0, None, ALU.mult).then_inc(sink_ready, 1)
                    v.tensor_scalar(s_sink8, mix[:, H:H + 1], 8.0, None, ALU.mult).then_inc(sink_ready, 1)
                    v.wait_ge(sink_ready, 2)

                    def tops(n, g):
                        keys, _ = keys_of(n)
                        v.wait_ge(scored, 4 * n + g + 1)
                        after(v, probs_turned, 4 * n + g - 1)
                        settle(v, scores_seen)
                        for j in range(G4):
                            h = G4 * g + j
                            t = v.tensor_tensor_reduce(out=probs[:, g % 2, j, keys], in0=scores(g % 2)[:, j, keys],
                                                       in1=alibi[:, h, keys], scale=1.0, scalar=sink8[:, h:h + 1],
                                                       op0=ALU.add, op1=ALU.max, accum_out=top[:, h:h + 1])
                        t.then_inc(top_step, 1)
                        v.wait_ge(top_step, 4 * n + g + 1)
                        hs = slice(G4 * g, G4 * g + G4)
                        v.tensor_scalar(nbias[:, hs], top[:, hs], -0.125, None, ALU.mult).then_inc(topped, 1)

                    def keep(n, g):
                        _, halves = keys_of(n)
                        v.wait_ge(probs_turned, 4 * n + g + 1)
                        after(v, mixed, 4 * n + g - 1)
                        of = turned[:, 4:8, :].rearrange("p (j c) q -> p j c q", c=2)
                        v.tensor_copy(p_T[:, g % 2, 2:4, halves[0]:2, :], of[:, :, halves[0]:2, :]).then_inc(probs_kept, 1)

                    def keep_out(n):
                        v.wait_ge(o_turned, n + 1)
                        v.tensor_copy(o_T[:, :, ds(n * P, P)], turned).then_inc(o_kept, 1)

                    def attend(n, first, last):
                        if first:
                            tops(0, 0)
                            tops(0, 1)
                        keep(n, 0)
                        tops(n, 2)
                        if not first:
                            keep_out(n - 1)
                        keep(n, 1)
                        tops(n, 3)
                        v.tensor_tensor(gap, sink8, top, ALU.subtract).then_inc(sunk, 1)
                        keep(n, 2)
                        v.wait_ge(exped, 4 * n + 4)
                        v.wait_ge(sunk_exped, n + 1)
                        v.tensor_tensor(total, total, gap, ALU.add).then_inc(total_taken, 1)
                        v.wait_ge(total_taken, n + 1)
                        v.reciprocal(inv, total).then_inc(norm_step, 1)
                        if not last:
                            tops(n + 1, 0)
                        keep(n, 3)
                        if not last:
                            tops(n + 1, 1)
                        v.wait_ge(norm_step, n + 1)
                        v.wait_ge(mixed, 4 * n + 4)
                        v.tensor_tensor(o_blk.rearrange("p (h d) -> p h d", h=H), mix.rearrange("p (h d) -> p h d", h=H),
                                        inv.unsqueeze(2).to_broadcast([P, H, DH]),
                                        ALU.mult).then_inc(normed, 1)
                        if last:
                            keep_out(n)

                    blocks(v, attend)

        def sample_attention_stage():
            probs = h_flat[:, NB * NK:2 * NB * NK].rearrange("p (b s) -> p b s", b=NB)
            p_T = h_flat[:, 2560:3584].rearrange("p (b r) -> p b r", b=NB)
            pn_T = areaS[0:NS, 0:1024].rearrange("p (b r) -> p b r", b=NB)
            o_twice = areaS[:, 1024:2048].rearrange("p (b a d) -> p b a d", b=NB, a=2)
            top, total, gap, inv, nbias = (small[:, 40 + 8 * i:48 + 8 * i] for i in range(5))
            k_out = areaS[:, 2048:2304]
            ks_out = areaS[0:NS, 2304:2560]

            step, scored = sem("sample_step"), sem("sample_scored")
            shifted, exped = sem("sample_shifted"), sem("sample_exped")
            turned, kept, mixed = sem("sample_turned"), sem("sample_kept"), sem("sample_mixed")
            o_ready, o_turned = sem("sample_o_ready"), sem("sample_o_turned")
            k_turned, k_kept, o_kept = sem("k_out_turned"), sem("k_out_kept"), sem("sample_o_kept")
            score_tile = lambda g: ps[32 * g:32 * g + 32, 4 * (g % 2):4 * (g % 2) + 4, :]\
                .rearrange("p c (b s) -> p (c b) s", s=256)[:, :, 0:NK]

            with nc.Block() as block:
                @block.sync
                def _(sp):
                    for new, old in ((k_sample, cache_k), (v_sample, cache_v)):
                        sp.dma_start(new[0, :, 0:WIN - NQ].rearrange("b s g d -> b s (g d)"),
                                     old[0, :, NQ:WIN].rearrange("b s g d -> b s (g d)")).then_inc(kv_stored, 16)
                    sp.dma_start(v_prompt[0, 0].rearrange("s g d -> s (g d)"), v_rows[:, 3, :]).then_inc(kv_stored, 16)
                    for b in range(NB):
                        sp.dma_start(v_sample[0, b, WIN - NQ:WIN].rearrange("s g d -> s (g d)"),
                                     v_rows[NQ * b:NQ * b + NQ, 4, :]).then_inc(kv_stored, 16)
                    first_columns(sp, "w_o", w_o[0], (0, P))
                    sp.wait_ge(k_kept, 2)
                    sp.dma_start(k_prompt[0, 0].rearrange("s g d -> s (g d)"), k_out).then_inc(kv_stored, 16)
                    for b in range(NB):
                        sp.dma_start(k_sample[0, b, WIN - NQ:WIN].rearrange("s g d -> s (g d)"),
                                     ks_out[NQ * b:NQ * b + NQ, :]).then_inc(kv_stored, 16)

                @block.tensor
                def _(pe):
                    for g in range(HKV):
                        lo, m = DH * (g % 2), g // 2
                        for b in range(NB):
                            q = s_q_new[lo:lo + DH, b].rearrange("p k t -> p (k t)")
                            out = score_tile(g)[:, b, :]
                            pe.matmul(out[:, 0:WIN], q, s_keys_T[lo:lo + DH, b, m, :], start=True, stop=True)
                            mm = pe.matmul(out[:, WIN:NK], q, k_T[lo:lo + DH, m, NP:T], start=True, stop=True)
                        mm.then_inc(scored, 1)
                    for b in range(NB):
                        pe.wait_ge(exped, b + 1)
                        pe.transpose(ps[:, b // 4, (b % 4) * P:(b % 4 + 1) * P], probs[:, b, 0:WIN], ident[:, :])
                        mm = pe.transpose(ps[0:NS, 2 + b // 4, (b % 4) * P:(b % 4 + 1) * P], probs[:, b, WIN:NK], ident[:, :])
                    mm.then_inc(turned, 1)
                    for m in range(2):
                        pe.transpose(ps[:, 5, m * P:(m + 1) * P], k_T[:, m, NP - P:NP], ident[:, :])
                        mm = pe.transpose(ps[0:NS, 5, 256 + m * P:256 + (m + 1) * P], k_T[:, m, NP:T], ident[:, :])
                    mm.then_inc(k_turned, 1)
                    pe.wait_ge(kept, 2)
                    pe.wait_ge(vcache_landed, 16)
                    for b in range(NB):
                        for g in range(HKV):
                            out = ps[32 * g:32 * g + 32, 4, b * DH:(b + 1) * DH]
                            pe.matmul(out, p_T[:, b, 32 * g:32 * g + 32], s_val_rows[:, b, g * DH:(g + 1) * DH],
                                      start=True, stop=False)
                            mm = pe.matmul(out, pn_T[:, b, 32 * g:32 * g + 32], v_rows[0:NS, 4, g * DH:(g + 1) * DH],
                                           start=False, stop=True)
                    mm.then_inc(mixed, 1)
                    pe.wait_ge(o_ready, 2)
                    for b in range(NB):
                        mm = pe.transpose(ps[:, 6 + b // 4, (b % 4) * P:(b % 4 + 1) * P],
                                          o_twice[:, b].rearrange("p a d -> p (a d)"), ident[:, :])
                    mm.then_inc(o_turned, 1)

                @block.scalar
                def _(act):
                    act.wait_ge(shifted, 2)
                    for b in range(NB):
                        nc.scalar.activation(probs[:, b, :], probs[:, b, :], ACT.Exp, scale=0.125, bias=nbias[:, b:b + 1],
                                             accum_out=total[:, b:b + 1]).then_inc(exped, 1)
                    nc.scalar.activation(gap, gap, ACT.Exp, scale=0.125).then_inc(exped, 1)
                    act.wait_ge(turned, 1)
                    nc.scalar.activation(p_T.rearrange("p b r -> p (b r)"), ps[:, 0:2, :].rearrange("p c n -> p (c n)"),
                                         ACT.Copy).then_inc(kept, 1)

                @block.vector
                def _(v):
                    s = Steps(v, step)
                    for g in range(HKV):
                        v.wait_ge(scored, g + 1)
                        q = slice(32 * g, 32 * g + 32)
                        s.done(v.tensor_tensor(probs[q], score_tile(g), s_bias[q], ALU.add))
                    s.wait()
                    s.link(v.tensor_reduce(top, probs, AX_X, ALU.max))
                    s.link(v.tensor_scalar(top, top, s_sink8, None, ALU.max))
                    v.tensor_scalar(nbias, top, -0.125, None, ALU.mult).then_inc(shifted, 1)
                    v.tensor_scalar(gap, top, -1.0, s_sink8, ALU.mult, ALU.add).then_inc(shifted, 1)
                    v.wait_ge(exped, NB + 1)
                    s.link(v.tensor_tensor(total, total, gap, ALU.add))
                    s.link(v.reciprocal(inv, total))
                    v.wait_ge(turned, 1)
                    v.tensor_copy(pn_T.rearrange("p b r -> p (b r)"), ps[0:NS, 2:4, :].rearrange("p c n -> p (c n)")).then_inc(kept, 1)
                    v.wait_ge(k_turned, 1)
                    v.tensor_copy(k_out, ps[:, 5, 0:256]).then_inc(k_kept, 1)
                    v.tensor_copy(ks_out, ps[0:NS, 5, 256:512]).then_inc(k_kept, 1)
                    v.wait_ge(mixed, 1)
                    for a in range(2):
                        v.tensor_tensor(o_twice[:, :, a, :], ps[:, 4, :].rearrange("p (b d) -> p b d", d=DH),
                                        inv.unsqueeze(2).to_broadcast([P, NB, DH]), ALU.mult).then_inc(o_ready, 1)
                    v.wait_ge(o_turned, 1)
                    spread = ps[:, 6:8, :].rearrange("p c (b r) -> p (c b) r", r=P)
                    for g in range(HKV):
                        rows = spread[:, :, 32 * g + 16 * (g // 2):32 * g + 16 * (g // 2) + 16]
                        for a in range(2):
                            src = rows[DH * a:DH * a + DH].rearrange("p b (i a t) -> p i a b t", i=2, a=2)[:, :, a]
                            dst = o_T[DH * a:DH * a + DH, 2 * g:2 * g + 2, NP:T].rearrange("p i (b t) -> p i b t", t=NQ)
                            v.tensor_copy(dst, src).then_inc(o_kept, 1)
                    v.wait_ge(o_kept, 8)

        ln_std = areaS[:, 2048 + 2 * T:2048 + 3 * T]

        def project_back_stage(name, w, w_halves, operand, norm, offset, l, rows_stored, stores):
            sq = areaB[:, 0:2 * T].rearrange("p (b t) -> p b t", b=2)
            gateup_landed[l] = [sem(f"gateup_landed{l}{s}") for s in range(RING)]
            down_landed[l] = [sem(f"down_landed{l}{s}") for s in range(RING)]
            cols = Columns(name, w_halves, back_operand, columns_landed[name], 16)
            added = [sem(f"{name}_added{s}") for s in range(2)]
            squared, summed = sem(f"{name}_squared"), sem(f"{name}_summed")
            inverted, scaled, out = sem(f"{name}_inverted"), sem(f"{name}_scaled"), sem(f"{name}_operand_ready")
            route_landed[l], route_scaled[l] = sem(f"route_weights_landed{l}"), sem(f"route_weights_scaled{l}")
            with nc.Block() as block:
                @block.sync
                def _(sp):
                    sp.dma_start(w_route[:, :, 0:NG], w_group_router[l].rearrange("(k p) g -> p k g", p=P)).then_inc(route_landed[l], 16)
                    sp.dma_start(w_route[:, :, NG:NR], w_expert_router[l].rearrange("(k p) g -> p k g", p=P)).then_inc(route_landed[l], 16)
                    sp.dma_start(b_rows[:, 0:NG], b_group_router[l:l + 1, :].to_broadcast([P, NG])).then_inc(route_landed[l], 16)
                    sp.dma_start(b_rows[:, NG:NR], b_expert_router[l:l + 1, :].to_broadcast([P, NE])).then_inc(route_landed[l], 16)
                    with sp.Fori(1, 4) as n:
                        for s in range(2):
                            sp.wait_ge(cols.ready[s], n)
                            sp.dma_start(wring[:, s], columns(w, (2 * n + s) * P)).then_inc(cols.landed[s], 16)
                    for s in range(RING):
                        load_gateup(sp, l, s, s)
                        load_down(sp, l, s, s)
                    sp.wait_ge(rows_stored, 16 * stores)

                @block.gpsimd
                def _(gp):
                    for k in range(0, KT, 2):
                        cols.x_low(gp, operand, k)

                @block.tensor
                def _(pe):
                    def sums(k, s, first, last):
                        pe.wait_ge(squared, k + 1)
                        for c in range(2):
                            mm = pe.matmul(ps[:, 4 + c, 0:TH], ones[:, :], sq[:, s, c * TH:(c + 1) * TH],
                                           start=first, stop=last)
                        mm.then_inc(summed, 1)

                    for s in range(2):
                        cols.multiply(pe, s, 0, first=s == 0)

                    def turn(n):
                        for s in range(2):
                            pe.wait_ge(added[s], n)
                            cols.multiply(pe, s, n)
                            sums(2 * n + s - 2, s, isinstance(n, int) and n == 1 and s == 0, False)

                    turn(1)
                    with pe.Fori(2, 4) as n:
                        turn(n)
                    for s in range(2):
                        sums(KT - 2 + s, s, False, s == 1)

                @block.vector
                def _(v):
                    if norm:
                        v.reciprocal(ln_std, ln_std).then_inc(inverted, 1)
                    if norm:
                        v.wait_ge(inverted, 1)

                    def scale(k):
                        v.tensor_tensor(operand[:, k, :], operand[:, k, :], ln_std, ALU.mult).then_inc(scaled, 1)

                    cols.x_lows(v, operand, scale if norm else None)

                    def add(n, last):
                        for s in range(2):
                            v.wait_ge(cols.projected[s], n + 1)
                            xs = half(x_T[:, ds(2 * n + s, 1), :].rearrange("p k t -> p (k t)"))
                            off = 0.0 if offset is None else \
                                chan[:, ds(2 * n + s, 1), offset:offset + 1].rearrange("p k n -> p (k n)")
                            v.scalar_tensor_tensor(xs, ps[:, 2 * s:2 * s + 2, 0:TH], off, xs,
                                                   ALU.add, ALU.add).then_inc(added[s], 1)
                            if not last:
                                cols.low(v, s, n + 1)

                    with v.Fori(0, 3) as n:
                        add(n, False)
                    v.wait_ge(route_landed[l], 64)
                    v.tensor_tensor(w_route[:, :, :], w_route[:, :, :], chan[:, :, V_FFN + l:V_FFN + l + 1].to_broadcast([P, KT, NR]),
                                    ALU.mult).then_inc(route_scaled[l], 1)
                    add(3, True)

                @block.scalar
                def _(act):
                    cols.high(act, 0, 0)
                    for k in range(KT):
                        if norm:
                            act.wait_ge(scaled, k + 1)
                            nc.scalar.activation(operand[:, k, :], operand[:, k, :], ACT.Silu,
                                                 scale=chan[:, k, V_LNG:V_LNG + 1], bias=chan[:, k, V_LNB:V_LNB + 1]).then_inc(out, 1)
                            act.wait_ge(out, k + 1)
                        cols.x_high(operand, k)
                    cols.high(act, 1, 0)

                    def square(n, first, last):
                        for s in range(2):
                            if not last:
                                cols.high(act, s, n + 1)
                            act.wait_ge(added[s], n + 1)
                            if not first:
                                act.wait_ge(summed, 2 * n + s - 1)
                            nc.scalar.activation(sq[:, s, :], x_T[:, ds(2 * n + s, 1), :].rearrange("p k t -> p (k t)"),
                                                 ACT.Square).then_inc(squared, 1)

                    square(0, True, False)
                    with act.Fori(1, 3) as n:
                        square(n, False, False)
                    square(3, False, True)

        def conv_stage():
            u_T = areaB[:, :].rearrange("p (k n) -> p k n", k=KT)
            u_seg = u_T[:, :, HIST + NP:UW].rearrange("p k (b n) -> p k b n", b=NB)
            sig = areaS[:, 2048:2048 + T]
            prod = areaS[:, 2592:2592 + NS * CW].rearrange("p (r w) -> p r w", w=CW)
            diag = areaS[:, 3584:3584 + 2 * PE_TAPS * P].rearrange("p (b w c) -> p b w c", b=2, w=PE_TAPS)
            end_diag = areaC[:, 3072:3072 + END_TAPS * P].rearrange("p (w c) -> p w c", w=END_TAPS)
            end_diag_ready = sem("end_diag_ready")
            w = w_pw1[0]
            inverted, scaled = sem("mix1_inverted"), sem("mix1_scaled")
            state_turned, hist_ready = sem("state_turned"), sem("hist_ready")
            landed = columns_landed["pw1"]
            val_done, gate_done = sem("pw1_value_done"), sem("pw1_gate_done")
            sig_done, u_done, diag_ready = sem("sigmoid_done"), sem("u_done"), sem("diag_ready")
            taps_done, conv_done = sem("pe_taps_done"), sem("conv_done")
            product_ready, product_added = sem("product_ready"), sem("product_added")
            hist_copied, u_part = sem("hist_copied"), sem("u_part")
            tap_step, seg_step = sem("tap_step"), sem("seg_step")
            stored = sem("conv_stored")
            products = areaC[:, 0:2048].rearrange("p (b n) -> p b n", b=4)
            product_sum = areaC[:, 2048:3072].rearrange("p (b n) -> p b n", b=2)
            VEC_FIRST = PE_TAPS + ACT_TAPS
            VEC_STEPS = CW - VEC_FIRST + 1
            acc = lambda b: ps[:, 4 + b, :]
            acc2 = lambda b: ps[:, 6 + b, :]
            col = lambda k, n: chan[:, ds(k, 1), n:n + 1].rearrange("p k n -> p (k n)")
            shifted = lambda k, j: u_T[:, ds(k, 1), j:j + NP].rearrange("p k n -> p (k n)")

            with nc.Block() as block:
                @block.sync
                def _(sp):
                    sp.dma_start(conv_sample[0, :, 0:HIST - NQ], state_conv[0, :, NQ:HIST]).then_inc(stored, 16)
                    with sp.Fori(1, KT) as k:
                        sp.wait_ge(val_done, k)
                        sp.dma_start(wring[:, 0], columns(w, k * P)).then_inc(landed[0], 16)
                        sp.wait_ge(gate_done, k)
                        sp.dma_start(wring[:, 1], columns(w, k * P + D)).then_inc(landed[1], 16)
                    sp.wait_ge(stored, 16)

                @block.tensor
                def _(pe):
                    pe.wait_ge(state_landed, 16)
                    for i in range(2):
                        for k in range(KT):
                            mm = pe.transpose(ps[:, 4 + 2 * i + k // 4, (k % 4) * P:(k % 4) * P + 4 * HIST],
                                              state_rows[:, i, k * P:(k + 1) * P], ident[0:4 * HIST, 0:4 * HIST])
                    mm.then_inc(state_turned, 1)

                    def value(k, ready=None):
                        pe.wait_ge(landed[0], 16 * k + 16)
                        after(pe, u_done, 2 * k)
                        matmul_block(pe, 0, h_T, ready).then_inc(val_done, 1)

                    def gate(k):
                        pe.wait_ge(landed[1], 16 * k + 16)
                        after(pe, sig_done, k)
                        matmul_block(pe, 1, h_T).then_inc(gate_done, 1)

                    def taps(k, b, early, final=False):
                        pe.wait_ge(diag_ready, k + 1)
                        pe.wait_ge(u_done, 2 * k + 2)
                        if not early:
                            pe.wait_ge(conv_done, k - 1)
                        for j in range(PE_TAPS):
                            mm = pe.matmul(acc(b), diag[:, b, j, :],
                                           u_T[:, ds(k, 1), j:j + NP].rearrange("p k n -> p (k n)"),
                                           start=(j == 0), stop=(j == PE_TAPS - 1 and not final))
                        if final:
                            pe.wait_ge(end_diag_ready, END_TAPS)
                            for j in range(END_TAPS):
                                at = CW - END_TAPS + j
                                mm = pe.matmul(acc(b), end_diag[:, j, :], u_T[:, k, at:at + NP],
                                               start=False, stop=(j == END_TAPS - 1))
                        mm.then_inc(taps_done, 1)

                    value(0, scaled)
                    gate(0)
                    for k in (1, 2):
                        value(k)
                        gate(k)
                        if k == 1:
                            pe.wait_ge(hist_ready, 1)
                        taps(k - 1, (k - 1) % 2, True)
                    with pe.Fori(1, 3) as i:
                        for j in (1, 2):
                            k = 2 * i + j
                            value(k)
                            gate(k)
                            taps(k - 1, (j - 1) % 2, False)
                    value(7)
                    gate(7)
                    taps(6, 0, False)
                    taps(7, 1, False, True)
                    pe.wait_ge(u_done, 2 * KT)
                    for k in range(KT):
                        pe.wait_ge(conv_done, k + 1)
                        pe.wait_ge(seg_step, 7 * (k + 1))
                        for c in range(2):
                            pe.matmul(ps[:, c, 0:TH], ones[:, :], c_T[:, k, c * TH:(c + 1) * TH],
                                      start=(k == 0), stop=(k == KT - 1))

                @block.scalar
                def _(act):
                    def diags(k, b):
                        for j in range(PE_TAPS):
                            d = nc.scalar.activation(diag[:, b, j, :], ident[:, :], ACT.Copy,
                                                     scale=chan[:, ds(k, 1), V_DW + j:V_DW + j + 1].rearrange("p k n -> p (k n)"))
                        d.then_inc(diag_ready, 1)

                    def sigmoid(k):
                        act.wait_ge(gate_done, k + 1)
                        after(act, u_done, 2 * k)
                        nc.scalar.activation(half(sig), ps[:, 2:4, 0:TH], ACT.Sigmoid,
                                             bias=chan[:, ds(k, 1), V_BG:V_BG + 1].rearrange("p k n -> p (k n)")).then_inc(sig_done, 1)

                    def multiply(k, first):
                        act.wait_ge(u_done, 2 * k + 2)
                        for m in range(ACT_TAPS):
                            if m >= 4:
                                act.wait_ge(product_added, (ACT_TAPS - 1) * k + max(m - 4, 1))
                            elif not first:
                                act.wait_ge(product_added, (ACT_TAPS - 1) * (k - 1) + m + 4)
                            nc.scalar.activation(products[:, m % 4, :], shifted(k, PE_TAPS + m), ACT.Copy,
                                                 scale=col(k, V_DW + PE_TAPS + m)).then_inc(product_ready, 1)

                    diags(0, 0)
                    sigmoid(0)
                    diags(1, 1)
                    multiply(0, True)
                    sigmoid(1)
                    with act.Fori(1, 4) as i:
                        for j in range(2):
                            k = 2 * i + j
                            act.wait_ge(taps_done, k - 1)
                            diags(k, j)
                            multiply(k - 1, False)
                            sigmoid(k)
                    for j in range(END_TAPS):
                        at = V_DW + CW - END_TAPS + j
                        nc.scalar.activation(end_diag[:, j, :], ident[:, :], ACT.Copy, scale=chan[:, 7, at:at + 1]).then_inc(end_diag_ready, 1)
                    multiply(7, False)

                @block.vector
                def _(v):
                    v.reciprocal(rstd, std).then_inc(inverted, 1)
                    v.wait_ge(inverted, 1)
                    for k in range(KT):
                        scale_row(v, V_MIX + 1, scaled, k)
                    v.wait_ge(state_turned, 1)
                    for i in range(2):
                        for c in range(2):
                            v.tensor_copy(u_seg[:, 4 * c:4 * c + 4, 4 * i:4 * i + 4, 0:HIST],
                                          ps[:, 4 + 2 * i + c, :].rearrange("p (k t) -> p k t", k=4)[:, :, 0:4 * HIST]
                                          .rearrange("p k (b r) -> p k b r", b=4)).then_inc(hist_copied, 1)
                    v.wait_ge(hist_copied, 4)
                    v.memset(u_T[:, :, 0:HIST], 0.0).then_inc(hist_ready, 1)

                    def glu(k):
                        v.wait_ge(sig_done, k + 1)
                        ba = chan[:, ds(k, 1), V_BA:V_BA + 1].rearrange("p k n -> p (k n)")
                        uk = u_T[:, ds(k, 1), HIST:HIST + NP].rearrange("p k n -> p (k n)")
                        v.scalar_tensor_tensor(uk[:, 0:TH], ps[:, 0, 0:TH], ba, sig[:, 0:TH],
                                               ALU.add, ALU.mult).then_inc(u_part, 1)
                        v.scalar_tensor_tensor(u_seg[:, ds(k, 1), :, HIST:SEG].rearrange("p k b t -> p (k b) t"),
                                               ps[:, 1, NP - TH:TH].rearrange("p (b t) -> p b t", t=NQ), ba,
                                               sig[:, NP:T].rearrange("p (b t) -> p b t", t=NQ),
                                               ALU.add, ALU.mult).then_inc(u_done, 1)
                        v.wait_ge(u_part, k + 1)
                        v.scalar_tensor_tensor(uk[:, TH:NP], ps[:, 1, 0:NP - TH], ba, sig[:, TH:NP],
                                               ALU.add, ALU.mult).then_inc(u_done, 1)

                    def taps(k, b, js, steps, own):
                        for j in js:
                            if j == VEC_FIRST:
                                o = v.tensor_scalar(acc2(b), shifted(k, j), col(k, V_DW + j), None, ALU.mult)
                            else:
                                a = (acc2, acc2 if own else acc)[(j - VEC_FIRST) % 2](b)
                                if own:
                                    steps.wait()
                                elif j > VEC_FIRST + 1:
                                    steps.wait_before_last()
                                o = v.scalar_tensor_tensor(a, shifted(k, j), col(k, V_DW + j), a, ALU.mult, ALU.add)
                            steps.done(o)
                    def conv(k, b, last):
                        if not last:
                            glu(k + 1)
                        steps = Steps(v, tap_step, k * VEC_STEPS)
                        if not last:
                            v.wait_ge(taps_done, k + 1)
                        taps(k, b, range(VEC_FIRST, CW - END_TAPS if last else CW), steps, own=last)
                        steps.wait()
                        out = c_T[:, ds(k, 1), 0:NP].rearrange("p k n -> p (k n)")
                        v.wait_ge(product_added, (ACT_TAPS - 1) * (k + 1))
                        steps.link(v.scalar_tensor_tensor(out, acc2(b), col(k, V_BDW), product_sum[:, b], ALU.add, ALU.add))
                        if last:
                            v.wait_ge(taps_done, k + 1)
                        v.tensor_tensor(out, acc(b), out, ALU.add).then_inc(conv_done, 1)

                    glu(0)
                    with v.Fori(0, 3) as i:
                        for j in range(2):
                            conv(2 * i + j, j, False)
                    conv(6, 0, False)
                    conv(7, 1, True)

                @block.gpsimd
                def _(gp):
                    def samples(k):
                        s = Steps(gp, seg_step, 7 * k)
                        gp.wait_ge(u_done, 2 * k + 2)
                        taps = chan[:, ds(k, 1), V_DW:NV]
                        for t in range(NQ):
                            windows = u_seg[:, ds(k, 1), :, t:t + CW].rearrange("p k b w -> p (k b) w")
                            m = gp.tensor_tensor(prod.rearrange("p (b t) w -> p b t w", t=NQ)[:, :, t, :], windows,
                                                 taps.to_broadcast([P, NB, CW]), ALU.mult)
                        s.link(m)
                        out = c_T[:, ds(k, 1), NP:T].rearrange("p k n -> p (k n)")
                        for n in (15, 8, 4, 2):
                            up = CW - n if n == 15 else n
                            s.link(gp.tensor_tensor(prod[:, :, 0:n], prod[:, :, 0:n], prod[:, :, up:up + n], ALU.add))
                        s.link(gp.tensor_tensor(out, prod[:, :, 0], prod[:, :, 1], ALU.add))
                        s.done(gp.tensor_tensor(out, out, col(k, V_BDW).to_broadcast([P, NS]), ALU.add))

                    def add(k, b, early):
                        if not early:
                            gp.wait_ge(conv_done, k - 1)
                        for m in range(1, ACT_TAPS):
                            gp.wait_ge(product_ready, ACT_TAPS * k + m + 1)
                            if m > 1:
                                gp.wait_ge(product_added, (ACT_TAPS - 1) * k + m - 1)
                            gp.tensor_tensor(product_sum[:, b], products[:, 0, :] if m == 1 else product_sum[:, b],
                                             products[:, m % 4, :], ALU.add).then_inc(product_added, 1)

                    for k in range(2):
                        samples(k)
                        add(k, k, True)
                    with gp.Fori(1, KT // 2) as i:
                        for j in range(2):
                            samples(2 * i + j)
                            add(2 * i + j, j, False)

        def layernorm_stage():
            u_T = areaB[:, :].rearrange("p (k n) -> p k n", k=KT)
            u_seg = u_T[:, :, HIST + NP:UW].rearrange("p k (b n) -> p k b n", b=NB)
            u_turned, u_kept = sem("u_turned"), sem("u_rows_kept")
            tail = areaS[0:HIST, 0:1024]
            fresh = areaS[0:NS, 1024:2048]
            fresh_T = areaS[:, 3680:3680 + KT * NS].rearrange("p (k t) -> p k t", k=KT)
            fresh_ready = sem("u_fresh_ready")
            sq = areaS[:, 2048:2048 + 2 * T].rearrange("p (b t) -> p b t", b=2)
            centred, squared, summed = sem("ln_centred"), sem("ln_squared"), sem("ln_summed")
            rooted = sem("ln_rooted")
            with nc.Block() as block:
                @block.tensor
                def _(pe):
                    pe.wait_ge(fresh_ready, 1)
                    for k in range(KT):
                        pe.transpose(ps[0:HIST, 4 + k // 4, (k % 4) * P:(k % 4 + 1) * P], u_T[:, k, NP:NP + HIST], ident[:, :])
                        mm = pe.transpose(ps[0:NS, 6 + k // 4, (k % 4) * P:(k % 4 + 1) * P],
                                          fresh_T[:, k, :], ident[:, :])
                    mm.then_inc(u_turned, 1)
                    for k in range(KT):
                        pe.wait_ge(squared, k + 1)
                        for c in range(2):
                            mm = pe.matmul(ps[:, 2 + c, 0:TH], ones[:, :], sq[:, k % 2, c * TH:(c + 1) * TH],
                                           start=(k == 0), stop=(k == KT - 1))
                        mm.then_inc(summed, 1)

                @block.vector
                def _(v):
                    v.tensor_copy(fresh_T.rearrange("p k (b t) -> p k b t", b=NB), u_seg[:, :, :, HIST:SEG]).then_inc(fresh_ready, 1)
                    for k in range(KT):
                        v.scalar_tensor_tensor(half(c_T[:, k, :]), ps[:, 0:2, 0:TH], -1.0 / D, half(c_T[:, k, :]),
                                               ALU.mult, ALU.add).then_inc(centred, 1)
                    v.wait_ge(u_turned, 1)
                    v.tensor_copy(tail, ps[0:HIST, 4:6, :].rearrange("p c n -> p (c n)")).then_inc(u_kept, 1)
                    v.tensor_copy(fresh, ps[0:NS, 6:8, :].rearrange("p c n -> p (c n)")).then_inc(u_kept, 1)

                @block.sync
                def _(sp):
                    first_columns(sp, "w_pw2", w_pw2[0], (0, P))
                    sp.wait_ge(u_kept, 2)
                    sp.dma_start(conv_prompt[0, 0], tail).then_inc(u_stored, 16)
                    for b in range(NB):
                        sp.dma_start(conv_sample[0, b, HIST - NQ:HIST, :], fresh[NQ * b:NQ * b + NQ, :]).then_inc(u_stored, 16)

                @block.scalar
                def _(act):
                    for k in range(KT):
                        act.wait_ge(centred, k + 1)
                        if k >= 2:
                            act.wait_ge(summed, k - 1)
                        nc.scalar.activation(sq[:, k % 2, :], c_T[:, k, :], ACT.Square).then_inc(squared, 1)
                    act.wait_ge(summed, KT)
                    nc.scalar.activation(half(ln_std), ps[:, 2:4, 0:TH], ACT.Sqrt, scale=1.0 / D, bias=eps_col).then_inc(rooted, 1)
                    act.wait_ge(rooted, 1)

        area_route = areaS[:, :]
        off = [0]

        def part(n):
            off[0] += n
            return area_route[:, off[0] - n:off[0]]

        logits = part(NT * (NG + NE)).rearrange("p (t e) -> p t e", t=NT)
        picked = [part(NT * NE).rearrange("p (t e) -> p t e", t=NT) for _ in range(2)]
        tagged = [part(NT * NE).rearrange("p (t e) -> p t e", t=NT) for _ in range(2)]
        taken = part(NT * NE).rearrange("p (t e) -> p t e", t=NT)
        hot = part(NT * NE).rearrange("p (t e) -> p t e", t=NT)
        match = part(2 * NT * CAP).rearrange("p (c s) -> p c s", s=CAP)
        far, tok_of, pair_of = part(NE)[0:CAP], part(NE)[0:CAP], part(NE)[0:CAP]
        pair_no, rank, weight = part(2 * NT), part(2 * NT), part(2 * NT)
        g_top, g_sum, e_top, e_next, tie = part(NT), part(NT), part(NT), part(NT), part(NT)
        g_exp, g_hot, g_rev = part(NT * NG).rearrange("p (t g) -> p t g", t=NT), part(NT * NG).rearrange("p (t g) -> p t g", t=NT), part(NE)
        most = part(1)
        most_int = part(1).bitcast(I32)
        assert off[0] <= 5120, off[0]
        final_gain, final_gain_landed = areaC[:, 3 * D:4 * D], nc.alloc_semaphore("final_gain_landed")
        rows_in = areaC[:, 0:3 * D].rearrange("p (s n) -> p s n", s=3)
        rows_T = areaA[:, 0:3 * KT * CAP].rearrange("p (s k r) -> p s k r", s=3, k=KT)
        rows_out = areaB[:, 0:3 * D].rearrange("p (s n) -> p s n", s=3)
        hid_buf = areaB[:, 3072:3072 + 3 * F].rearrange("p (a f) -> p a f", a=3)
        gated, hid, hid_T = hid_buf[0:CAP, 0], hid_buf[0:CAP, 1], hid_buf[:, 2, 0:2 * CAP].rearrange("p (k r) -> p k r", k=2)

        def make_table(v, steps, match_ready, table_made, n):
            for c in range(2 * NT):
                m = v.tensor_scalar(match[:, c, :], slot_no[:, 0:CAP], rank[:, c:c + 1], None, ALU.is_equal)
            m.then_inc(match_ready, 1)
            v.wait_ge(table_made, n + 1)
            number = ps[0:CAP, 3, 256:256 + NE]
            steps.link(v.tensor_scalar(far, number, 0.0, FAR, ALU.is_equal, ALU.mult))
            steps.link(v.scalar_tensor_tensor(pair_of, number, -1.0, far, ALU.add, ALU.add))
            steps.link(v.tensor_scalar(far, pair_of, float(T), -float(T), ALU.is_ge, ALU.mult))
            steps.link(v.tensor_tensor(tok_of, pair_of, far, ALU.add))

        TABLE_STEPS = 4

        def table_matmuls(pe, table_made):
            for c in range(2 * NT):
                mm = pe.matmul(ps[0:CAP, 3, 256:256 + NE], match[:, c, :], tagged[c // NT][:, c % NT, :],
                               start=(c == 0), stop=(c == 2 * NT - 1))
            mm.then_inc(table_made, 1)

        def route_stage(l):
            std, gain_rows = areaB[:, 0:T], areaB[:, 1024:2048]
            rstd = small[:, 124:124 + NT]
            std_turned, inverted, gain_landed = sem(f"std_turned{l}"), sem(f"rstd_ready{l}"), sem(f"gain_rows_landed{l}")
            h_scaled, h_ready = sem(f"h_rows_scaled{l}"), sem(f"h_rows_ready{l}")
            h_out = areaB[:, 2048:2048 + 3 * D].rearrange("p (b n) -> p b n", b=3)
            logits_T = areaB[0:NR, 5120:5120 + T]
            rooted, logits_T_done, logits_T_kept = sem(f"rooted{l}"), sem(f"logits_T_done{l}"), sem(f"logits_T_kept{l}")
            logits_done, turned = sem(f"logits_done{l}"), sem(f"x_turned{l}")
            filled, step, exped = sem(f"route_filled{l}"), sem(f"route_step{l}"), sem(f"route_exped{l}")
            dif_ready, choice_ready, ranked = sem(f"route_dif_ready{l}"), sem(f"choice_ready{l}"), sem(f"ranked{l}")
            match_ready, table_made = sem(f"match_ready{l}"), sem(f"table_made{l}")
            h_stored = [sem(f"h_rows_stored{l}{b}") for b in range(3)]
            h_banks = (4, 6, 0)
            std_cols = ps[:, 3, 300:300 + NT]
            route_rows = ps[:, 2, 0:NT * NR].rearrange("p (t e) -> p t e", t=NT)
            rank_cols, count_cols = ps[:, 3, 0:NT * NE], ps[:, 3, NT * NE:(NT + 1) * NE]
            with nc.Block() as block:
                @block.sync
                def _(sp):
                    sp.dma_start(gain_rows, norm_ffn_g[l:l + 1, :].to_broadcast([P, D])).then_inc(gain_landed, 16)
                    for t in range(NT):
                        r = rows_of(t)
                        sp.wait_ge(h_ready, t + 1)
                        sp.dma_start(h_rows[t * P:t * P + r, :], h_out[0:r, t % 3, :]).then_inc(h_stored[t % 3], 16)
                    for b in range(3):
                        sp.wait_ge(h_stored[b], 16 * (2 if b < 2 else 1))

                @block.gpsimd
                def _(gp):
                    gp.iota(pair_no, [[T, 2], [P, NT]], base=1, channel_multiplier=1,
                            allow_small_or_imprecise_dtypes=True).then_inc(filled, 1)
                    gp.iota(g_rev, [[-1, NE]], base=NE, channel_multiplier=0,
                            allow_small_or_imprecise_dtypes=True).then_inc(filled, 1)
                    gp.memset(logits, 0.0).then_inc(filled, 1)
                    gp.memset(rows_in, 0.0).then_inc(filled, 1)
                    gp.wait_ge(filled, 4)
                    gp.wait_ge(gain_landed, 16)
                    for t in range(NT):
                        r = rows_of(t)
                        gp.wait_ge(h_scaled, t + 1)
                        gp.tensor_tensor(h_out[0:r, t % 3, :], h_out[0:r, t % 3, :], gain_rows[0:r, :], ALU.mult).then_inc(h_ready, 1)

                @block.tensor
                def _(pe):
                    pe.wait_ge(route_scaled[l], 1)
                    for k in range(KT):
                        for c in range(2):
                            mm = pe.matmul(ps[0:NR, c, 0:TH], w_route[:, k, :], x_T[:, k, c * TH:(c + 1) * TH],
                                           start=(k == 0), stop=(k == KT - 1))
                    mm.then_inc(logits_T_done, 1)
                    pe.wait_ge(rooted, 1)
                    for t in range(NT):
                        r = rows_of(t)
                        mm = pe.matmul(std_cols[0:r, t:t + 1], std[0:1, t * P:t * P + r], ones[0:1, 0:1], start=True, stop=True)
                    mm.then_inc(std_turned, 1)

                    def turn(t):
                        r, b = rows_of(t), h_banks[t % 3]
                        if t >= 3:
                            pe.wait_ge(h_scaled, t - 2)
                        for k in range(KT):
                            mm = pe.transpose(ps[0:r, b + k // 4, (k % 4) * P:(k % 4 + 1) * P],
                                              x_T[:, k, t * P:t * P + r], ident[:, :])
                        mm.then_inc(turned, 1)

                    turn(0)
                    pe.wait_ge(logits_T_kept, 1)
                    for t in range(NT):
                        r = rows_of(t)
                        mm = pe.transpose(route_rows[0:r, t, :], logits_T[:, t * P:t * P + r], ident[0:NR, 0:NR])
                    mm.then_inc(logits_done, 1)
                    for t in range(1, NT):
                        turn(t)
                    pe.wait_ge(choice_ready, 1)
                    for t in range(NT):
                        out = rank_cols[:, t * NE:(t + 1) * NE]
                        for u in range(t + 1):
                            pe.matmul(out, (before if u == t else ones)[:, :], taken[:, u, :], start=(u == 0), stop=(u == t))
                    for u in range(NT):
                        mm = pe.matmul(count_cols, ones[:, :], taken[:, u, :], start=(u == 0), stop=(u == NT - 1))
                    mm.then_inc(ranked, 1)
                    pe.wait_ge(match_ready, 1)
                    table_matmuls(pe, table_made)

                @block.scalar
                def _(act):
                    nc.scalar.activation(half(std), ps[:, 4:6, 0:TH], ACT.Sqrt, scale=1.0 / D, bias=eps_col).then_inc(rooted, 1)

                    def keep(t):
                        r, b = rows_of(t), h_banks[t % 3]
                        act.wait_ge(turned, t + 1)
                        if t >= 3:
                            act.wait_ge(h_stored[t % 3], 16)
                        nc.scalar.activation(h_out[0:r, t % 3, :], ps[0:r, b:b + 2, :].rearrange("p c n -> p (c n)"),
                                             ACT.Copy, scale=rstd[0:r, t:t + 1]).then_inc(h_scaled, 1)

                    act.wait_ge(logits_T_done, 1)
                    nc.scalar.activation(half(logits_T), ps[0:NR, 0:2, 0:TH], ACT.Copy).then_inc(logits_T_kept, 1)
                    act.wait_ge(inverted, 2)
                    for t in range(4):
                        keep(t)
                    act.wait_ge(dif_ready, 1)
                    nc.scalar.activation(g_exp, g_exp, ACT.Exp).then_inc(exped, 1)
                    nc.scalar.activation(tie, tie, ACT.Exp).then_inc(exped, 1)
                    keep(4)

                @block.vector
                def _(v):
                    s = Steps(v, step)
                    wide = lambda a, n: a.unsqueeze(2).to_broadcast([P, NT, n])
                    rev = lambda n: g_rev[:, NE - n:NE].unsqueeze(1).to_broadcast([P, NT, n])
                    v.wait_ge(std_turned, 1)
                    v.reciprocal(rstd[:, 0:4], std_cols[:, 0:4]).then_inc(inverted, 1)
                    v.reciprocal(rstd[0:NS, 4:5], std_cols[0:NS, 4:5]).then_inc(inverted, 1)
                    v.wait_ge(inverted, 2)
                    v.wait_ge(logits_done, 1)
                    v.wait_ge(filled, 3)
                    for t in range(NT):
                        r = rows_of(t)
                        s.done(v.scalar_tensor_tensor(logits[0:r, t, :], route_rows[0:r, t, :], rstd[0:r, t:t + 1], b_rows[0:r, :],
                                                      ALU.mult, ALU.add))
                    s.wait()
                    group, expert = logits[:, :, 0:NG], logits[:, :, NG:NG + NE]
                    s.link(v.tensor_reduce(g_top, group, AX_X, ALU.max))
                    s.link(v.tensor_tensor(g_hot, group, wide(g_top, NG), ALU.is_equal))
                    s.link(v.tensor_tensor(g_hot, g_hot, rev(NG), ALU.mult))
                    s.link(v.tensor_reduce(tie, g_hot, AX_X, ALU.max))
                    s.link(v.tensor_tensor(g_hot, g_hot, wide(tie, NG), ALU.is_equal))
                    s.link(v.tensor_tensor(g_exp, group, wide(g_top, NG), ALU.subtract))
                    by_group = lambda a: a.rearrange("p t (g e) -> p (t g) e", g=NG)
                    g_flat = g_hot.rearrange("p t g -> p (t g)").unsqueeze(2).to_broadcast([P, NT * NG, EG])
                    s.link(v.tensor_scalar(by_group(hot), g_flat, -1.0, -LOW, ALU.add, ALU.mult))
                    s.link(v.tensor_copy(taken, expert))
                    s.link(v.tensor_tensor(by_group(taken), by_group(taken), g_flat, ALU.mult))
                    s.link(v.tensor_tensor(taken, taken, hot, ALU.add))
                    for c, top in enumerate((e_top, e_next)):
                        s.link(v.tensor_reduce(top, taken, AX_X, ALU.max))
                        s.link(v.tensor_tensor(hot, taken, wide(top, NE), ALU.is_equal))
                        s.link(v.tensor_tensor(hot, hot, rev(NE), ALU.mult))
                        s.link(v.tensor_reduce(tie, hot, AX_X, ALU.max))
                        s.link(v.tensor_tensor(picked[c], hot, wide(tie, NE), ALU.is_equal))
                        if c == 0:
                            s.link(v.scalar_tensor_tensor(taken, picked[0], LOW, taken, ALU.mult, ALU.add))
                    for c in range(2):
                        s.done(v.memset(picked[c][32:64, 4, :], 0.0))
                        s.done(v.memset(picked[c][64:P, 4, :], 0.0))
                    s.wait()
                    v.tensor_tensor(taken, picked[0], picked[1], ALU.add).then_inc(choice_ready, 1)
                    v.tensor_tensor(tie, e_next, e_top, ALU.subtract).then_inc(dif_ready, 1)
                    for c in range(2):
                        s.link(v.tensor_tensor(tagged[c], picked[c], wide(pair_no[:, c * NT:(c + 1) * NT], NE), ALU.mult))
                    v.wait_ge(exped, 2)
                    s.link(v.tensor_reduce(g_sum, g_exp, AX_X, ALU.add))
                    s.link(v.tensor_scalar(e_top, tie, 1.0, None, ALU.add))
                    s.link(v.tensor_tensor(g_sum, g_sum, e_top, ALU.mult))
                    s.link(v.reciprocal(weight[:, 0:NT], g_sum))
                    s.link(v.tensor_tensor(weight[:, NT:2 * NT], weight[:, 0:NT], tie, ALU.mult))
                    v.wait_ge(ranked, 1)
                    ranks = rank_cols.rearrange("p (t e) -> p t e", t=NT)
                    for c in range(2):
                        s.link(v.tensor_tensor(hot, picked[c], ranks, ALU.mult))
                        s.link(v.tensor_reduce(rank[:, c * NT:(c + 1) * NT], hot, AX_X, ALU.add))
                    s.link(v.tensor_reduce(most, count_cols, AX_X, ALU.max))
                    s.link(v.tensor_copy(most_int, most))
                    make_table(v, s, match_ready, table_made, 0)

        class Nth:

            def __init__(self, i, c):
                self.i, self.c = i, c
                self.e, self.s, self.q = 3 * i + c, c % 3, i + c // 3

            def shift(self, d):
                return Nth(self.i, self.c + d)

        def expert_stage(l):
            gathered = [sem(f"rows_gathered{l}{s}") for s in range(3)]
            scattered = [sem(f"rows_scattered{l}{s}") for s in range(3)]
            tok_ready, pair_ready = sem(f"tok_ready{l}"), sem(f"pair_ready{l}")
            turned, turned_kept = sem(f"rows_turned{l}"), sem(f"rows_T_kept{l}")
            gateup_done, silued, hid_ready = sem(f"gateup_done{l}"), sem(f"silued{l}"), sem(f"hid_ready{l}")
            hid_turned, hid_high, hid_kept = sem(f"hid_turned{l}"), sem(f"hid_high_ready{l}"), sem(f"hid_T_kept{l}")
            down_high, down_split = sem(f"down_high_ready{l}"), sem(f"down_split{l}")
            down_done, out_kept = sem(f"down_done{l}"), sem(f"out_kept{l}")
            pool_settled = sem(f"pool_settled{l}")
            last = NE - 1

            def everywhere(eng, step):
                for e in range(1 + RING):
                    step(Nth(0, e), e == 0, False)
                with eng.Fori(1, (NE - 2) // RING) as i:
                    for u in range(RING):
                        step(Nth(i, 1 + u), False, False)
                step(Nth((NE - 2) // RING, 1), False, True)

            def turn_rows(pe, s):
                for k in range(KT):
                    mm = pe.transpose(ps[:, k // 4, (k % 4) * P:(k % 4) * P + CAP], rows_in[0:CAP, s, k * P:(k + 1) * P], ident[0:CAP, 0:CAP])
                return mm

            def gate_and_up(pe, s, w):
                for a, wt in ((0, ring_gate(w)), (1, ring_up(w))):
                    for k in range(KT):
                        mm = pe.matmul(ps[0:CAP, 2, a * F:(a + 1) * F], rows_T[:, s, k, :], wt[:, k, :],
                                       start=(k == 0), stop=(k == KT - 1))
                return mm

            def turn_hidden(pe):
                for k in range(2):
                    mm = pe.transpose(ps[:, 3, k * P:k * P + CAP], hid[:, k * P:(k + 1) * P], ident[0:CAP, 0:CAP])
                return mm

            def down(pe, w):
                for k in range(2):
                    for c in range(2):
                        mm = pe.matmul(ps[0:CAP, 4 + c, :], hid_T[:, k, :], ring_down(w)[:, k, c * 512:(c + 1) * 512],
                                       start=(k == 0), stop=(k == 1))
                return mm

            def keep_turned(act, s):
                return nc.scalar.activation(rows_T[:, s], ps[:, 0:2, :].rearrange("p c (k r) -> p (c k) r", r=P)[:, :, 0:CAP], ACT.Copy)

            def silu_gate():
                return nc.scalar.activation(gated, ps[0:CAP, 2, 0:F], ACT.Silu)

            def keep_hidden_T():
                return nc.scalar.activation(hid_T, ps[:, 3, 0:F].rearrange("p (k r) -> p k r", k=2)[:, :, 0:CAP], ACT.Copy)

            def fill_idx(gp, s, e, sem_, of, at):
                gp.tensor_copy(idx[0:CAP, at + s:at + s + 1], of[:, ds(e, 1)]).then_inc(sem_, 1)

            def gather(gp, s):
                settle(gp, pool_settled)
                return gp.indirect_dma_start(rows_in[0:CAP, s, :], None, h_rows, bass.IndirectOffsetOnAxis(idx[0:CAP, s:s + 1], 0),
                                             bounds_check=T - 1, oob_is_err=False)

            def scatter(gp, s):
                settle(gp, pool_settled)
                return gp.indirect_dma_start(pair_rows, bass.IndirectOffsetOnAxis(idx[0:CAP, 3 + s:4 + s], 0), rows_out[0:CAP, s, :],
                                             None, bounds_check=PAIRS - 1, oob_is_err=False)

            turned_hid_T = ps[:, 3, 0:F].rearrange("p (k r) -> p k r", k=2)[:, :, 0:CAP]

            def down_in_halves(pe):
                for k in range(2):
                    for r, w in ((0, 0), (0, 1), (1, 0)):
                        for c in range(2):
                            mm = pe.matmul(ps[0:CAP, 4 + c, :], hid_halves[:, r, k, :], down_halves[:, w, k, c * 512:(c + 1) * 512],
                                           start=(k == 0 and r == 0 and w == 0), stop=(k == 1 and r == 1))
                return mm

            with nc.Block() as block:
                @block.sync
                def _(sp):
                    if l == 1:
                        sp.dma_start(final_gain, final_norm_g.rearrange("(a n) -> a n", a=1).to_broadcast([P, D])).then_inc(final_gain_landed, 16)

                    def load(x):
                        sp.wait_ge(gateup_done, x.e - 2)
                        load_gateup(sp, l, x.e, x.s)
                        y = x.shift(-1)
                        if not (isinstance(y.e, int) and y.e < RING):
                            sp.wait_ge(down_split, y.e - 2)
                            load_down(sp, l, y.e, y.s)

                    for e in range(RING, 2 * RING):
                        load(Nth(0, e))
                    with sp.Fori(2, NE // RING) as i:
                        for u in range(RING):
                            load(Nth(i, u))
                    for e in range(NE // RING * RING, NE):
                        load(Nth(0, e))
                    sp.wait_ge(down_split, NE - RING)
                    load_down(sp, l, NE - 1, (NE - 1) % RING)

                @block.gpsimd
                def _(gp):
                    def fetch(x):
                        after(gp, gathered[x.s], 16 * x.q)
                        fill_idx(gp, x.s, x.e, tok_ready, tok_of, 0)
                        after(gp, turned, x.e - 2)
                        gp.wait_ge(tok_ready, x.e + 1)
                        gather(gp, x.s).then_inc(gathered[x.s], 16)

                    def store(x):
                        after(gp, scattered[x.s], 16 * x.q)
                        fill_idx(gp, x.s, x.e, pair_ready, pair_of, 3)
                        gp.wait_ge(pair_ready, x.e + 1)
                        gp.wait_ge(out_kept, 2 * x.e + 2)
                        scatter(gp, x.s).then_inc(scattered[x.s], 16)

                    for e in range(5):
                        fetch(Nth(0, e))
                    for e in range(3):
                        fetch(Nth(0, e + 5))
                        store(Nth(0, e))
                    with gp.Fori(1, (NE - 5) // RING) as i:
                        for u in range(RING):
                            fetch(Nth(i, u + 5))
                            store(Nth(i, u))
                    for e in range(NE - 5, NE):
                        store(Nth(0, e))
                    for s in range(3):
                        gp.wait_ge(scattered[s], 16 * len(range(s, NE, 3)))

                @block.tensor
                def _(pe):
                    def turn(x, first):
                        pe.wait_ge(gathered[x.s], 16 * x.q + 16)
                        if not first:
                            pe.wait_ge(turned_kept, x.e)
                        turn_rows(pe, x.s).then_inc(turned, 1)

                    def hidden(x):
                        pe.wait_ge(hid_ready, x.e + 1)
                        turn_hidden(pe).then_inc(hid_turned, 1)

                    def out(x):
                        pe.wait_ge(hid_kept, x.e + 1)
                        pe.wait_ge(down_split, x.e + 1)
                        after(pe, out_kept, 2 * x.e)
                        down_in_halves(pe).then_inc(down_done, 1)

                    def step(x, first, final):
                        if not final:
                            turn(x.shift(1), False)
                        if not first:
                            hidden(x.shift(-1))
                        pe.wait_ge(turned_kept, x.e + 1)
                        pe.wait_ge(gateup_landed[l][x.s], 32 * x.q + 32)
                        if not first:
                            pe.wait_ge(hid_ready, x.e)
                        gate_and_up(pe, x.s, x.s).then_inc(gateup_done, 1)
                        if not first:
                            out(x.shift(-1))

                    turn(Nth(0, 0), True)
                    everywhere(pe, step)
                    hidden(Nth(0, last))
                    out(Nth(0, last))

                @block.scalar
                def _(act):
                    def turned_rows(x):
                        act.wait_ge(turned, x.e + 1)
                        keep_turned(act, x.s).then_inc(turned_kept, 1)

                    def hidden(x):
                        act.wait_ge(hid_turned, x.e + 1)
                        nc.scalar.activation(hid_halves[:, 0], turned_hid_T, ACT.Copy).then_inc(hid_high, 1)

                    def down_high_half(x):
                        act.wait_ge(down_landed[l][x.s], 16 * x.q + 16)
                        after(act, down_done, x.e)
                        nc.scalar.activation(down_halves[:, 0], ring_down(x.s), ACT.Copy).then_inc(down_high, 1)

                    def out(x):
                        act.wait_ge(down_done, x.e + 1)
                        after(act, scattered[x.s], 16 * x.q)
                        nc.scalar.activation(rows_out[0:CAP, x.s, 0:512], ps[0:CAP, 4, :], ACT.Copy).then_inc(out_kept, 1)

                    def step(x, first, final):
                        if not final:
                            turned_rows(x.shift(1))
                        if not first:
                            hidden(x.shift(-1))
                            down_high_half(x.shift(-1))
                        act.wait_ge(gateup_done, x.e + 1)
                        silu_gate().then_inc(silued, 1)
                        if not first:
                            out(x.shift(-1))

                    turned_rows(Nth(0, 0))
                    everywhere(act, step)
                    hidden(Nth(0, last))
                    down_high_half(Nth(0, last))
                    out(Nth(0, last))

                @block.vector
                def _(v):
                    def out(x):
                        v.wait_ge(down_done, x.e + 1)
                        after(v, scattered[x.s], 16 * x.q)
                        v.tensor_copy(rows_out[0:CAP, x.s, 512:D], ps[0:CAP, 5, :]).then_inc(out_kept, 1)

                    def hidden(x):
                        v.wait_ge(hid_high, x.e + 1)
                        v.tensor_tensor(hid_halves[:, 1], turned_hid_T, hid_halves[:, 0].bitcast(F32), ALU.subtract).then_inc(hid_kept, 1)
                        v.wait_ge(down_high, x.e + 1)
                        v.tensor_tensor(down_halves[:, 1], ring_down(x.s), down_halves[:, 0].bitcast(F32),
                                        ALU.subtract).then_inc(down_split, 1)

                    def step(x, first, final):
                        if not first:
                            hidden(x.shift(-1))
                        v.wait_ge(silued, x.e + 1)
                        if not first:
                            v.wait_ge(hid_turned, x.e)
                        v.tensor_tensor(hid, gated, ps[0:CAP, 2, F:2 * F], ALU.mult).then_inc(hid_ready, 1)
                        if not first:
                            out(x.shift(-1))

                    everywhere(v, step)
                    hidden(Nth(0, last))
                    out(Nth(0, last))

            overflow_stage(l, turn_rows, gate_and_up, turn_hidden, down, keep_turned, silu_gate, keep_hidden_T,
                           fill_idx, gather, scatter)

        def overflow_stage(l, turn_rows, gate_and_up, turn_hidden, down, keep_turned, silu_gate, keep_hidden_T,
                           fill_idx, gather, scatter):
            names = ("idle match_ready table_made table_ready table_step landed idx_ready gathered turned turned_kept gateup_done "
                     "silued hid_ready hid_turned hid_kept down_done out_kept scattered").split()
            o = {n: sem(f"more_{n}{l}") for n in names}
            with nc.Block() as block:
                def over(eng, body, before_round=None, before=None):
                    most = eng.value_load(most_int[0:1, 0:1], min_val=0, max_val=T)
                    with eng.If(most > CAP):
                        if before:
                            before()
                        with eng.Fori(0, CHUNKS - 1) as j:
                            if before_round:
                                before_round(j)
                            with eng.Fori(0, NE) as e:
                                body(e, NE * j + e, j)

                @block.sync
                def _(sp):
                    def body(e, n, j):
                        sp.wait_ge(o["idle"], n + 1)
                        for dst, src in ((ring_gate(0), w_gate), (ring_up(0), w_up)):
                            sp.dma_start(dst, src[l, ds(e, 1)].rearrange("e (k p) f -> p (e k) f", p=P)).then_inc(o["landed"], 16)
                        sp.dma_start(ring_down(0), w_down[l, ds(e, 1)].rearrange("e (k p) n -> p (e k) n", p=P)).then_inc(o["landed"], 16)
                    over(sp, body)

                @block.gpsimd
                def _(gp):
                    def body(e, n, j):
                        gp.wait_ge(o["table_ready"], j + 1)
                        fill_idx(gp, 0, e, o["idx_ready"], tok_of, 0)
                        fill_idx(gp, 0, e, o["idx_ready"], pair_of, 3)
                        gp.wait_ge(o["idx_ready"], 2 * n + 2)
                        gather(gp, 0).then_inc(o["gathered"], 16)
                        gp.wait_ge(o["out_kept"], 2 * n + 2)
                        scatter(gp, 0).then_inc(o["scattered"], 16)
                        gp.wait_ge(o["scattered"], 16 * n + 16)
                        gp.sem_inc(o["idle"], 1)
                    over(gp, body, before=lambda: gp.sem_inc(o["idle"], 1))

                @block.tensor
                def _(pe):
                    def table(j):
                        pe.wait_ge(o["match_ready"], j + 1)
                        table_matmuls(pe, o["table_made"])

                    def body(e, n, j):
                        pe.wait_ge(o["gathered"], 16 * n + 16)
                        turn_rows(pe, 0).then_inc(o["turned"], 1)
                        pe.wait_ge(o["turned_kept"], n + 1)
                        pe.wait_ge(o["landed"], 48 * n + 48)
                        gate_and_up(pe, 0, 0).then_inc(o["gateup_done"], 1)
                        pe.wait_ge(o["hid_ready"], n + 1)
                        turn_hidden(pe).then_inc(o["hid_turned"], 1)
                        pe.wait_ge(o["hid_kept"], n + 1)
                        down(pe, 0).then_inc(o["down_done"], 1)
                        pe.wait_ge(o["out_kept"], 2 * n + 2)
                    over(pe, body, table)

                @block.scalar
                def _(act):
                    def body(e, n, j):
                        act.wait_ge(o["turned"], n + 1)
                        keep_turned(act, 0).then_inc(o["turned_kept"], 1)
                        act.wait_ge(o["gateup_done"], n + 1)
                        silu_gate().then_inc(o["silued"], 1)
                        act.wait_ge(o["hid_turned"], n + 1)
                        keep_hidden_T().then_inc(o["hid_kept"], 1)
                        act.wait_ge(o["down_done"], n + 1)
                        nc.scalar.activation(rows_out[0:CAP, 0, 0:512], ps[0:CAP, 4, :], ACT.Copy).then_inc(o["out_kept"], 1)
                    over(act, body)

                @block.vector
                def _(v):
                    def table(j):
                        v.wait_ge(o["idle"], NE * j + 1)
                        s = Steps(v, o["table_step"], (TABLE_STEPS + 1) * j)
                        s.link(v.tensor_scalar(rank, rank, -float(CAP), None, ALU.add))
                        make_table(v, s, o["match_ready"], o["table_made"], j)
                        v.sem_inc(o["table_ready"], 1)

                    def body(e, n, j):
                        v.wait_ge(o["silued"], n + 1)
                        v.tensor_tensor(hid, gated, ps[0:CAP, 2, F:2 * F], ALU.mult).then_inc(o["hid_ready"], 1)
                        v.wait_ge(o["down_done"], n + 1)
                        v.tensor_copy(rows_out[0:CAP, 0, 512:D], ps[0:CAP, 5, :]).then_inc(o["out_kept"], 1)
                    over(v, body, table)

        def combine_stage(l):
            final = l == 1
            flat = ring[:, :, :].rearrange("p s n -> p (s n)")
            pairs = flat[:, 0:NT * 2 * D].rearrange("p (t c n) -> p t c n", t=NT, c=2)
            x_rows = flat[:, NT * 2 * D:NT * 3 * D].rearrange("p (t n) -> p t n", t=NT)
            diag = areaB[:, 0:NT * P].rearrange("p (t n) -> p t n", t=NT)
            square = areaC[:, D:2 * D]
            ssq, rstd = small[:, 140:145], small[:, 145:150]
            landed = [sem(f"pairs_landed{l}{t}") for t in range(NT)]
            banks = lambda t: ps[:, 2 * (t % 4):2 * (t % 4) + 2, :]

            def load_pairs(sp):
                by_choice = pair_rows.rearrange("(c t) n -> t c n", c=2)
                for t in range(NT):
                    r = rows_of(t)
                    sp.dma_start(pairs[0:r, t], by_choice[t * P:t * P + r]).then_inc(landed[t], 16)

            def to_stream():
                first_scaled, mixed = sem("first_scaled"), sem("pairs_mixed")
                turned, added = sem("mixed_turned"), sem("mixed_added")
                with nc.Block() as block:
                    @block.sync
                    def _(sp):
                        load_pairs(sp)
                        sp.dma_start(state_rows, state_conv[0].rearrange("(i b) r n -> (b r) i n", i=2)).then_inc(state_landed, 16)
                        first_columns(sp, "pw1", w_pw1[0], (0, D))

                    @block.scalar
                    def _(act):
                        for t in range(NT):
                            r = rows_of(t)
                            act.wait_ge(landed[t], 16)
                            nc.scalar.activation(x_rows[0:r, t, :], pairs[0:r, t, 0, :], ACT.Copy,
                                                 scale=weight[0:r, t:t + 1]).then_inc(first_scaled, 1)

                    @block.tensor
                    def _(pe):
                        for t in range(NT):
                            r = rows_of(t)
                            pe.wait_ge(mixed, t + 1)
                            if t >= 4:
                                pe.wait_ge(added, t - 3)
                            for k in range(KT):
                                mm = pe.transpose(banks(t)[:, k // 4, (k % 4) * P:(k % 4) * P + r],
                                                  x_rows[0:r, t, k * P:(k + 1) * P], ident[0:r, 0:r])
                            mm.then_inc(turned, 1)

                    @block.vector
                    def _(v):
                        def mix(t):
                            r = rows_of(t)
                            v.wait_ge(first_scaled, t + 1)
                            v.scalar_tensor_tensor(x_rows[0:r, t, :], pairs[0:r, t, 1, :], weight[0:r, NT + t:NT + t + 1],
                                                   x_rows[0:r, t, :], ALU.mult, ALU.add).then_inc(mixed, 1)

                        def add(t):
                            r = rows_of(t)
                            v.wait_ge(turned, t + 1)
                            xs = x_T[:, :, t * P:t * P + r]
                            v.tensor_tensor(xs, banks(t).rearrange("p c (k t) -> p (c k) t", t=P)[:, :, 0:r],
                                            xs, ALU.add).then_inc(added, 1)

                        for t in range(NT):
                            mix(t)
                            if t >= 1:
                                add(t - 1)
                        add(NT - 1)
                        v.wait_ge(added, NT)

            def to_outputs():
                diag_ready, turned, summed = sem("weights_diag_ready"), sem("x_rows_turned"), sem("final_summed")
                squared, rooted, inverted = sem("final_squared"), sem("final_rooted"), sem("final_inverted")
                y_ready, y_stored = sem("y_ready"), sem("y_stored")
                with nc.Block() as block:
                    @block.sync
                    def _(sp):
                        load_pairs(sp)
                        for t in range(NT):
                            r = rows_of(t)
                            dst = y_prompt.rearrange("b t d -> (b t) d")[t * P:(t + 1) * P, :] if t < 4 \
                                else y_sample.rearrange("b t d -> (b t) d")
                            sp.wait_ge(y_ready, t + 1)
                            sp.dma_start(dst, pairs[0:r, t, 1, :]).then_inc(y_stored, 16)
                        sp.wait_ge(y_stored, 16 * NT)

                    @block.tensor
                    def _(pe):
                        for t in range(NT):
                            r = rows_of(t)
                            if t >= 4:
                                pe.wait_ge(summed, t - 3)
                            for k in range(KT):
                                pe.matmul(banks(t)[0:r, k // 4, (k % 4) * P:(k % 4 + 1) * P],
                                          x_T[:, k, t * P:t * P + r], ident[:, :], start=(k % 4 == 0), stop=False)
                            pe.wait_ge(landed[t], 16)
                            pe.wait_ge(diag_ready, t + 1)
                            for c in range(2):
                                mm = pe.matmul(banks(t)[0:r, c, :], diag[0:r, t, 0:r], pairs[0:r, t, 0, c * 512:(c + 1) * 512],
                                               start=False, stop=True)
                            mm.then_inc(turned, 1)

                    @block.scalar
                    def _(act):
                        for t in range(NT):
                            r = rows_of(t)
                            act.wait_ge(summed, t + 1)
                            nc.scalar.activation(square[0:r, :], x_rows[0:r, t, :], ACT.Square,
                                                 accum_out=ssq[0:r, t:t + 1]).then_inc(squared, 1)
                            act.wait_ge(squared, t + 1)
                            nc.scalar.activation(rstd[0:r, t:t + 1], ssq[0:r, t:t + 1], ACT.Sqrt, scale=1.0 / D,
                                                 bias=eps_col[0:r]).then_inc(rooted, 1)

                    @block.vector
                    def _(v):
                        def add_up(t):
                            r = rows_of(t)
                            v.wait_ge(turned, t + 1)
                            v.scalar_tensor_tensor(x_rows[0:r, t, :], pairs[0:r, t, 1, :], weight[0:r, NT + t:NT + t + 1],
                                                   banks(t)[0:r].rearrange("p c n -> p (c n)"), ALU.mult, ALU.add).then_inc(summed, 1)

                        def finish(t):
                            r = rows_of(t)
                            v.wait_ge(rooted, t + 1)
                            v.reciprocal(rstd[0:r, t:t + 1], rstd[0:r, t:t + 1]).then_inc(inverted, 1)
                            v.wait_ge(inverted, t + 1)
                            v.scalar_tensor_tensor(pairs[0:r, t, 1, :], x_rows[0:r, t, :], rstd[0:r, t:t + 1], final_gain[0:r, :],
                                                   ALU.mult, ALU.mult).then_inc(y_ready, 1)

                        for t in range(NT):
                            v.tensor_scalar(diag[:, t, :], ident[:, :], weight[:, t:t + 1], None, ALU.mult).then_inc(diag_ready, 1)
                        v.wait_ge(final_gain_landed, 16)
                        add_up(0)
                        for t in range(1, NT):
                            add_up(t)
                            finish(t - 1)
                        finish(NT - 1)

            if final:
                to_outputs()
            else:
                to_stream()

        state_landed = nc.alloc_semaphore("state_landed")
        kv_stored = nc.alloc_semaphore("kv_stored")
        sink_landed, s_q_ready = sem("sink_landed"), sem("sample_q_ready")
        cache_landed, vcache_landed = sem("cache_landed"), sem("vcache_landed")
        load_stage()
        norm_stage("mix0", lambda sp: (load_queries(sp, 0), load_queries(sp, 1)))
        qkv_stage()
        prompt_attention_stage()
        sample_attention_stage()
        semaphores_back()
        project_back_stage("w_o", w_o[0], w_halves_A, o_T, False, None, 0, kv_stored, 4 + 2 * NB)
        route_stage(0)
        expert_stage(0)
        combine_stage(0)
        semaphores_back()
        norm_stage("mix1")
        u_stored = sem("u_rows_stored")
        conv_stage()
        layernorm_stage()
        project_back_stage("w_pw2", w_pw2[0], w_halves_C, c_T, True, V_BPW2, 1, u_stored, 1 + NB)
        route_stage(1)
        expert_stage(1)
        combine_stage(1)


_INS = ["x_prompt", "x_sample", "cache_k", "cache_v", "state_conv", "w_qkv", "w_o", "attn_sinks",
        "w_pw1", "b_pw1", "w_dw", "b_dw", "conv_ln_g", "conv_ln_b", "w_pw2", "b_pw2", "norm_mix_g", "norm_ffn_g",
        "w_group_router", "b_group_router", "w_expert_router", "b_expert_router",
        "w_gate", "w_up", "w_down", "final_norm_g"]
_OUTS = [(1, NP, D), (NB, NQ, D), (1, 1, WIN, HKV, DH), (1, 1, WIN, HKV, DH), (1, 1, HIST, D),
         (1, NB, WIN, HKV, DH), (1, NB, WIN, HKV, DH), (1, NB, HIST, D)]


def kernel(**inputs):
    import concourse.bacc as bacc
    from concourse.bass_utils import run_bass_kernel_spmd

    nc = bacc.Bacc("TRN2", target_bir_lowering=False, num_devices=1)
    arrays, args = {}, []
    for name in _INS:
        a = np.ascontiguousarray(inputs[name])
        arrays[f"in_{name}"] = a
        args.append(nc.dram_tensor(f"in_{name}", a.shape, mybir.dt.from_np(a.dtype), kind="ExternalInput").ap())
    for i, shape in enumerate(_OUTS):
        args.append(nc.dram_tensor(f"out_{i}", shape, F32, kind="ExternalOutput").ap())
    hybrid_step(nc, *args)
    r = run_bass_kernel_spmd(nc, [arrays], core_ids=[0])
    return tuple(r.results[0][f"out_{i}"] for i in range(len(_OUTS)))
```
